# Optimizing a Trainium2 kernel written in Bass

```python
import math
import numpy as np
import jax
import jax.numpy as jnp
from jax import lax
import jax, jax.numpy as jnp

D_MODEL = 1024
BATCH = 1
SEQ = 512
DEPTH = 1

HEAD_DIM = 64
ROPE_THETA = 10000.0
NORM_EPS = 1e-6
NEG_INF = -1e30

DIFF_HEADS = 4
DIFF_V_DIM = 2 * HEAD_DIM
DIFF_WIDTH = DIFF_HEADS * DIFF_V_DIM
Q_BLOCK = 128

NSA_HEADS = 8
NSA_KV_GROUPS = 2
NSA_HEADS_PER_GROUP = NSA_HEADS // NSA_KV_GROUPS
NSA_WIDTH = NSA_HEADS * HEAD_DIM
KV_COLS = NSA_KV_GROUPS * HEAD_DIM
CMP_BLOCK = 32
CMP_STRIDE = 16
CMP_HIDDEN = 4 * HEAD_DIM
SLC_BLOCK = 64
SLC_TOPK = 16
WINDOW = 512
NSA_Q_BLOCK = 64
N_BRANCHES = 3

MIX_WIDTH = DIFF_WIDTH + NSA_WIDTH
IN_COLS = 2 * DIFF_HEADS * 2 * HEAD_DIM + DIFF_WIDTH + NSA_WIDTH + 6 * KV_COLS + NSA_HEADS * N_BRANCHES
D_FF = ((8 * D_MODEL + 3 * 256 - 1) // (3 * 256)) * 256


def rms_norm(x, g):
    xf = x.astype(jnp.float32)
    y = xf * lax.rsqrt(jnp.mean(xf * xf, axis=-1, keepdims=True) + NORM_EPS)
    return (y * g.astype(jnp.float32)).astype(x.dtype)

def rope_tables(S):
    inv = 1.0 / (ROPE_THETA ** (jnp.arange(0, HEAD_DIM, 2, dtype=jnp.float32) / HEAD_DIM))
    ang = jnp.arange(S, dtype=jnp.float32)[:, None] * inv[None, :]
    return jnp.cos(ang), jnp.sin(ang)

def apply_rope(x, cos, sin):
    x1, x2 = jnp.split(x, 2, axis=-1)
    c = cos.astype(x.dtype)
    s = sin.astype(x.dtype)
    return jnp.concatenate([x1 * c - x2 * s, x1 * s + x2 * c], axis=-1)

def masked_softmax(s, mask):
    p = jax.nn.softmax(jnp.where(mask, s, NEG_INF), axis=-1)
    return jnp.where(mask, p, 0.0)

def diff_attention(q, k, v, lam):
    B, H, _, S, d = q.shape
    scale = d ** -0.5
    kpos = jnp.arange(S)

    def block(i):
        s0 = i * Q_BLOCK
        qb = lax.dynamic_slice_in_dim(q, s0, Q_BLOCK, axis=3)
        s = jnp.einsum('bhmqd,bhmkd->bhmqk', qb, k).astype(jnp.float32) * scale
        qpos = s0 + jnp.arange(Q_BLOCK)
        mask = kpos[None, :] <= qpos[:, None]
        p = jax.nn.softmax(jnp.where(mask, s, NEG_INF), axis=-1)
        a = p[:, :, 0] - lam * p[:, :, 1]
        return jnp.einsum('bhqk,bhke->bhqe', a.astype(v.dtype), v)

    o = lax.map(block, jnp.arange(S // Q_BLOCK))
    return o.transpose(1, 0, 3, 2, 4).reshape(B, S, H, v.shape[-1])

def compress_tokens(t, tok_idx, pos, w1, w2):
    blocks = t[:, :, tok_idx] + pos.astype(t.dtype)
    flat = blocks.reshape(blocks.shape[0], blocks.shape[1], blocks.shape[2], -1)
    return jax.nn.silu(flat @ w1) @ w2

def selection_overlap(n_cmp, n_sel):
    c0 = np.arange(n_cmp)[:, None] * CMP_STRIDE
    s0 = np.arange(n_sel)[None, :] * SLC_BLOCK
    ov = np.clip(np.minimum(c0 + CMP_BLOCK, s0 + SLC_BLOCK) - np.maximum(c0, s0), 0, None)
    return (ov / CMP_BLOCK).astype(np.float32)

def nsa_attention(q, kc_tok, vc_tok, ks, vs, kw, vw, gates,
                  k_pos, k_w1, k_w2, v_pos, v_w1, v_w2):
    B, G, Hg, S, d = q.shape
    dt = q.dtype
    scale = d ** -0.5
    QB = NSA_Q_BLOCK
    n_cmp = (S - CMP_BLOCK) // CMP_STRIDE + 1
    n_sel = S // SLC_BLOCK
    top_n = min(SLC_TOPK, n_sel)

    tok_idx = np.arange(n_cmp)[:, None] * CMP_STRIDE + np.arange(CMP_BLOCK)[None, :]
    kc = compress_tokens(kc_tok, tok_idx, k_pos, k_w1, k_w2)
    vc = compress_tokens(vc_tok, tok_idx, v_pos, v_w1, v_w2)
    cmp_end = jnp.asarray(tok_idx[:, -1])
    overlap = jnp.asarray(selection_overlap(n_cmp, n_sel))

    ks_blk = ks.reshape(B, G, n_sel, SLC_BLOCK, d)
    vs_blk = vs.reshape(B, G, n_sel, SLC_BLOCK, d)
    kw_pad = jnp.pad(kw, ((0, 0), (0, 0), (WINDOW, 0), (0, 0)))
    vw_pad = jnp.pad(vw, ((0, 0), (0, 0), (WINDOW, 0), (0, 0)))
    gather_blocks = jax.vmap(jax.vmap(lambda t, i: t[i]))
    blk = jnp.arange(n_sel)

    def block(i):
        s0 = i * QB
        qb = lax.dynamic_slice_in_dim(q, s0, QB, axis=3)
        gb = lax.dynamic_slice_in_dim(gates, s0, QB, axis=3)
        qpos = s0 + jnp.arange(QB)

        sc = jnp.einsum('bghqd,bgnd->bghqn', qb, kc).astype(jnp.float32) * scale
        pc = masked_softmax(sc, cmp_end[None, :] <= qpos[:, None])
        o_cmp = jnp.einsum('bghqn,bgnd->bghqd', pc.astype(dt), vc)

        imp = jnp.einsum('bghqn,nj->bgqj', pc, overlap)
        cur = qpos // SLC_BLOCK
        valid = blk[None, :] * SLC_BLOCK <= qpos[:, None]
        forced = (blk[None, :] == 0) | (blk[None, :] == cur[:, None]) | (blk[None, :] == cur[:, None] - 1)
        imp = jnp.where(forced, jnp.inf, jnp.where(valid, imp, -jnp.inf))
        _, sel = lax.top_k(imp, top_n)
        kg = gather_blocks(ks_blk, sel)
        vg = gather_blocks(vs_blk, sel)
        tpos = sel[..., None] * SLC_BLOCK + jnp.arange(SLC_BLOCK)
        smask = (tpos <= qpos[:, None, None]).reshape(B, G, 1, QB, top_n * SLC_BLOCK)
        ss = jnp.einsum('bghqd,bgqnld->bghqnl', qb, kg).astype(jnp.float32) * scale
        ps = masked_softmax(ss.reshape(B, G, Hg, QB, top_n * SLC_BLOCK), smask)
        o_slc = jnp.einsum('bghqm,bgqmd->bghqd', ps.astype(dt),
                           vg.reshape(B, G, QB, top_n * SLC_BLOCK, d))

        kwb = lax.dynamic_slice_in_dim(kw_pad, s0, WINDOW + QB, axis=2)
        vwb = lax.dynamic_slice_in_dim(vw_pad, s0, WINDOW + QB, axis=2)
        wpos = s0 - WINDOW + jnp.arange(WINDOW + QB)
        wmask = (wpos[None, :] <= qpos[:, None]) & (wpos[None, :] > qpos[:, None] - WINDOW) & (wpos[None, :] >= 0)
        sw = jnp.einsum('bghqd,bgkd->bghqk', qb, kwb).astype(jnp.float32) * scale
        pw = masked_softmax(sw, wmask)
        o_win = jnp.einsum('bghqk,bgkd->bghqd', pw.astype(dt), vwb)

        return gb[..., 0:1] * o_cmp + gb[..., 1:2] * o_slc + gb[..., 2:3] * o_win

    o = lax.map(block, jnp.arange(S // QB))
    return o.transpose(1, 0, 4, 2, 3, 5).reshape(B, S, G * Hg * d)

def hybrid_mixer(h, layer, w_in, lambda_q1, lambda_k1, lambda_q2, lambda_k2, diff_subln,
                 k_cmp_pos, k_cmp_w1, k_cmp_w2, v_cmp_pos, v_cmp_w1, v_cmp_w2, w_out):
    B, S, _ = h.shape
    cos, sin = rope_tables(S)
    proj = h @ w_in
    sizes = [DIFF_HEADS * 2 * HEAD_DIM, DIFF_HEADS * 2 * HEAD_DIM, DIFF_WIDTH, NSA_WIDTH,
             KV_COLS, KV_COLS, KV_COLS, KV_COLS, KV_COLS, KV_COLS, NSA_HEADS * N_BRANCHES]
    dq, dk, dv, nq, kc, vc, ks, vs, kw, vw, gt = jnp.split(
        proj, np.cumsum(sizes)[:-1].tolist(), axis=-1)

    dq = apply_rope(dq.reshape(B, S, DIFF_HEADS, 2, HEAD_DIM).transpose(0, 2, 3, 1, 4), cos, sin)
    dk = apply_rope(dk.reshape(B, S, DIFF_HEADS, 2, HEAD_DIM).transpose(0, 2, 3, 1, 4), cos, sin)
    dv = dv.reshape(B, S, DIFF_HEADS, DIFF_V_DIM).transpose(0, 2, 1, 3)
    lam_init = 0.8 - 0.6 * math.exp(-0.3 * layer)
    f32 = jnp.float32
    lam = (jnp.exp(jnp.sum(lambda_q1.astype(f32) * lambda_k1.astype(f32)))
           - jnp.exp(jnp.sum(lambda_q2.astype(f32) * lambda_k2.astype(f32))) + lam_init)
    o_diff = diff_attention(dq, dk, dv, lam)
    o_diff = (rms_norm(o_diff, diff_subln) * (1.0 - lam_init)).reshape(B, S, DIFF_WIDTH)

    def q_heads(t):
        return t.reshape(B, S, NSA_KV_GROUPS, NSA_HEADS_PER_GROUP, HEAD_DIM).transpose(0, 2, 3, 1, 4)

    def kv_heads(t):
        return t.reshape(B, S, NSA_KV_GROUPS, HEAD_DIM).transpose(0, 2, 1, 3)

    nq = apply_rope(q_heads(nq), cos, sin)
    kc = apply_rope(kv_heads(kc), cos, sin)
    ks = apply_rope(kv_heads(ks), cos, sin)
    kw = apply_rope(kv_heads(kw), cos, sin)
    gates = jax.nn.sigmoid(gt.reshape(B, S, NSA_KV_GROUPS, NSA_HEADS_PER_GROUP, N_BRANCHES)
                           .transpose(0, 2, 3, 1, 4))
    o_nsa = nsa_attention(nq, kc, kv_heads(vc), ks, kv_heads(vs), kw, kv_heads(vw), gates,
                          k_cmp_pos, k_cmp_w1, k_cmp_w2, v_cmp_pos, v_cmp_w1, v_cmp_w2)

    return jnp.concatenate([o_diff, o_nsa], axis=-1) @ w_out

def first_inputs(seed: int = 0) -> dict:
    key = jax.random.key(seed)
    k = jax.random.split(key, 24)
    L = DEPTH

    def nrm(kk, shape, scale):
        return jax.random.normal(kk, shape, jnp.float32) * scale

    def gain(kk, n):
        return 1.0 + 0.05 * jax.random.normal(kk, (L, n), jnp.float32)

    cmp_in = CMP_BLOCK * HEAD_DIM
    return {
        'x': nrm(k[0], (BATCH, SEQ, D_MODEL), 1.0),
        'attn_pre_norm': gain(k[1], D_MODEL),
        'w_in': nrm(k[2], (L, D_MODEL, IN_COLS), D_MODEL ** -0.5),
        'lambda_q1': nrm(k[3], (L, HEAD_DIM), 0.1),
        'lambda_k1': nrm(k[4], (L, HEAD_DIM), 0.1),
        'lambda_q2': nrm(k[5], (L, HEAD_DIM), 0.1),
        'lambda_k2': nrm(k[6], (L, HEAD_DIM), 0.1),
        'diff_subln': gain(k[7], DIFF_V_DIM),
        'k_cmp_pos': nrm(k[8], (L, CMP_BLOCK, HEAD_DIM), 0.1),
        'k_cmp_w1': nrm(k[9], (L, cmp_in, CMP_HIDDEN), cmp_in ** -0.5),
        'k_cmp_w2': nrm(k[10], (L, CMP_HIDDEN, HEAD_DIM), CMP_HIDDEN ** -0.5),
        'v_cmp_pos': nrm(k[11], (L, CMP_BLOCK, HEAD_DIM), 0.1),
        'v_cmp_w1': nrm(k[12], (L, cmp_in, CMP_HIDDEN), cmp_in ** -0.5),
        'v_cmp_w2': nrm(k[13], (L, CMP_HIDDEN, HEAD_DIM), CMP_HIDDEN ** -0.5),
        'w_out': nrm(k[14], (L, MIX_WIDTH, D_MODEL), MIX_WIDTH ** -0.5),
        'attn_post_norm': gain(k[15], D_MODEL),
        'ffn_pre_norm': gain(k[16], D_MODEL),
        'w_gate': nrm(k[17], (L, D_MODEL, D_FF), D_MODEL ** -0.5),
        'w_up': nrm(k[18], (L, D_MODEL, D_FF), D_MODEL ** -0.5),
        'w_down': nrm(k[19], (L, D_FF, D_MODEL), D_FF ** -0.5),
        'ffn_post_norm': gain(k[20], D_MODEL),
    }

def first_block(x, attn_pre_norm, w_in, lambda_q1, lambda_k1, lambda_q2, lambda_k2, diff_subln,
              k_cmp_pos, k_cmp_w1, k_cmp_w2, v_cmp_pos, v_cmp_w1, v_cmp_w2, w_out,
              attn_post_norm, ffn_pre_norm, w_gate, w_up, w_down, ffn_post_norm):
    for l in range(DEPTH):
        h = rms_norm(x, attn_pre_norm[l])
        mix = hybrid_mixer(h, l, w_in[l], lambda_q1[l], lambda_k1[l], lambda_q2[l], lambda_k2[l],
                           diff_subln[l], k_cmp_pos[l], k_cmp_w1[l], k_cmp_w2[l],
                           v_cmp_pos[l], v_cmp_w1[l], v_cmp_w2[l], w_out[l])
        x = x + rms_norm(mix, attn_post_norm[l])
        h = rms_norm(x, ffn_pre_norm[l])
        f = (jax.nn.silu(h @ w_gate[l]) * (h @ w_up[l])) @ w_down[l]
        x = x + rms_norm(f, ffn_post_norm[l])
    return x


DEPTH_2 = 2

N_EVEN = (DEPTH_2 + 1) // 2
N_ODD = DEPTH_2 // 2

D_CONV_A = D_MODEL // 2
N_FOX_HEADS = (D_MODEL // 2) // HEAD_DIM
D_FOX = N_FOX_HEADS * HEAD_DIM
SHORT_CONV_WIDTH = 3
CONFORMER_CONV_WIDTH = 31
BLOCK_Q = 128
_FF_RAW = -(-8 * D_MODEL // 3)
D_FF_2 = -(-_FF_RAW // 256) * 256
RMS_EPS = 1e-6
LN_EPS = 1e-5

OFF_GB = 0
OFF_GC = OFF_GB + D_CONV_A
OFF_XA = OFF_GC + D_CONV_A
OFF_Q = OFF_XA + D_CONV_A
OFF_K = OFF_Q + D_FOX
OFF_V = OFF_K + D_FOX
OFF_F = OFF_V + D_FOX
D_IN_EVEN = OFF_F + N_FOX_HEADS


def rms_norm_2(x, g):
    xf = x.astype(jnp.float32)
    y = xf * lax.rsqrt(jnp.mean(xf * xf, axis=-1, keepdims=True) + RMS_EPS)
    return (y * g.astype(jnp.float32)).astype(x.dtype)

def layer_norm(x, g, b):
    xf = x.astype(jnp.float32)
    mu = jnp.mean(xf, axis=-1, keepdims=True)
    xc = xf - mu
    var = jnp.mean(xc * xc, axis=-1, keepdims=True)
    y = xc * lax.rsqrt(var + LN_EPS)
    return (y * g.astype(jnp.float32) + b.astype(jnp.float32)).astype(x.dtype)

def causal_depthwise_conv(x, w):
    k_width, ch = w.shape
    return lax.conv_general_dilated(
        x, w[:, None, :].astype(x.dtype), window_strides=(1,),
        padding=[(k_width - 1, 0)], dimension_numbers=("NWC", "WIO", "NWC"),
        feature_group_count=ch)

def forgetting_attention(q, k, v, log_f):
    seq = q.shape[1]
    c = jnp.cumsum(log_f, axis=1).transpose(0, 2, 1)
    scale = HEAD_DIM ** -0.5
    outs = []
    for start in range(0, seq, BLOCK_Q):
        end = start + BLOCK_Q
        s = jnp.einsum("bqhd,bkhd->bhqk", q[:, start:end], k[:, :end],
                       preferred_element_type=jnp.float32) * scale
        bias = c[:, :, start:end, None] - c[:, :, None, :end]
        mask = (start + jnp.arange(BLOCK_Q))[:, None] >= jnp.arange(end)[None, :]
        s = jnp.where(mask, s + bias, -jnp.inf)
        p = jax.nn.softmax(s, axis=-1)
        outs.append(jnp.einsum("bhqk,bkhd->bqhd", p.astype(v.dtype), v[:, :end]))
    return jnp.concatenate(outs, axis=1)

def shortconv_fox_mixer(h, w_in, b_f, conv_w, w_out):
    bsz, seq, _ = h.shape
    proj = h @ w_in
    gate_b = proj[..., OFF_GB:OFF_GC]
    gate_c = proj[..., OFF_GC:OFF_XA]
    xa = proj[..., OFF_XA:OFF_Q]
    y_a = gate_b * causal_depthwise_conv(gate_c * xa, conv_w)
    q = proj[..., OFF_Q:OFF_K].reshape(bsz, seq, N_FOX_HEADS, HEAD_DIM)
    k = proj[..., OFF_K:OFF_V].reshape(bsz, seq, N_FOX_HEADS, HEAD_DIM)
    v = proj[..., OFF_V:OFF_F].reshape(bsz, seq, N_FOX_HEADS, HEAD_DIM)
    log_f = jax.nn.log_sigmoid((proj[..., OFF_F:] + b_f).astype(jnp.float32))
    y_b = forgetting_attention(q, k, v, log_f).reshape(bsz, seq, D_FOX)
    return jnp.concatenate([y_a, y_b.astype(h.dtype)], axis=-1) @ w_out

def conformer_conv_module(h, w_pw1, b_pw1, w_dw, b_dw, ln_g, ln_b, w_pw2, b_pw2):
    a, g = jnp.split(h @ w_pw1 + b_pw1, 2, axis=-1)
    u = a * jax.nn.sigmoid(g)
    u = causal_depthwise_conv(u, w_dw) + b_dw
    u = jax.nn.silu(layer_norm(u, ln_g, ln_b))
    return u @ w_pw2 + b_pw2

def swiglu_ffn(h, w_ffn_in, w_ffn_out):
    g, u = jnp.split(h @ w_ffn_in, 2, axis=-1)
    return (jax.nn.silu(g) * u) @ w_ffn_out

def second_inputs(seed: int = 0) -> dict:
    key = jax.random.key(seed)
    ks = jax.random.split(key, 20)
    f32 = jnp.float32
    nrm = lambda k, shape, s: (jax.random.normal(k, shape, f32) * s)
    gain = lambda k, shape: 1.0 + 0.05 * jax.random.normal(k, shape, f32)
    return {
        "x": jax.random.normal(ks[0], (BATCH, SEQ, D_MODEL), f32),
        "norm_mix_pre": gain(ks[1], (DEPTH_2, D_MODEL)),
        "norm_mix_post": gain(ks[2], (DEPTH_2, D_MODEL)),
        "norm_ffn_pre": gain(ks[3], (DEPTH_2, D_MODEL)),
        "norm_ffn_post": gain(ks[4], (DEPTH_2, D_MODEL)),
        "w_in": nrm(ks[5], (N_EVEN, D_MODEL, D_IN_EVEN), D_MODEL ** -0.5),
        "b_forget": 1.0 + 3.0 * jax.random.uniform(ks[6], (N_EVEN, N_FOX_HEADS), f32),
        "w_short_conv": nrm(ks[7], (N_EVEN, SHORT_CONV_WIDTH, D_CONV_A), SHORT_CONV_WIDTH ** -0.5),
        "w_out": nrm(ks[8], (N_EVEN, D_CONV_A + D_FOX, D_MODEL), (D_CONV_A + D_FOX) ** -0.5),
        "w_pw1": nrm(ks[9], (N_ODD, D_MODEL, 2 * D_MODEL), D_MODEL ** -0.5),
        "b_pw1": nrm(ks[10], (N_ODD, 2 * D_MODEL), 0.02),
        "w_dw": nrm(ks[11], (N_ODD, CONFORMER_CONV_WIDTH, D_MODEL), CONFORMER_CONV_WIDTH ** -0.5),
        "b_dw": nrm(ks[12], (N_ODD, D_MODEL), 0.02),
        "ln_g": gain(ks[13], (N_ODD, D_MODEL)),
        "ln_b": nrm(ks[14], (N_ODD, D_MODEL), 0.02),
        "w_pw2": nrm(ks[15], (N_ODD, D_MODEL, D_MODEL), D_MODEL ** -0.5),
        "b_pw2": nrm(ks[16], (N_ODD, D_MODEL), 0.02),
        "w_ffn_in": nrm(ks[17], (DEPTH_2, D_MODEL, 2 * D_FF_2), D_MODEL ** -0.5),
        "w_ffn_out": nrm(ks[18], (DEPTH_2, D_FF_2, D_MODEL), D_FF_2 ** -0.5),
    }

def second_block(x, norm_mix_pre, norm_mix_post, norm_ffn_pre, norm_ffn_post,
              w_in, b_forget, w_short_conv, w_out,
              w_pw1, b_pw1, w_dw, b_dw, ln_g, ln_b, w_pw2, b_pw2,
              w_ffn_in, w_ffn_out):
    h = x
    for layer in range(DEPTH_2):
        j = layer // 2
        u = rms_norm_2(h, norm_mix_pre[layer])
        if layer % 2 == 0:
            m = shortconv_fox_mixer(u, w_in[j], b_forget[j], w_short_conv[j], w_out[j])
        else:
            m = conformer_conv_module(u, w_pw1[j], b_pw1[j], w_dw[j], b_dw[j],
                                      ln_g[j], ln_b[j], w_pw2[j], b_pw2[j])
        h = h + rms_norm_2(m, norm_mix_post[layer])
        f = swiglu_ffn(rms_norm_2(h, norm_ffn_pre[layer]), w_ffn_in[layer], w_ffn_out[layer])
        h = h + rms_norm_2(f, norm_ffn_post[layer])
    return h


def setup_inputs(seed=0):
    out = dict(first_inputs(seed))
    for name, value in second_inputs(seed + 1).items():
        if name != "x":
            out[name + "_2"] = value
    return out


def reference(
    x, attn_pre_norm, w_in, lambda_q1, lambda_k1, lambda_q2, lambda_k2, diff_subln, k_cmp_pos,
    k_cmp_w1, k_cmp_w2, v_cmp_pos, v_cmp_w1, v_cmp_w2, w_out, attn_post_norm, ffn_pre_norm,
    w_gate, w_up, w_down, ffn_post_norm, norm_mix_pre_2, norm_mix_post_2, norm_ffn_pre_2,
    norm_ffn_post_2, w_in_2, b_forget_2, w_short_conv_2, w_out_2, w_pw1_2, b_pw1_2, w_dw_2,
    b_dw_2, ln_g_2, ln_b_2, w_pw2_2, b_pw2_2, w_ffn_in_2, w_ffn_out_2,
):
    x = first_block(
        x, attn_pre_norm, w_in, lambda_q1, lambda_k1, lambda_q2, lambda_k2, diff_subln,
        k_cmp_pos, k_cmp_w1, k_cmp_w2, v_cmp_pos, v_cmp_w1, v_cmp_w2, w_out, attn_post_norm,
        ffn_pre_norm, w_gate, w_up, w_down, ffn_post_norm,
    )
    return second_block(
        x, norm_mix_pre_2, norm_mix_post_2, norm_ffn_pre_2, norm_ffn_post_2, w_in_2, b_forget_2,
        w_short_conv_2, w_out_2, w_pw1_2, b_pw1_2, w_dw_2, b_dw_2, ln_g_2, ln_b_2, w_pw2_2,
        b_pw2_2, w_ffn_in_2, w_ffn_out_2,
    )


_drawn_inputs = setup_inputs


def setup_inputs(seed=0):
    import zlib

    import numpy as np

    out = dict(_drawn_inputs(seed))
    spreads = {}
    factors = {'lambda_q2': 8.0,
     'k_cmp_pos': 8.0,
     'b_pw1_2': 5.798,
     'b_dw_2': 3.237,
     'ln_b_2': 6.635,
     'b_pw2_2': 3.814}
    for name, (base, spread) in spreads.items():
        noise = np.random.default_rng([zlib.crc32(name.encode()), seed]).standard_normal(out[name].shape)
        drawn = base * np.exp(spread * noise) if base else spread * noise
        out[name] = jnp.asarray(drawn.astype(out[name].dtype))
    for name, factor in factors.items():
        out[name] = (out[name] * factor).astype(out[name].dtype)
    return out
```

```python
import math
from contextlib import ExitStack, contextmanager

import numpy as np

import concourse.bass as bass
from concourse import mybir

P = 128
S = 512
D = 1024
KC = D // P
NB = S // P
HD = 64
F = 2816
FC = F // P
CMP_STRIDE, CMP_LEN = 16, 32
NCMP = (S - CMP_LEN) // CMP_STRIDE + 1
TAPS = 31
NEG = -1e30
EPS_RMS, EPS_LN = 1e-6, 1e-5
LAM_INIT = 0.8 - 0.6 * math.exp(-0.3 * 0)

UNIT, DOWN_UNIT = 8, FC // 2
SLOTS, RAW = 4, 4
A_PROJ = 23
A_CMP = 9
B_PROJ = 25
SEGMENTS = [(UNIT, A_PROJ + A_CMP + KC + 2 * FC), (DOWN_UNIT, 2 * KC),
            (UNIT, B_PROJ + KC + 2 * FC), (DOWN_UNIT, 2 * KC),
            (UNIT, 2 * KC + KC + 2 * FC), (DOWN_UNIT, 2 * KC)]

F32, F32R, BF16 = mybir.dt.float32, mybir.dt.float32r, mybir.dt.bfloat16
ALU = mybir.AluOpType
ACT = mybir.ActivationFunctionType
AX = mybir.AxisListType.X

_COLS = [("attn_pre", 8), ("attn_post", 8), ("ffn_pre", 8), ("ffn_post", 8),
         ("mix_pre_0", 8), ("mix_post_0", 8), ("ffn_pre_0", 8), ("ffn_post_0", 8),
         ("mix_pre_1", 8), ("mix_post_1", 8), ("ffn_pre_1", 8), ("ffn_post_1", 8),
         ("b_pw1", 16), ("b_dw", 8), ("ln_g", 8), ("ln_b", 8), ("b_pw2", 8), ("w_dw", 8 * TAPS), ("w_short", 12),
         ("subln", 1), ("b_forget", 1), ("k_pos", 32), ("v_pos", 32), ("lam", 4)]
COL, NCOL = {}, 0
for _name, _n in _COLS:
    COL[_name] = NCOL
    NCOL += _n
_TABS = [("rot", P), ("ident", P), ("causal", P), ("cmp_mask", NB * 32), ("cmp_keep", 32)]
TAB, NTAB = {}, 0
for _name, _n in _TABS:
    TAB[_name] = NTAB
    NTAB += _n


class Count:

    def __init__(self):
        self.base, self.reg, self.per = {}, None, {}

    def now(self, name, more=0):
        value = self.base.get(name, 0) + more
        return self.reg * self.per[name] + value if self.reg is not None and name in self.per else value

    def take(self, name, n=1):
        self.base[name] = self.base.get(name, 0) + n
        return self.now(name)

    @contextmanager
    def loop(self, engine, times, **per):
        start = dict(self.base)
        with engine.Fori(0, times) as i:
            self.reg, self.per = i, per
            yield i
        for name, value in self.base.items():
            assert value - start.get(name, 0) == per.get(name, 0), name
            self.base[name] = start.get(name, 0) + times * (value - start.get(name, 0))
        self.reg, self.per = None, {}


def diff_rows():
    return [("diff", h, 0, i) for h in range(4) for i in range(NB)]


def nsa_rows():
    return [("nsa", n, b, i) for n in range(8) for b in (1, 2) for i in range(NB)]


def fox_rows():
    return [("fox", n, 0, i) for n in range(8) for i in range(NB)]


def scores_of(row):
    return 2 if row[0] == "diff" else 1


LAG_TURN, LAG_MIX = 3, 4
TURNED_BY_ACT = (1, 2)


def two_blocks(nc, xt, cols_in, tabs_in, angles_in, w8, w11, out, stop):
    ctx = ExitStack()
    with ctx:
        def sb(name, shape, dt=F32, where=None):
            return (where or ctx).enter_context(nc.sbuf_tensor(name, shape, dt))

        def sem(name):
            return ctx.enter_context(nc.semaphore(name))

        x = sb("x", [P, KC, S])
        cols = sb("cols", [P, NCOL])
        tabs = sb("tabs", [P, NTAB])
        ones = sb("ones", [P, P])
        raw = sb("raw", [P, RAW, DOWN_UNIT * P])
        w_hi = sb("w_hi", [P, SLOTS, DOWN_UNIT * P], F32R)
        w_lo = sb("w_lo", [P, SLOTS, DOWN_UNIT * P], F32R)
        squares = sb("squares", [P, 2, S])
        total = sb("total", [P, S])
        scale_row = sb("scale_row", [P, S])
        variance = sb("variance", [P, NB])
        root = sb("root", [P, NB])
        scale_col = sb("scale_col", [P, NB])
        tmp = sb("tmp", [P, 2, S])
        ident16 = sb("ident16", [P, P], BF16)
        causal16 = sb("causal16", [P, P], BF16)
        lam = sb("lam", [P, 8])
        subln_s = sb("subln_s", [P, 1])
        k_cmp = sb("k_cmp", [P, 2 * NCMP])
        v_cmp = sb("v_cmp", [P, 2, 4 * HD])
        cmp_small = sb("cmp_small", [P, 4, NB, 8])
        diff_ms = sb("diff_ms", [P, 4, 16])
        region = ExitStack()
        h_hi = sb("h_hi", [P, KC, S], F32R, region)
        region.close()
        m_ffn = sb("m_ffn", [P, KC, S])
        h_lo = sb("h_lo", [P, KC, S], F32R)

        region = ExitStack()
        g_hi = sb("g_hi", [P, FC, S], F32R, region)
        g_lo = sb("g_lo", [P, FC, S], F32R, region)
        region.close()
        region = ExitStack()
        m_mix = sb("m_mix", [P, KC, S], F32, region)
        region.close()
        region = ExitStack()
        dqk = sb("dqk", [P, 8, S], F32, region)
        nqk = sb("nqk", [P, 8, S], F32, region)
        v_diff = sb("v_diff", [P, NB, 4 * P], F32, region)
        v_nsa = sb("v_nsa", [P, 2, NB, P], F32, region)
        o_all = sb("o_all", [P, NB, D], F32, region)
        gates = sb("gates", [P, NB, 24], F32, region)
        stage = ExitStack()
        angles = sb("angles", [P, 2, S], F32, stage)
        stage.close()
        stage = ExitStack()
        blocks_hi = sb("blocks_hi", [P, 2, 16, 2 * NCMP], F32R, stage)
        blocks_lo = sb("blocks_lo", [P, 2, 16, 2 * NCMP], F32R, stage)
        blocks = sb("blocks", [P, 2, 16, 2 * NCMP], F32, stage)
        hid = sb("hid", [P, 4, 2 * NCMP], F32, stage)
        hid_s = sb("hid_s", [P, 4, 2 * NCMP], F32, stage)
        hid_hi = sb("hid_hi", [P, 4, 2 * NCMP], F32R, stage)
        hid_lo = sb("hid_lo", [P, 4, 2 * NCMP], F32R, stage)
        stage.close()
        e_ring = sb("e_ring", [P, 2, 4, S], F32, region)
        t_ring = sb("t_ring", [P, 3, NB, P], F32, region)
        neg_max = sb("neg_max", [P, 96], F32, region)
        row_sum = sb("row_sum", [P, 96], F32, region)
        inv_sum = sb("inv_sum", [P, 96], F32, region)
        coef = sb("coef", [P, 96], F32, region)
        region.close()
        region = ExitStack()
        sb("below_m_mix_b", [P, 1], F32, region)
        q_fox = sb("q_fox", [HD + 1, 8, S], F32, region)
        k_fox = sb("k_fox", [HD + 1, 8, S], F32, region)
        v_fox = sb("v_fox", [P, NB, 8 * HD], F32, region)
        o_fox = sb("o_fox", [P, NB, 8 * HD], F32, region)
        y_conv = sb("y_conv", [P, 4, S], F32, region)
        padded = sb("padded", [P, S + 2], F32, region)
        e_ring_b = sb("e_ring_b", [P, 2, 4, S], F32, region)
        t_ring_b = sb("t_ring_b", [P, 3, NB, P], F32, region)
        neg_max_b = sb("neg_max_b", [P, 32], F32, region)
        row_sum_b = sb("row_sum_b", [P, 32], F32, region)
        inv_sum_b = sb("inv_sum_b", [P, 32], F32, region)
        region.close()
        region = ExitStack()
        forget = sb("forget", [8, 5, S], F32, region)
        region.close()
        region = ExitStack()
        sb("below_conformer", [P, KC, S], F32, region)
        glu = sb("glu", [P, KC, S + TAPS - 1], F32, region)
        y_dw = sb("y_dw", [P, KC, S], F32, region)
        region.close()

        psum = ctx.enter_context(nc.psum_tensor("psum", [P, 8, 512], F32))
        STAT_ROW, STAT_COL = 6, 7
        rot, ident = tabs[:, TAB["rot"]:TAB["rot"] + P], tabs[:, TAB["ident"]:TAB["ident"] + P]

        weights_landed = [sem(f"weights_landed_{j}") for j in range(RAW)]
        x_landed, consts_landed, decay_landed, stored = (sem(s) for s in ("x_landed", "consts_landed", "decay_landed", "stored"))
        unit_taken, high_split, units_split = sem("unit_taken"), sem("high_split"), sem("units_split")
        unit_done, col_summed, row_spread, rotated = (sem(s) for s in ("unit_done", "col_summed", "row_spread", "rotated"))
        lam_summed, cmp_scored, cmp_transposed, cmp_mixed = (
            sem(s) for s in ("lam_summed", "cmp_scored", "cmp_transposed", "cmp_mixed"))
        scored, transposed, mixed, o_turned = (sem(s) for s in ("scored", "transposed", "mixed", "o_turned"))
        evacuated, summed, col_scaled, col_ready, row_ready = (
            sem(s) for s in ("evacuated", "summed", "col_scaled", "col_ready", "row_ready"))
        x_ready, post_scaled, h_low = (sem(s) for s in ("x_ready", "post_scaled", "h_low"))
        set_up, rope_cos, rope_sin, rope_added, angles_scaled = (
            sem(s) for s in ("set_up", "rope_cos", "rope_sin", "rope_added", "angles_scaled"))
        blocks_added, blocks_low, hid_low, cmp_step, cmp_weighed, cmp_done = (
            sem(s) for s in ("blocks_added", "blocks_low", "hid_low", "cmp_step", "cmp_weighed", "cmp_done"))
        maxed, combined, coef_step, turned_dve, row_done, diff_step = (
            sem(s) for s in ("maxed", "combined", "coef_step", "turned_dve", "row_done", "diff_step"))
        hidden, hidden_low, mix_step, forget_step, conv_step, centred, normed = (
            sem(s) for s in ("hidden", "hidden_low", "mix_step", "forget_step", "conv_step", "centred", "normed"))
        h_high, squared, rooted, lam_exped, gates_ready = (
            sem(s) for s in ("h_high", "squared", "rooted", "lam_exped", "gates_ready"))
        blocks_high, hid_silu, hid_high, cmp_exped, cmp_turned = (
            sem(s) for s in ("blocks_high", "hid_silu", "hid_high", "cmp_exped", "cmp_turned"))
        exped, turned_act, diff_squared, diff_rooted = (
            sem(s) for s in ("exped", "turned_act", "diff_squared", "diff_rooted"))
        silu_ready, hidden_high, forget_act, sigmoid_ready, ln_silu = (
            sem(s) for s in ("silu_ready", "hidden_high", "forget_act", "sigmoid_ready", "ln_silu"))

        def col(name, j=0, n=1):
            return cols[:, bass.ds(j + COL[name], n)]

        ROPE = list(range(8)) + list(range(12, 17)) + [18, 20]
        A_TOKEN = {8, 9, 10, 11, 19, 21, 22}
        B_TOKEN = set(range(21, 25))

        def rope_place(u):
            return dqk[:, u, :] if u < 8 else nqk[:, u - 12, :] if u < 18 else nqk[:, 6 if u == 18 else 7, :]

        def fox_place(which):
            return {"gc": 0, "xa": 1, "gb": 2}[which]

        B_UNITS = [("f", 0)] + [(w, c) for c in range(4) for w in ("gc", "xa", "gb")] + \
                  [(w, c) for w in ("q", "k", "v") for c in range(4)]

        def query(row, m):
            kind, n, b, i = row
            t = slice(i * P, (i + 1) * P)
            if kind == "diff":
                return dqk[HD * m:HD * m + HD, n, t]
            if kind == "nsa":
                return nqk[HD * (n // 4):HD * (n // 4) + HD, n % 4, t]
            return q_fox[:, n, t]

        def keys(row, m):
            kind, n, b, i = row
            t = slice(0, (i + 1) * P)
            if kind == "diff":
                return dqk[HD * m:HD * m + HD, 4 + n, t]
            if kind == "nsa":
                return nqk[HD * (n // 4):HD * (n // 4) + HD, 5 + b, t]
            return k_fox[:, n, t]

        def values(row, j):
            kind, n, b, i = row
            if kind == "diff":
                return v_diff[:, j, n * P:(n + 1) * P]
            if kind == "nsa":
                return v_nsa[:, b - 1, j, HD * (n // 4):HD * (n // 4) + HD]
            return v_fox[:, j, HD * n:HD * n + HD]

        def mixed_place(row):
            kind, n, b, i = row
            if kind == "diff":
                return o_all[:, i, n * P:(n + 1) * P]
            if kind == "nsa":
                return o_all[:, i, 4 * P + HD * n:4 * P + HD * n + HD]
            return o_fox[:, i, HD * n:HD * n + HD]

        block = ctx.enter_context(nc.Block())

        @block.sync
        def _(sp):
            sp.dma_start(x[:], xt).then_inc(x_landed, 16)
            sp.dma_start(cols[:], cols_in).then_inc(consts_landed, 16)
            sp.dma_start(tabs[:], tabs_in).then_inc(consts_landed, 16)
            sp.dma_start(angles[:], angles_in).then_inc(consts_landed, 16)
            n = Count()
            at = {UNIT: 0, DOWN_UNIT: 0}

            def load(tiles, source, i, j):
                slot = j % RAW
                if n.base.get("units_split", 0) + 1 > RAW:
                    sp.wait_ge(units_split, n.now("units_split", 1 - RAW))
                n.take("units_split")
                sp.dma_start(raw[:, slot, 0:tiles * P], source[i]).then_inc(weights_landed[slot], 16)

            for tiles, count in SEGMENTS:
                source = w8 if tiles == UNIT else w11
                peel = SLOTS if n.base.get("units_split", 0) == 0 else 0
                for j in range(peel):
                    load(tiles, source, j, j)
                times, rest = divmod(count - peel, SLOTS)
                phase = n.base.get("units_split", 0)
                first = at[tiles] + peel
                with n.loop(sp, times, units_split=SLOTS) as i:
                    for j in range(SLOTS):
                        load(tiles, source, i * SLOTS + (first + j), phase + j)
                for j in range(rest):
                    load(tiles, source, first + times * SLOTS + j, phase + j)
                at[tiles] += count
            if stop == 99:
                for c in range(KC):
                    sp.wait_ge(x_ready, 5 * KC + c + 1)
                    sp.dma_start(out[:, c, :], x[:, c, :]).then_inc(stored, 16)
                sp.wait_ge(stored, 16 * KC)

        @block.gpsimd
        def _(pool):
            n = Count()

            def split(tiles, j):
                slot, w = j % SLOTS, tiles * P
                pool.wait_ge(weights_landed[j % RAW], n.take(f"landed_{j % RAW}", 16))
                if n.base.get("units", 0) >= SLOTS:
                    pool.wait_ge(unit_done, n.now("units", 1 - SLOTS))
                pool.sem_inc(unit_taken, 1)
                nc.gpsimd.tensor_scalar(w_hi[:, slot, 0:w], raw[:, j % RAW, 0:w], 1.0, 1.0, ALU.mult, ALU.mult)\
                    .then_inc(high_split, 1)
                pool.wait_ge(high_split, n.take("units"))
                nc.gpsimd.tensor_tensor(w_lo[:, slot, 0:w], raw[:, j % RAW, 0:w], w_hi[:, slot, 0:w].bitcast(F32),
                                        ALU.subtract).then_inc(units_split, 1)

            for tiles, count in SEGMENTS:
                peel = SLOTS if n.base.get("units", 0) == 0 else 0
                for j in range(peel):
                    split(tiles, j)
                times, rest = divmod(count - peel, SLOTS)
                phase = n.base.get("units", 0)
                per = {f"landed_{j}": 16 * SLOTS // RAW for j in range(RAW)}
                with n.loop(pool, times, units=SLOTS, **per):
                    for j in range(SLOTS):
                        split(tiles, phase + j)
                for j in range(rest):
                    split(tiles, phase + j)

        @block.tensor
        def _(pe):
            n = Count()

            def three(out_ap, lhs, rhs, first, last):
                pe.matmul(out_ap, lhs[0], rhs[0], start=first, stop=False)
                pe.matmul(out_ap, lhs[0], rhs[1], start=False, stop=False)
                return pe.matmul(out_ap, lhs[1], rhs[0], start=False, stop=last)

            def next_unit():
                slot = n.base.get("units_split", 0) % SLOTS
                pe.wait_ge(units_split, n.take("units_split"))
                return [lambda t, w=w: w[:, slot, t * P:(t + 1) * P] for w in (w_hi, w_lo)]

            def next_bank():
                g = n.base.get("group", 0)
                if g >= 4:
                    pe.wait_ge(evacuated, n.now("group", -3))
                n.take("group")
                return g % 4

            def feature_unit(h, tiles=UNIT, first=True, last=True, bank=None, width=S, k_wait=None):
                w = next_unit()
                for t in range(tiles):
                    if k_wait is not None:
                        pe.wait_ge(h_low, k_wait + t + 1)
                    mm = three(psum[:, bank, 0:width], [w[0](t), w[1](t)], h(t), first and t == 0,
                               last and t == tiles - 1)
                mm.then_inc(unit_done, 1)

            def token_unit(bank):
                w = next_unit()
                for b in range(NB):
                    for t in range(UNIT):
                        mm = three(psum[:, bank, b * P:(b + 1) * P],
                                   [h_hi[:, t, b * P:(b + 1) * P], h_lo[:, t, b * P:(b + 1) * P]],
                                   [w[0](t), w[1](t)], t == 0, t == UNIT - 1)
                mm.then_inc(unit_done, 1)

            def h_of(t):
                return [h_hi[:, t, :], h_lo[:, t, :]]

            def col_stat():
                pe.wait_ge(summed, n.take("summed", KC + 1))
                for b in range(NB):
                    mm = pe.matmul(psum[:, STAT_COL, b:b + 1], total[:, b * P:(b + 1) * P], ones[:, 0:1],
                                   start=True, stop=True)
                mm.then_inc(col_summed, 1)

            def row_stat():
                pe.wait_ge(col_ready, n.take("col_ready"))
                for b in range(NB):
                    mm = pe.matmul(psum[:, STAT_ROW, b * P:(b + 1) * P], scale_col[:, b:b + 1].to_broadcast([P, P]),
                                   ident, start=True, stop=True)
                mm.then_inc(row_spread, 1)

            def project(units, token=(), after=lambda u: None):
                start = n.base.get("h_low", 0)
                n.take("h_low", KC)
                for u in range(units):
                    bank = next_bank()
                    if u in token:
                        token_unit(bank)
                    else:
                        feature_unit(h_of, bank=bank, k_wait=start if u == 0 else None)
                    if u == 0:
                        col_stat()
                    if u == 1:
                        row_stat()
                    after(u)

            def w_out():
                start = n.base["h_low"]
                n.take("h_low", KC)
                for u in range(KC):
                    feature_unit(h_of, bank=next_bank(), k_wait=start if u == 0 else None)
                col_stat()
                row_stat()

            def swiglu():
                project(4)
                times = (2 * FC - 4) // 4
                with n.loop(pe, times, units_split=4, group=4):
                    for u in range(4):
                        feature_unit(h_of, bank=next_bank())
                pe.wait_ge(hidden_low, n.take("hidden_low", FC))
                with n.loop(pe, 2, units_split=8, group=4):
                    for c in range(4):
                        bank = next_bank()
                        for half in range(2):
                            feature_unit(lambda t: [g_hi[:, half * DOWN_UNIT + t, :], g_lo[:, half * DOWN_UNIT + t, :]],
                                         DOWN_UNIT, half == 0, half == 1, bank)
                col_stat()
                row_stat()

            def attention(rows, e, t_out):
                base = {k: n.base.get(k, 0) for k in ("scored", "rows", "combined", "turned_act", "turned_dve")}
                pe.wait_ge(evacuated, n.now("group"))
                first_score = np.cumsum([0] + [scores_of(r) for r in rows]).tolist()

                def turned_before(r, what):
                    return sum((row[3] in TURNED_BY_ACT) == (what == "act") for row in rows[:r + 1])

                def wait_turned(r):
                    act = rows[r][3] in TURNED_BY_ACT
                    pe.wait_ge(turned_act if act else turned_dve,
                               base["turned_act" if act else "turned_dve"] + turned_before(r, "act" if act else "dve"))

                for t in range(len(rows) + LAG_MIX):
                    if t < len(rows):
                        i = rows[t][3]
                        for m in range(scores_of(rows[t])):
                            s = first_score[t] + m
                            if s >= 4:
                                pe.wait_ge(exped, base["scored"] + s - 3)
                            pe.matmul(psum[:, s % 4, 0:(i + 1) * P], query(rows[t], m), keys(rows[t], m),
                                      start=True, stop=False)
                            pe.matmul(psum[:, s % 4, i * P:(i + 1) * P], ident16[:], causal16[:],
                                      start=False, stop=True).then_inc(scored, 1)
                    r = t - LAG_TURN
                    if 0 <= r < len(rows):
                        if rows[r][0] == "diff":
                            pe.wait_ge(combined, base["combined"] + r + 1)
                        else:
                            pe.wait_ge(exped, base["scored"] + first_score[r + 1])
                        if r >= 2:
                            wait_turned(r - 2)
                        for j in range(rows[r][3] + 1):
                            mm = pe.transpose(psum[:, 4 + r % 2, j * P:(j + 1) * P], e[:, 0, r % 4, j * P:(j + 1) * P],
                                              ident)
                        mm.then_inc(transposed, 1)
                    r = t - LAG_MIX
                    if 0 <= r < len(rows):
                        wait_turned(r)
                        if r >= 2:
                            pe.wait_ge(row_done, base["rows"] + r - 1)
                        width = P if rows[r][0] == "diff" else HD
                        for j in range(rows[r][3] + 1):
                            mm = pe.matmul(psum[:, 6 + r % 2, 0:width], t_out[:, r % 3, j, :], values(rows[r], j),
                                           start=j == 0, stop=j == rows[r][3])
                        mm.then_inc(mixed, 1)
                n.take("scored", first_score[-1])
                n.take("rows", len(rows))
                n.take("combined", sum(r[0] == "diff" for r in rows))
                n.take("turned_act", turned_before(len(rows), "act"))
                n.take("turned_dve", turned_before(len(rows), "dve"))

            def turn_outputs(o, chunks, done):
                for c in range(chunks):
                    if c >= 4:
                        pe.wait_ge(h_low, done + c - 3)
                    for b in range(NB):
                        mm = pe.transpose(psum[:, 4 + c % 4, b * P:(b + 1) * P], o[:, b, c * P:(c + 1) * P], ident)
                    mm.then_inc(o_turned, 1)

            pe.wait_ge(consts_landed, 48)
            pe.wait_ge(set_up, 4)
            pe.matmul(psum[:, STAT_COL, 8:10], ones[0:HD, :], lam[0:HD, 0:2], start=True, stop=True).then_inc(lam_summed, 1)

            def rotate(u):
                if u - 1 in ROPE:
                    r = ROPE.index(u - 1)
                    pe.wait_ge(evacuated, u)
                    if r >= 2:
                        pe.wait_ge(rope_sin, r - 1)
                    pe.matmul(psum[:, 4 + r % 2, :], rot, tmp[:, r % 2, :], start=True, stop=True).then_inc(rotated, 1)

            project(A_PROJ, A_TOKEN, rotate)
            if stop == 1:
                return

            for kind in range(2):
                pe.wait_ge(blocks_low, kind + 1)
                for m in range(2):
                    bank = next_bank()
                    for half in range(2):
                        feature_unit(lambda t: [blocks_hi[:, kind, half * UNIT + t, :], blocks_lo[:, kind, half * UNIT + t, :]],
                                     UNIT, half == 0, half == 1, bank, 2 * NCMP)
            pe.wait_ge(hid_low, 1)
            bank = next_bank()
            w = next_unit()
            for m in range(2):
                three(psum[:, bank, 0:2 * NCMP], [w[0](m), w[1](m)], [hid_hi[:, m, :], hid_lo[:, m, :]], m == 0, m == 1)
            for g in range(2):
                part = slice(g * NCMP, (g + 1) * NCMP)
                for m in range(2):
                    mm = three(psum[0:NCMP, bank, HD + g * HD:2 * HD + g * HD],
                               [hid_hi[:, 2 + m, part], hid_lo[:, 2 + m, part]],
                               [w[0](2 + m)[:, 0:HD], w[1](2 + m)[:, 0:HD]], m == 0, m == 1)
            mm.then_inc(unit_done, 1)

            pe.wait_ge(evacuated, n.now("group"))
            for i in range(NB):
                for head in range(8):
                    g = head // 4
                    mm = pe.matmul(psum[:, i + NB * g, 32 * (head % 4):32 * (head % 4) + NCMP], nqk[HD * g:HD * g + HD, head % 4, i * P:(i + 1) * P],
                                   k_cmp[HD * g:HD * g + HD, g * NCMP:(g + 1) * NCMP], start=True, stop=True)
                mm.then_inc(cmp_scored, 1)
            for i in range(NB):
                pe.wait_ge(cmp_weighed, i + 1)
                for g in range(2):
                    if i >= 1:
                        pe.wait_ge(cmp_turned, 2 * i + g - 1)
                    pe.transpose(psum[:, 4 + g, 0:P], e_ring[:, 0, i, g * P:(g + 1) * P], ident).then_inc(cmp_transposed, 1)
                if i >= 2:
                    pe.wait_ge(cmp_done, i - 1)
                for g in range(2):
                    pe.wait_ge(cmp_turned, 2 * i + g + 1)
                    mm = pe.matmul(psum[:, 6 + i % 2, g * 4 * HD:(g + 1) * 4 * HD], t_ring[:, g, i, :], v_cmp[:, g, :],
                                   start=True, stop=True)
                mm.then_inc(cmp_mixed, 1)
            pe.wait_ge(cmp_done, NB)
            if stop == 2:
                return

            attention(diff_rows() + nsa_rows(), e_ring, t_ring)
            pe.wait_ge(row_done, n.now("rows"))
            pe.wait_ge(diff_step, 5)
            turn_outputs(o_all, KC, n.base["h_low"])
            w_out()
            if stop == 3:
                return
            swiglu()
            if stop == 4:
                return

            project(B_PROJ, B_TOKEN)
            pe.wait_ge(decay_landed, 16 * 8)
            attention(fox_rows(), e_ring_b, t_ring_b)
            pe.wait_ge(row_done, n.now("rows"))
            turn_outputs(o_fox, 4, n.base["h_low"])
            w_out()
            if stop == 5:
                return
            swiglu()
            if stop == 6:
                return

            project(4)
            with n.loop(pe, 3, units_split=4, group=4):
                for u in range(4):
                    feature_unit(h_of, bank=next_bank())
            col_stat()
            row_stat()
            col_stat()
            row_stat()
            w_out()
            if stop == 7:
                return
            swiglu()

        @block.scalar
        def _(act):
            n = Count()

            def copy(out_ap, in_ap, **kw):
                return nc.scalar.activation(out_ap, in_ap, ACT.Copy, **kw)

            def square(c, source, j):
                base = n.base.get("summed", 0)
                if base or j >= 2:
                    act.wait_ge(summed, base + (j if j >= 2 else 0))
                nc.scalar.activation(squares[:, c, :], source, ACT.Square).then_inc(squared, 1)

            def stat_done():
                n.take("summed", KC + 1)

            def roots():
                act.wait_ge(col_scaled, n.take("col_scaled"))
                nc.scalar.activation(root[:], variance[:], ACT.Sqrt).then_inc(rooted, 1)

            def norm(pre):
                for c in range(KC):
                    act.wait_ge(x_ready, n.take("x_ready"))
                    copy(h_hi[:, c, :], x[:, c, :], scale=col(pre, c)).then_inc(h_high, 1)
                    square(c % 2, x[:, c, :], c)
                stat_done()
                roots()

            def outputs(m, loops):
                if loops:
                    start = n.base["summed"]
                    for c in range(2):
                        act.wait_ge(evacuated, n.take("evacuated"))
                        square(c % 2, m[:, c, :], c)
                    n.base["sq"] = start
                    with n.loop(act, 3, evacuated=2, sq=2) as i:
                        for c in range(2):
                            act.wait_ge(evacuated, n.take("evacuated"))
                            act.wait_ge(summed, n.take("sq") + 1)
                            nc.scalar.activation(squares[:, c, :], m[:, i * 2 + (2 + c), :], ACT.Square).then_inc(squared, 1)
                stat_done()
                roots()

            def swiglu(m):
                def chunk(f):
                    act.wait_ge(evacuated, n.take("evacuated"))
                    nc.scalar.activation(squares[:, 0, :], tmp[:, 0, :], ACT.Silu).then_inc(silu_ready, 1)
                    n.take("evacuated")
                    act.wait_ge(hidden, n.take("hidden"))
                    copy(g_hi[:, f, :], squares[:, 1, :]).then_inc(hidden_high, 1)

                chunk(0)
                chunk(1)
                with n.loop(act, FC // 2 - 1, evacuated=4, hidden=2) as i:
                    chunk(i * 2 + 2)
                    chunk(i * 2 + 3)
                outputs(m, True)

            def attention(rows, e, t_out, maxima, sums, extra=lambda t: None):
                base = {k: n.base.get(k, 0) for k in ("scored", "rows")}
                first_score = np.cumsum([0] + [scores_of(r) for r in rows]).tolist()
                for t in range(len(rows) + LAG_TURN + 1):
                    if t < len(rows):
                        i = rows[t][3]
                        if t >= 4:
                            act.wait_ge(transposed, base["rows"] + t - 3)
                        for m in range(scores_of(rows[t])):
                            s = first_score[t] + m
                            act.wait_ge(maxed, base["scored"] + s + 1)
                            nc.scalar.activation(e[:, m, t % 4, 0:(i + 1) * P], psum[:, s % 4, 0:(i + 1) * P], ACT.Exp,
                                                 bias=maxima[:, s:s + 1], accum_out=sums[:, s:s + 1]).then_inc(exped, 1)
                    r = t - LAG_TURN
                    if 0 <= r < len(rows) and rows[r][3] in TURNED_BY_ACT:
                        act.wait_ge(transposed, base["rows"] + r + 1)
                        if r >= 3:
                            act.wait_ge(mixed, base["rows"] + r - 2)
                        w = (rows[r][3] + 1) * P
                        copy(t_out[:, r % 3, 0:rows[r][3] + 1, :].rearrange("p b q -> p (b q)"), psum[:, 4 + r % 2, 0:w])\
                            .then_inc(turned_act, 1)
                    extra(t)
                n.take("scored", first_score[-1])
                n.take("rows", len(rows))

            def turn_outputs(chunks, scale, first):
                for c in range(chunks):
                    act.wait_ge(o_turned, n.take("o_turned"))
                    kw = dict(scale=subln_s[:, 0:1]) if scale and c < 4 else {}
                    copy(h_hi[:, first + c, :], psum[:, 4 + c % 4, :], **kw).then_inc(h_high, 1)

            act.wait_ge(lam_summed, 1)
            nc.scalar.activation(lam[:, 2:4], psum[:, STAT_COL, 8:10], ACT.Exp).then_inc(lam_exped, 1)

            act.wait_ge(x_landed, 16)
            act.wait_ge(consts_landed, 48)
            for c in range(KC):
                copy(h_hi[:, c, :], x[:, c, :], scale=col("attn_pre", c)).then_inc(h_high, 1)
                square(c % 2, x[:, c, :], c)
            stat_done()
            roots()
            n.take("evacuated", A_PROJ)
            act.wait_ge(evacuated, n.now("evacuated"))
            nc.scalar.activation(gates[:], gates[:], ACT.Sigmoid).then_inc(gates_ready, 1)
            if stop == 1:
                return

            for kind in range(2):
                act.wait_ge(blocks_added, 8 * (kind + 1))
                copy(blocks_hi[:, kind, :, :], blocks[:, kind, :, :]).then_inc(blocks_high, 1)
            n.take("evacuated", 4)
            act.wait_ge(evacuated, n.now("evacuated"))
            nc.scalar.activation(hid_s[:], hid[:], ACT.Silu).then_inc(hid_silu, 1)
            act.wait_ge(hid_silu, 1)
            copy(hid_hi[:], hid_s[:]).then_inc(hid_high, 1)
            n.take("evacuated")
            for i in range(NB):
                act.wait_ge(cmp_step, 4 * i + 5)
                nc.scalar.activation(e_ring[:, 0, i, 0:256], e_ring[:, 0, i, 0:256], ACT.Exp).then_inc(cmp_exped, 1)
            for i in range(NB):
                for g in range(2):
                    act.wait_ge(cmp_transposed, 2 * i + g + 1)
                    copy(t_ring[:, g, i, :], psum[:, 4 + g, 0:P]).then_inc(cmp_turned, 1)
            if stop == 2:
                return

            def diff_norm(t):
                if t == 24:
                    act.wait_ge(row_done, 16)
                    nc.scalar.activation(m_ffn[:, 0:4, :], o_all[:, :, 0:4 * P], ACT.Square).then_inc(diff_squared, 1)
                if t == 30:
                    act.wait_ge(diff_step, 3)
                    nc.scalar.activation(diff_ms[:, 2, :], diff_ms[:, 1, :], ACT.Sqrt).then_inc(diff_rooted, 1)

            attention(diff_rows() + nsa_rows(), e_ring, t_ring, neg_max, row_sum, diff_norm)
            turn_outputs(KC, True, 0)
            for c in range(KC):
                act.wait_ge(evacuated, n.take("evacuated"))
                square(c % 2, m_mix[:, c, :], c)
            stat_done()
            roots()
            if stop == 3:
                return
            norm("ffn_pre")
            swiglu(m_ffn)
            if stop == 4:
                return

            norm("mix_pre_0")
            act.wait_ge(forget_step, 4)
            nc.scalar.activation(forget[:, 3, :], forget[:, 2, :], ACT.Exp, scale=-1.0).then_inc(forget_act, 1)
            act.wait_ge(forget_act, 1)
            nc.scalar.activation(forget[:, 4, :], forget[:, 3, :], ACT.Ln, bias=1.0).then_inc(forget_act, 1)
            act.wait_ge(forget_step, 6)
            for head in range(8):
                act.dma_start(k_fox[HD:HD + 1, head, :], forget[head:head + 1, 3, :]).then_inc(decay_landed, 16)
            n.take("evacuated", B_PROJ)
            for c in range(4):
                act.wait_ge(mix_step, 5 * (c + 1))
                if c == 0:
                    act.wait_ge(unit_done, sum(c for _, c in SEGMENTS[:2]) + B_PROJ)
                copy(h_hi[:, c, :], y_conv[:, c, :]).then_inc(h_high, 1)
            attention(fox_rows(), e_ring_b, t_ring_b, neg_max_b, row_sum_b)
            turn_outputs(4, False, 4)
            for c in range(KC):
                act.wait_ge(evacuated, n.take("evacuated"))
                square(c % 2, m_mix[:, c, :], c)
            stat_done()
            roots()
            if stop == 5:
                return
            norm("ffn_pre_0")
            swiglu(m_ffn)
            if stop == 6:
                return

            norm("mix_pre_1")

            def gate(c):
                act.wait_ge(evacuated, n.take("evacuated"))
                nc.scalar.activation(squares[:, 0, :], tmp[:, 0, :], ACT.Sigmoid, bias=col("b_pw1", c + KC)).then_inc(sigmoid_ready, 1)
                n.take("evacuated")

            gate(0)
            gate(1)
            with n.loop(act, 3, evacuated=4) as i:
                gate(i * 2 + 2)
                gate(i * 2 + 3)
            stat_done()
            for c in range(KC):
                act.wait_ge(centred, c + 1)
                square(c % 2, y_dw[:, c, :], c)
            stat_done()
            roots()
            for c in range(KC):
                act.wait_ge(normed, c + 1)
                if c >= 2:
                    act.wait_ge(h_low, n.base.get("h_low", 0) + 6 * KC + c - 1)
                nc.scalar.activation(squares[:, c % 2, :], tmp[:, c % 2, :], ACT.Silu, scale=col("ln_g", c),
                                     bias=col("ln_b", c)).then_inc(ln_silu, 1)
                act.wait_ge(ln_silu, c + 1)
                copy(h_hi[:, c, :], squares[:, c % 2, :]).then_inc(h_high, 1)
            for c in range(KC):
                act.wait_ge(evacuated, n.take("evacuated"))
                if c < 2:
                    act.wait_ge(h_low, n.base.get("h_low", 0) + 6 * KC + KC)
                square(c % 2, m_mix[:, c, :], c)
            stat_done()
            roots()
            if stop == 7:
                return
            norm("ffn_pre_1")
            swiglu(m_ffn)
            act.wait_ge(x_ready, 1)

        @block.vector
        def _(dve):
            n = Count()
            v = nc.vector

            def clear_total():
                v.memset(total[:], 0.0).then_inc(summed, 1)
                n.take("summed")

            def add_square(c):
                dve.wait_ge(squared, n.take("squared"))
                dve.wait_ge(summed, n.now("summed"))
                v.tensor_tensor(total[:], total[:], squares[:, c, :], ALU.add).then_inc(summed, 1)
                n.take("summed")

            def stat(eps):
                dve.wait_ge(col_summed, n.take("col_summed"))
                v.tensor_scalar(variance[:], psum[:, STAT_COL, 0:NB], 1.0 / D, eps, ALU.mult, ALU.add).then_inc(col_scaled, 1)
                dve.wait_ge(rooted, n.take("rooted"))
                v.reciprocal(scale_col[:], root[:]).then_inc(col_ready, 1)
                row()

            def row():
                dve.wait_ge(row_spread, n.take("row_spread"))
                v.tensor_copy(scale_row[:], psum[:, STAT_ROW, :]).then_inc(row_ready, 1)
                dve.wait_ge(row_ready, n.take("row_ready"))

            def low_part(c, pre):
                dve.wait_ge(h_high, n.take("h_high"))
                v.scalar_tensor_tensor(h_lo[:, c, :], x[:, c, :], col(pre, c), h_hi[:, c, :].bitcast(F32),
                                       ALU.mult, ALU.subtract).then_inc(h_low, 1)
                n.take("h_low")

            def norm(m, post, pre):
                if pre:
                    clear_total()
                for c in range(KC + 1):
                    if c < KC:
                        v.scalar_tensor_tensor(tmp[:, c % 2, :], m[:, c, :], col(post, c), scale_row[:], ALU.mult, ALU.mult)\
                            .then_inc(post_scaled, 1)
                        dve.wait_ge(post_scaled, n.take("post_scaled"))
                        v.tensor_tensor(x[:, c, :], x[:, c, :], tmp[:, c % 2, :], ALU.add).then_inc(x_ready, 1)
                        n.take("x_ready")
                    if c and pre:
                        low_part(c - 1, pre)
                        add_square((c - 1) % 2)
                if pre:
                    stat(EPS_RMS)

            def group(u=1):
                bank = n.base.get("evacuated", 0) % 4
                dve.wait_ge(unit_done, n.take("unit_done", u))
                n.take("evacuated")
                return psum[:, bank, :]

            def outputs(m, times, units, bias=None):
                clear_total()

                def one(c, place):
                    source = group(units)
                    if bias:
                        v.tensor_scalar(m[:, c, :], source, col(bias, c), None, ALU.add).then_inc(evacuated, 1)
                    else:
                        v.tensor_copy(m[:, c, :], source).then_inc(evacuated, 1)
                    add_square(place)

                if times == 1:
                    for c in range(KC):
                        one(c, c % 2)
                else:
                    with n.loop(dve, times, unit_done=4 * units, evacuated=4, squared=4, summed=4) as i:
                        for c in range(4):
                            one(i * 4 + c, c % 2)
                stat(EPS_RMS)

            def swiglu(m):
                def chunk(f):
                    v.tensor_tensor(tmp[:, 0, :], group(), scale_row[:], ALU.mult).then_inc(evacuated, 1)
                    v.tensor_tensor(tmp[:, 1, :], group(), scale_row[:], ALU.mult).then_inc(evacuated, 1)
                    dve.wait_ge(silu_ready, n.take("silu_ready"))
                    dve.wait_ge(evacuated, n.now("evacuated"))
                    v.tensor_tensor(squares[:, 1, :], squares[:, 0, :], tmp[:, 1, :], ALU.mult).then_inc(hidden, 1)
                    dve.wait_ge(hidden_high, n.take("hidden_high"))
                    v.tensor_tensor(g_lo[:, f, :], squares[:, 1, :], g_hi[:, f, :].bitcast(F32), ALU.subtract)\
                        .then_inc(hidden_low, 1)

                chunk(0)
                chunk(1)
                with n.loop(dve, FC // 2 - 1, unit_done=4, evacuated=4, silu_ready=2, hidden_high=2) as i:
                    chunk(i * 2 + 2)
                    chunk(i * 2 + 3)
                outputs(m, 2, 2)

            def attention(rows, e, t_out, maxima, sums, inverse, extra=lambda t: None):
                base = {k: n.base.get(k, 0) for k in ("scored", "rows")}
                first_score = np.cumsum([0] + [scores_of(r) for r in rows]).tolist()
                for t in range(len(rows) + LAG_MIX + 1):
                    if t < len(rows):
                        for m in range(scores_of(rows[t])):
                            s = first_score[t] + m
                            dve.wait_ge(scored, base["scored"] + s + 1)
                            v.tensor_reduce(maxima[:, s:s + 1], psum[:, s % 4, 0:(rows[t][3] + 1) * P], AX, ALU.max, negate=True)\
                                .then_inc(maxed, 1)
                    r = t - 2
                    if 0 <= r < len(rows) and rows[r][0] == "diff":
                        s = first_score[r]
                        w = (rows[r][3] + 1) * P
                        dve.wait_ge(exped, base["scored"] + s + 2)
                        v.reciprocal(inverse[:, s + 1:s + 2], sums[:, s + 1:s + 2]).then_inc(coef_step, 1)
                        dve.wait_ge(coef_step, n.take("coef_step"))
                        v.scalar_tensor_tensor(coef[:, s:s + 1], sums[:, s:s + 1], inverse[:, s + 1:s + 2], lam[:, 5:6],
                                               ALU.mult, ALU.mult).then_inc(coef_step, 1)
                        dve.wait_ge(coef_step, n.take("coef_step"))
                        v.scalar_tensor_tensor(e[:, 0, r % 4, 0:w], e[:, 1, r % 4, 0:w], coef[:, s:s + 1], e[:, 0, r % 4, 0:w],
                                               ALU.mult, ALU.add).then_inc(combined, 1)
                    r = t - LAG_TURN
                    if 0 <= r < len(rows) and rows[r][3] not in TURNED_BY_ACT:
                        dve.wait_ge(transposed, base["rows"] + r + 1)
                        if r >= 3:
                            dve.wait_ge(mixed, base["rows"] + r - 2)
                        w = (rows[r][3] + 1) * P
                        v.tensor_copy(t_out[:, r % 3, 0:rows[r][3] + 1, :].rearrange("p b q -> p (b q)"), psum[:, 4 + r % 2, 0:w])\
                            .then_inc(turned_dve, 1)
                    r = t - LAG_MIX
                    if 0 <= r < len(rows):
                        kind, head, b, i = rows[r]
                        s = first_score[r]
                        v.reciprocal(inverse[:, s:s + 1], sums[:, s:s + 1]).then_inc(coef_step, 1)
                        dve.wait_ge(coef_step, n.take("coef_step"))
                        dve.wait_ge(mixed, base["rows"] + r + 1)
                        place = mixed_place(rows[r])
                        if kind == "nsa":
                            v.tensor_scalar(coef[:, s:s + 1], inverse[:, s:s + 1], gates[:, i, 3 * head + b:3 * head + b + 1],
                                            None, ALU.mult).then_inc(coef_step, 1)
                            dve.wait_ge(coef_step, n.take("coef_step"))
                            if b == 2:
                                dve.wait_ge(row_done, base["rows"] + r - NB + 1)
                            v.scalar_tensor_tensor(place, psum[:, 6 + r % 2, 0:HD], coef[:, s:s + 1], place,
                                                   ALU.mult, ALU.add).then_inc(row_done, 1)
                        else:
                            width = P if kind == "diff" else HD
                            v.tensor_scalar(place, psum[:, 6 + r % 2, 0:width], inverse[:, s:s + 1], None, ALU.mult)\
                                .then_inc(row_done, 1)
                    extra(t)
                n.take("scored", first_score[-1])
                n.take("rows", len(rows))

            def turn_outputs(chunks, scale, first):
                for c in range(chunks):
                    dve.wait_ge(h_high, n.take("h_high"))
                    hi = h_hi[:, first + c, :].bitcast(F32)
                    if scale and c < 4:
                        ins = v.scalar_tensor_tensor(h_lo[:, first + c, :], psum[:, 4 + c % 4, :], subln_s[:, 0:1], hi,
                                                     ALU.mult, ALU.subtract)
                    else:
                        ins = v.tensor_tensor(h_lo[:, first + c, :], psum[:, 4 + c % 4, :], hi, ALU.subtract)
                    ins.then_inc(h_low, 1)
                    n.take("h_low")

            v.memset(ones[:], 1.0).then_inc(set_up, 1)
            v.memset(v_cmp[:], 0.0)
            dve.wait_ge(consts_landed, 48)
            v.tensor_copy(ident16[:], ident).then_inc(set_up, 1)
            v.tensor_copy(causal16[:], tabs[:, TAB["causal"]:TAB["causal"] + P]).then_inc(set_up, 1)
            c0 = COL["lam"]
            v.tensor_tensor(lam[0:HD, 0:2], cols[0:HD, c0:c0 + 4:2], cols[0:HD, c0 + 1:c0 + 4:2], ALU.mult).then_inc(set_up, 1)
            v.tensor_scalar(subln_s[:], col("subln"), 1.0 - LAM_INIT, None, ALU.mult).then_inc(set_up, 1)
            dve.wait_ge(x_landed, 16)
            clear_total()
            for c in range(KC):
                low_part(c, "attn_pre")
                add_square(c % 2)
            dve.wait_ge(lam_exped, 1)
            v.tensor_tensor(lam[:, 4:5], lam[:, 3:4], lam[:, 2:3], ALU.subtract).then_inc(set_up, 1)
            dve.wait_ge(set_up, 6)
            v.tensor_scalar(lam[:, 5:6], lam[:, 4:5], -LAM_INIT, None, ALU.add).then_inc(set_up, 1)
            stat(EPS_RMS)
            for j in range(2):
                v.tensor_tensor(angles[:, j, :], angles[:, j, :], scale_row[:], ALU.mult).then_inc(angles_scaled, 1)

            def rotate(u):
                r = ROPE.index(u)
                scale = HD ** -0.5 if u < 4 or 12 <= u < 16 else 1.0
                if r == 0:
                    dve.wait_ge(angles_scaled, 2)
                else:
                    dve.wait_ge(rope_added, r)
                dve.wait_ge(evacuated, u + 1)
                v.scalar_tensor_tensor(squares[:, 0, :], tmp[:, r % 2, :], scale, angles[:, 0, :], ALU.mult, ALU.mult)\
                    .then_inc(rope_cos, 1)
                dve.wait_ge(rotated, r + 1)
                v.scalar_tensor_tensor(squares[:, 1, :], psum[:, 4 + r % 2, :], scale, angles[:, 1, :], ALU.mult, ALU.mult)\
                    .then_inc(rope_sin, 1)
                dve.wait_ge(rope_cos, r + 1)
                dve.wait_ge(rope_sin, r + 1)
                v.tensor_tensor(rope_place(u), squares[:, 0, :], squares[:, 1, :], ALU.add).then_inc(rope_added, 1)

            def by_token(out_ap, bank, width=P):
                source = bank.rearrange("p (b f) -> p b f", b=NB)[:, :, 0:width]
                v.tensor_tensor(out_ap, source, scale_col[:].unsqueeze(2).to_broadcast([P, NB, width]), ALU.mult)\
                    .then_inc(evacuated, 1)

            for u in range(A_PROJ):
                bank = group()
                if u in ROPE:
                    v.tensor_copy(tmp[:, ROPE.index(u) % 2, :], bank).then_inc(evacuated, 1)
                elif 8 <= u < 12:
                    by_token(v_diff[:, :, (u - 8) * P:(u - 7) * P], bank)
                elif u in (19, 21):
                    by_token(v_nsa[:, (u - 19) // 2, :, :], bank)
                elif u == 22:
                    by_token(gates[:], bank, 24)
                else:
                    v.tensor_tensor(nqk[:, 5, :], bank, scale_row[:], ALU.mult).then_inc(evacuated, 1)
                if u - 1 in ROPE:
                    rotate(u - 1)
            if stop == 1:
                dve.wait_ge(rope_added, len(ROPE))
                dve.wait_ge(gates_ready, 1)
                return

            dve.wait_ge(rope_added, len(ROPE))
            dve.wait_ge(evacuated, A_PROJ)
            for kind in range(2):
                for g in range(2):
                    half = slice(g * HD, (g + 1) * HD)
                    tokens = nqk[half, 4 + kind, :].rearrange("p (n s) -> p n s", s=CMP_STRIDE)
                    for parity in range(2):
                        for a in range(2):
                            place = blocks[parity * HD:(parity + 1) * HD, kind, 8 * a:8 * a + 8, g * NCMP:(g + 1) * NCMP]
                            p0 = COL["k_pos" if kind == 0 else "v_pos"] + 16 * a + parity
                            pos = cols[half, p0:p0 + 15:2].unsqueeze(1).to_broadcast([HD, NCMP, 8])
                            v.tensor_tensor(place.rearrange("p b n -> p n b"), tokens[:, a:a + NCMP, parity:CMP_STRIDE:2], pos,
                                            ALU.add).then_inc(blocks_added, 1)
            dve.wait_ge(blocks_added, 16)
            for kind in range(2):
                dve.wait_ge(blocks_high, kind + 1)
                v.tensor_tensor(blocks_lo[:, kind, :, :], blocks[:, kind, :, :], blocks_hi[:, kind, :, :].bitcast(F32), ALU.subtract)\
                    .then_inc(blocks_low, 1)
            for j in range(4):
                v.tensor_copy(hid[:, j, :], group(2)[:, 0:2 * NCMP]).then_inc(evacuated, 1)
            dve.wait_ge(hid_high, 1)
            v.tensor_tensor(hid_lo[:], hid_s[:], hid_hi[:].bitcast(F32), ALU.subtract).then_inc(hid_low, 1)
            bank = group()
            v.tensor_copy(k_cmp[:], bank[:, 0:2 * NCMP])
            for g in range(2):
                for j in range(4):
                    ins = v.tensor_copy(v_cmp[32 * j:32 * j + NCMP, g, j * HD:(j + 1) * HD],
                                        bank[0:NCMP, HD + g * HD:2 * HD + g * HD])
            ins.then_inc(evacuated, 1)
            dve.wait_ge(hid_low, 1)
            v.memset(e_ring[:, 0, :, 0:256], NEG).then_inc(cmp_step, 1)
            dve.wait_ge(gates_ready, 1)
            for i in range(NB):
                e = e_ring[:, 0, i, 0:256].rearrange("p (h n) -> p h n", h=8)
                mask = tabs[:, TAB["cmp_mask"] + 32 * i:TAB["cmp_mask"] + 32 * i + NCMP].unsqueeze(1).to_broadcast([P, 4, NCMP])
                if i == 0:
                    dve.wait_ge(cmp_step, 1)
                dve.wait_ge(cmp_scored, i + 1)
                for g in range(2):
                    v.tensor_tensor(e[:, 4 * g:4 * g + 4, 0:NCMP],
                                    psum[:, i + NB * g, 0:P].rearrange("p (h n) -> p h n", h=4)[:, :, 0:NCMP], mask, ALU.add)\
                        .then_inc(cmp_step, 1)
                dve.wait_ge(cmp_step, 4 * i + 3)
                v.tensor_reduce(cmp_small[:, 0, i, :], e, AX, ALU.max).then_inc(cmp_step, 1)
                dve.wait_ge(cmp_step, 4 * i + 4)
                v.tensor_tensor(e, e, cmp_small[:, 0, i, :].unsqueeze(2).to_broadcast([P, 8, 32]), ALU.subtract).then_inc(cmp_step, 1)
            steps = 1 + 4 * NB
            for i in range(NB):
                e = e_ring[:, 0, i, 0:256].rearrange("p (h n) -> p h n", h=8)
                dve.wait_ge(cmp_exped, i + 1)
                v.tensor_reduce(cmp_small[:, 1, i, :], e, AX, ALU.add).then_inc(cmp_step, 1)
                dve.wait_ge(cmp_step, steps + 1)
                v.reciprocal(cmp_small[:, 2, i, :], cmp_small[:, 1, i, :]).then_inc(cmp_step, 1)
                dve.wait_ge(cmp_step, steps + 2)
                v.tensor_tensor(cmp_small[:, 3, i, :], cmp_small[:, 2, i, :], gates[:, i, 0:24:3], ALU.mult).then_inc(cmp_step, 1)
                steps += 3
                if i == 0:
                    keep = tabs[:, TAB["cmp_keep"]:TAB["cmp_keep"] + 32].unsqueeze(1).to_broadcast([P, 8, 32])
                    v.tensor_tensor(e, e, keep, ALU.mult).then_inc(cmp_step, 1)
                    steps += 1
                dve.wait_ge(cmp_step, steps)
                v.tensor_tensor(e, e, cmp_small[:, 3, i, :].unsqueeze(2).to_broadcast([P, 8, 32]), ALU.mult).then_inc(cmp_weighed, 1)
            for i in range(NB):
                dve.wait_ge(cmp_mixed, i + 1)
                v.tensor_copy(o_all[:, i, 4 * P:D], psum[:, 6 + i % 2, :]).then_inc(cmp_done, 1)
            dve.wait_ge(cmp_done, NB)
            if stop == 2:
                return

            def diff_norm(t):
                o = o_all[:, :, 0:4 * P].rearrange("p b (h e) -> p b h e", h=4)
                sixteen = [diff_ms[:, j, :].rearrange("p (b h) -> p b h", b=NB) for j in range(4)]
                if t == 26:
                    dve.wait_ge(diff_squared, 1)
                    v.tensor_reduce(diff_ms[:, 0, :], m_ffn[:, 0:4, :].rearrange("p b (h e) -> p (b h) e", h=4), AX, ALU.add)\
                        .then_inc(diff_step, 1)
                if t == 27:
                    dve.wait_ge(diff_step, 1)
                    v.tensor_scalar(diff_ms[:, 3, :], diff_ms[:, 0, :], 1.0 / P, EPS_RMS, ALU.mult, ALU.add).then_inc(diff_step, 1)
                    dve.wait_ge(diff_step, 2)
                    v.tensor_copy(diff_ms[:, 1, :], diff_ms[:, 3, :]).then_inc(diff_step, 1)
                if t == 31:
                    dve.wait_ge(diff_rooted, 1)
                    v.reciprocal(diff_ms[:, 3, :], diff_ms[:, 2, :]).then_inc(diff_step, 1)
                    dve.wait_ge(diff_step, 4)
                    dve.wait_ge(row_done, 16)
                    for b in range(NB):
                        part = o_all[:, b, 0:4 * P].rearrange("p (h e) -> p h e", h=4)
                        ins = v.tensor_tensor(part, part, diff_ms[:, 3, 4 * b:4 * b + 4].unsqueeze(2).to_broadcast([P, 4, P]), ALU.mult)
                    ins.then_inc(diff_step, 1)

            attention(diff_rows() + nsa_rows(), e_ring, t_ring, neg_max, row_sum, inv_sum, diff_norm)
            turn_outputs(KC, True, 0)
            outputs(m_mix, 1, 1)
            norm(m_mix, "attn_post", "ffn_pre")
            if stop == 3:
                return
            swiglu(m_ffn)
            norm(m_ffn, "ffn_post", "mix_pre_0")
            if stop == 4:
                return

            for which, c in B_UNITS:
                bank = group()
                if which == "f":
                    v.tensor_tensor(forget[:, 0, :], bank[0:8, :], scale_row[0:8, :], ALU.mult).then_inc(evacuated, 1)
                    dve.wait_ge(evacuated, n.now("evacuated"))
                    v.tensor_scalar(forget[:, 1, :], forget[:, 0, :], cols[0:8, COL["b_forget"]:COL["b_forget"] + 1], None, ALU.add)\
                        .then_inc(forget_step, 1)
                    dve.wait_ge(forget_step, 1)
                    v.tensor_scalar(forget[:, 0, :], forget[:, 1, :], 0.0, None, ALU.min).then_inc(forget_step, 1)
                    v.memset(forget[:, 3, :], 1.0).then_inc(forget_step, 1)
                    v.scalar_tensor_tensor(forget[:, 2, :], forget[:, 1, :], -1.0, forget[:, 1, :], ALU.mult, ALU.max)\
                        .then_inc(forget_step, 1)
                    dve.wait_ge(forget_act, 2)
                    v.tensor_tensor(forget[:, 1, :], forget[:, 4, :], forget[:, 0, :], ALU.subtract).then_inc(forget_step, 1)
                    dve.wait_ge(forget_step, 5)
                    v.tensor_tensor_scan(forget[:, 3, :], ones[0:8, 0:1].to_broadcast([8, S]), forget[:, 1, :], 0.0,
                                         ALU.mult, ALU.add).then_inc(forget_step, 1)
                    v.memset(padded[:, 0:2], 0.0)
                elif which in ("gc", "xa"):
                    if c:
                        dve.wait_ge(mix_step, n.now("mix_step"))
                    v.tensor_tensor(tmp[:, int(which == "xa"), :], bank, scale_row[:], ALU.mult).then_inc(evacuated, 1)
                elif which == "gb":
                    dve.wait_ge(evacuated, n.now("evacuated", -1))
                    v.tensor_tensor(padded[:, 2:S + 2], tmp[:, 0, :], tmp[:, 1, :], ALU.mult).then_inc(mix_step, 1)
                    dve.wait_ge(mix_step, n.take("mix_step"))
                    v.tensor_tensor(tmp[:, 0, :], bank, scale_row[:], ALU.mult).then_inc(evacuated, 1)
                    w = [col("w_short", 3 * c + k) for k in range(3)]
                    v.tensor_scalar(squares[:, 0, :], padded[:, 0:S], w[0], None, ALU.mult).then_inc(mix_step, 1)
                    dve.wait_ge(mix_step, n.take("mix_step"))
                    v.scalar_tensor_tensor(squares[:, 1, :], padded[:, 1:S + 1], w[1], squares[:, 0, :], ALU.mult, ALU.add)\
                        .then_inc(mix_step, 1)
                    dve.wait_ge(mix_step, n.take("mix_step"))
                    v.scalar_tensor_tensor(squares[:, 0, :], padded[:, 2:S + 2], w[2], squares[:, 1, :], ALU.mult, ALU.add)\
                        .then_inc(mix_step, 1)
                    dve.wait_ge(mix_step, n.take("mix_step"))
                    dve.wait_ge(evacuated, n.now("evacuated"))
                    v.tensor_tensor(y_conv[:, c, :], squares[:, 0, :], tmp[:, 0, :], ALU.mult).then_inc(mix_step, 1)
                    n.take("mix_step")
                elif which in ("q", "k"):
                    if (which, c) == ("q", 0):
                        dve.wait_ge(decay_landed, 16 * 8)
                        v.memset(q_fox[HD:HD + 1, :, :], 1.0)
                    place = q_fox if which == "q" else k_fox
                    scale = HD ** -0.5 if which == "q" else 1.0
                    for half in range(2):
                        part = slice(half * HD, (half + 1) * HD)
                        ins = v.scalar_tensor_tensor(place[0:HD, 2 * c + half, :], bank[part, :], scale, scale_row[part, :],
                                                     ALU.mult, ALU.mult)
                    ins.then_inc(evacuated, 1)
                else:
                    by_token(v_fox[:, :, c * P:(c + 1) * P], bank)
            for c in range(4):
                dve.wait_ge(h_high, n.take("h_high"))
                v.tensor_tensor(h_lo[:, c, :], y_conv[:, c, :], h_hi[:, c, :].bitcast(F32), ALU.subtract).then_inc(h_low, 1)
                n.take("h_low")
            attention(fox_rows(), e_ring_b, t_ring_b, neg_max_b, row_sum_b, inv_sum_b)
            turn_outputs(4, False, 4)
            outputs(m_mix, 1, 1)
            norm(m_mix, "mix_post_0", "ffn_pre_0")
            if stop == 5:
                return
            swiglu(m_ffn)
            norm(m_ffn, "ffn_post_0", "mix_pre_1")
            if stop == 6:
                return

            clear_total()
            v.memset(glu[:, :, 0:TAPS - 1], 0.0).then_inc(conv_step, 1)
            n.take("conv_step")

            def conformer_chunk(c):
                v.tensor_tensor(tmp[:, 0, :], group(), scale_row[:], ALU.mult).then_inc(evacuated, 1)
                v.tensor_tensor(tmp[:, 1, :], group(), scale_row[:], ALU.mult).then_inc(evacuated, 1)
                dve.wait_ge(sigmoid_ready, n.take("sigmoid_ready"))
                dve.wait_ge(evacuated, n.now("evacuated"))
                v.scalar_tensor_tensor(glu[:, c, TAPS - 1:TAPS - 1 + S], tmp[:, 1, :], col("b_pw1", c), squares[:, 0, :], ALU.add, ALU.mult)\
                    .then_inc(conv_step, 1)
                dve.wait_ge(conv_step, n.take("conv_step"))
                v.tensor_scalar(y_dw[:, c, :], glu[:, c, 0:S], col("w_dw", c * TAPS), col("b_dw", c), ALU.mult, ALU.add)\
                    .then_inc(conv_step, 1)
                for k in range(1, TAPS):
                    dve.wait_ge(conv_step, n.take("conv_step"))
                    v.scalar_tensor_tensor(y_dw[:, c, :], glu[:, c, k:k + S], col("w_dw", c * TAPS + k), y_dw[:, c, :],
                                           ALU.mult, ALU.add).then_inc(conv_step, 1)
                dve.wait_ge(conv_step, n.take("conv_step"))
                dve.wait_ge(summed, n.now("summed"))
                v.tensor_tensor(total[:], total[:], y_dw[:, c, :], ALU.add).then_inc(summed, 1)
                n.take("summed")

            conformer_chunk(0)
            conformer_chunk(1)
            with n.loop(dve, 3, unit_done=4, evacuated=4, sigmoid_ready=2, conv_step=2 * (TAPS + 1), summed=2) as i:
                conformer_chunk(i * 2 + 2)
                conformer_chunk(i * 2 + 3)
            dve.wait_ge(col_summed, n.take("col_summed"))
            v.tensor_scalar(scale_col[:], psum[:, STAT_COL, 0:NB], 1.0 / D, None, ALU.mult).then_inc(col_ready, 1)
            row()
            clear_total()
            for c in range(KC + 1):
                if c < KC:
                    v.tensor_tensor(y_dw[:, c, :], y_dw[:, c, :], scale_row[:], ALU.subtract).then_inc(centred, 1)
                if c:
                    add_square((c - 1) % 2)
            stat(EPS_LN)
            for c in range(KC + 1):
                if c < KC:
                    if c >= 2:
                        dve.wait_ge(ln_silu, c - 1)
                    v.tensor_tensor(tmp[:, c % 2, :], y_dw[:, c, :], scale_row[:], ALU.mult).then_inc(normed, 1)
                if c:
                    dve.wait_ge(h_high, n.take("h_high"))
                    v.tensor_tensor(h_lo[:, c - 1, :], squares[:, (c - 1) % 2, :], h_hi[:, c - 1, :].bitcast(F32), ALU.subtract)\
                        .then_inc(h_low, 1)
                    n.take("h_low")
            outputs(m_mix, 1, 1, "b_pw2")
            norm(m_mix, "mix_post_1", "ffn_pre_1")
            if stop == 7:
                return
            swiglu(m_ffn)
            norm(m_ffn, "ffn_post_1", None)


def shape_tables():
    inv = (1.0 / (np.float32(10000.0) ** (np.arange(0, HD, 2, dtype=np.float32) / np.float32(HD)))).astype(np.float32)
    angle = np.arange(S, dtype=np.float32)[:, None] * inv[None, :]
    which = np.arange(P) % 32
    angles = np.stack([np.cos(angle).T[which], np.sin(angle).T[which]], axis=1).astype(np.float32)
    t = np.zeros((P, NTAB), np.float32)
    out = np.arange(P)
    lower = out % HD < 32
    t[np.where(lower, out + 32, out - 32), TAB["rot"] + out] = np.where(lower, -1.0, 1.0)
    t[:, TAB["ident"]:TAB["ident"] + P] = np.eye(P)
    t[:, TAB["causal"]:TAB["causal"] + P] = np.where(np.arange(P)[None, :] <= np.arange(P)[:, None], 0.0, NEG)
    token = np.arange(S).reshape(NB, P).T
    end = np.arange(32) * CMP_STRIDE + CMP_LEN - 1
    seen = (end[None, None, :] <= token[:, :, None]) & (np.arange(32) < NCMP)
    t[:, TAB["cmp_mask"]:TAB["cmp_mask"] + NB * 32] = np.where(seen, 0.0, NEG).reshape(P, NB * 32)
    t[:, TAB["cmp_keep"]:TAB["cmp_keep"] + 32] = seen[:, 0, :]
    return angles, t


def tiles_of(w, rows, cols):
    return w.reshape(-1, P, w.shape[1])[rows, :, cols * P:(cols + 1) * P].transpose(1, 0, 2)


def pad_columns(w, n):
    out = np.zeros((w.shape[0], n), w.dtype)
    out[:, :w.shape[1]] = w
    return out


def lay_out(a):
    a = {k: np.asarray(v) for k, v in a.items()}
    w_in = a["w_in"][0]
    nq = 12 * P
    order = np.concatenate([np.arange(nq)] + [np.arange(nq + HD * (c + 4 * g), nq + HD * (c + 4 * g) + HD)
                                              for c in range(4) for g in range(2)] + [np.arange(nq + 8 * HD, w_in.shape[1])])
    w_in = pad_columns(w_in[:, order], A_PROJ * P)
    all8 = slice(0, 8)
    wide = [tiles_of(w_in, all8, c) for c in range(A_PROJ)]
    for name in ("k_cmp_w1", "v_cmp_w1"):
        wide += [tiles_of(a[name][0], slice(8 * half, 8 * half + 8), m) for m in range(2) for half in range(2)]
    w2 = np.zeros((P, 8, P), np.float32)
    k2, v2 = a["k_cmp_w2"][0].reshape(2, P, HD), a["v_cmp_w2"][0].reshape(2, P, HD)
    for m in range(2):
        w2[:, m, 0:HD] = w2[:, m, HD:P] = k2[m]
        w2[:, 2 + m, 0:HD] = v2[m]
    wide.append(w2)
    down = []

    def swiglu(gate, up, w_down):
        for f in range(FC):
            wide.extend([tiles_of(gate, all8, f), tiles_of(up, all8, f)])
        for c in range(KC):
            down.extend([tiles_of(w_down, slice(DOWN_UNIT * h, DOWN_UNIT * (h + 1)), c) for h in range(2)])

    wide += [tiles_of(a["w_out"][0], all8, c) for c in range(KC)]
    swiglu(a["w_gate"][0], a["w_up"][0], a["w_down"][0])
    w = a["w_in_2"][0]
    wide.append(tiles_of(pad_columns(w[:, 24 * P:], P), all8, 0))
    for c in range(4):
        wide += [tiles_of(w, all8, 4 + c), tiles_of(w, all8, 8 + c), tiles_of(w, all8, c)]
    wide += [tiles_of(w, all8, 12 + c) for c in range(12)]
    wide += [tiles_of(a["w_out_2"][0], all8, c) for c in range(KC)]
    swiglu(a["w_ffn_in_2"][0][:, :F], a["w_ffn_in_2"][0][:, F:], a["w_ffn_out_2"][0])
    for c in range(KC):
        wide += [tiles_of(a["w_pw1_2"][0], all8, KC + c), tiles_of(a["w_pw1_2"][0], all8, c)]
    wide += [tiles_of(a["w_pw2_2"][0], all8, c) for c in range(KC)]
    swiglu(a["w_ffn_in_2"][1][:, :F], a["w_ffn_in_2"][1][:, F:], a["w_ffn_out_2"][1])

    cols = np.zeros((P, NCOL), np.float32)

    def put(name, vector):
        vector = vector.reshape(-1, P).T
        cols[:, COL[name]:COL[name] + vector.shape[1]] = vector

    for name, source in (("attn_pre", a["attn_pre_norm"][0]), ("attn_post", a["attn_post_norm"][0]),
                         ("ffn_pre", a["ffn_pre_norm"][0]), ("ffn_post", a["ffn_post_norm"][0]),
                         ("b_pw1", a["b_pw1_2"][0]), ("b_dw", a["b_dw_2"][0]), ("ln_g", a["ln_g_2"][0]),
                         ("ln_b", a["ln_b_2"][0]), ("b_pw2", a["b_pw2_2"][0]), ("subln", a["diff_subln"][0])):
        put(name, source)
    for j in range(2):
        put(f"mix_pre_{j}", a["norm_mix_pre_2"][j])
        put(f"mix_post_{j}", a["norm_mix_post_2"][j])
        put(f"ffn_pre_{j}", a["norm_ffn_pre_2"][j])
        put(f"ffn_post_{j}", a["norm_ffn_post_2"][j])
    cols[:, COL["w_dw"]:COL["w_dw"] + 8 * TAPS] = a["w_dw_2"][0].reshape(TAPS, KC, P).transpose(2, 1, 0).reshape(P, -1)
    cols[:, COL["w_short"]:COL["w_short"] + 12] = a["w_short_conv_2"][0].reshape(3, 4, P).transpose(2, 1, 0).reshape(P, -1)
    cols[0:8, COL["b_forget"]] = a["b_forget_2"][0]
    for name, source in (("k_pos", a["k_cmp_pos"][0]), ("v_pos", a["v_cmp_pos"][0])):
        cols[0:HD, COL[name]:COL[name] + 32] = cols[HD:P, COL[name]:COL[name] + 32] = source.T
    for j, name in enumerate(("lambda_q1", "lambda_k1", "lambda_q2", "lambda_k2")):
        cols[0:HD, COL["lam"] + j] = a[name][0]
    angles, tables = shape_tables()
    return {
        "in_xt": np.ascontiguousarray(a["x"][0].reshape(S, KC, P).transpose(2, 1, 0)),
        "in_cols": cols, "in_tables": tables, "in_angles": angles,
        "in_wide": np.ascontiguousarray(np.stack(wide)).reshape(len(wide), P, UNIT * P),
        "in_down": np.ascontiguousarray(np.stack(down)).reshape(len(down), P, DOWN_UNIT * P),
    }


def declare(nc, arrays, stop=99):
    ins = [nc.dram_tensor(k, v.shape, F32, kind="ExternalInput").ap() for k, v in arrays.items()]
    out = nc.dram_tensor("out", (P, KC, S), F32, kind="ExternalOutput").ap()
    two_blocks(nc, *ins, out, stop)


def kernel(**inputs):
    import concourse.bacc as _bacc
    from concourse.bass_utils import run_bass_kernel_spmd as _run
    arrays = lay_out(inputs)
    nc = _bacc.Bacc("TRN2", target_bir_lowering=False, num_devices=1, dynamic_dma_scratch_size=1024)
    declare(nc, arrays)
    got = _run(nc, [arrays], core_ids=[0]).results[0]["out"]
    return np.ascontiguousarray(got.transpose(2, 1, 0).reshape(1, S, D))
```

```python
import math
from contextlib import ExitStack, contextmanager

import numpy as np

import concourse.bass as bass
from concourse import mybir

P = 128
S = 512
D = 1024
KC = D // P
NB = S // P
HD = 64
F = 2816
FC = F // P
CMP_STRIDE, CMP_LEN = 16, 32
NCMP = (S - CMP_LEN) // CMP_STRIDE + 1
TAPS = 31
NEG = -1e30
EPS_RMS, EPS_LN = 1e-6, 1e-5
LAM_INIT = 0.8 - 0.6 * math.exp(-0.3 * 0)

UNIT, DOWN_UNIT = 8, FC // 2
SLOTS, RAW = 4, 4
A_ORDER = ["kc", "vc", "nq0", "nq1", "nq2", "cmp0", "nq3", "cmp1", "gates", "cmp2", "ks", "cmp3", "vs", "w2", "kw", "vw"] + \
          [f"{w}{c}" for w in ("dq", "dk", "dv") for c in range(4)]
A_CHUNK = {**{f"{w}{c}": 4 * j + c for j, w in enumerate(("dq", "dk", "dv", "nq")) for c in range(4)},
           "kc": 16, "vc": 17, "ks": 18, "vs": 19, "kw": 20, "vw": 21, "gates": 22}
A_UNITS = sum(2 if a.startswith("cmp") else 1 for a in A_ORDER)
CMP_FROM = A_ORDER.index("kw") + 1
B_ORDER = ["f"] + [f"{w}{c}" for c in range(4) for w in ("gc", "xa", "gb")] + [f"{w}{c}" for w in "vqk" for c in range(4)]
B_CHUNK = {**{f"{w}{c}": 4 * j + c for j, w in enumerate(("gb", "gc", "xa", "q", "k", "v")) for c in range(4)}, "f": 24}
SEGMENTS = [(UNIT, A_UNITS + KC + 2 * FC), (DOWN_UNIT, 2 * KC),
            (UNIT, len(B_ORDER) + KC + 2 * FC), (DOWN_UNIT, 2 * KC),
            (UNIT, 2 * KC + KC + 2 * FC), (DOWN_UNIT, 2 * KC)]
_A, _B = A_UNITS + KC, len(B_ORDER) + KC
_FFN = 2 * FC + 2 * KC
NORMS_AT = [_A, _A + _FFN, _A + _FFN + _B, _A + 2 * _FFN + _B, _A + 2 * _FFN + _B + 3 * KC, _A + 3 * _FFN + _B + 3 * KC]
A_NQ_ROPES = 5
CONV_ORDER = [0, 1, 4, 5, 6, 7, 2, 3]
CONV_PE = (2, 3)


def partnered_chunk(name):
    if name[:2] in ("dq", "dk", "nq", "kc", "ks", "kw"):
        return "rope"
    return "turn" if name[:2] in ("dv", "vs", "vw", "ga", "v0", "v1", "v2", "v3") else None


F32, F32R, BF16 = mybir.dt.float32, mybir.dt.float32r, mybir.dt.bfloat16
ALU = mybir.AluOpType
ACT = mybir.ActivationFunctionType
AX = mybir.AxisListType.X

_COLS = [("attn_pre", 8), ("attn_post", 8), ("ffn_pre", 8), ("ffn_post", 8),
         ("mix_pre_0", 8), ("mix_post_0", 8), ("ffn_pre_0", 8), ("ffn_post_0", 8),
         ("mix_pre_1", 8), ("mix_post_1", 8), ("ffn_pre_1", 8), ("ffn_post_1", 8),
         ("b_pw1", 16), ("b_dw", 8), ("ln_g", 8), ("ln_b", 8), ("b_pw2", 8), ("w_dw", 8 * TAPS), ("w_short", 12),
         ("subln", 1), ("b_forget", 1), ("k_pos", 32), ("v_pos", 32), ("lam", 4)]
COL, NCOL = {}, 0
for _name, _n in _COLS:
    COL[_name] = NCOL
    NCOL += _n
_TABS = [("rot", P), ("ident", P), ("causal", P), ("cmp_mask", NB * 32), ("cmp_keep", 32)]
TAB, NTAB = {}, 0
for _name, _n in _TABS:
    TAB[_name] = NTAB
    NTAB += _n


class Count:

    def __init__(self):
        self.base, self.reg, self.per = {}, None, {}

    def now(self, name, more=0):
        value = self.base.get(name, 0) + more
        return self.reg * self.per[name] + value if self.reg is not None and name in self.per else value

    def take(self, name, n=1):
        self.base[name] = self.base.get(name, 0) + n
        return self.now(name)

    @contextmanager
    def loop(self, engine, times, **per):
        start = dict(self.base)
        with engine.Fori(0, times) as i:
            self.reg, self.per = i, per
            yield i
        for name, value in self.base.items():
            assert value - start.get(name, 0) == per.get(name, 0), name
            self.base[name] = start.get(name, 0) + times * (value - start.get(name, 0))
        self.reg, self.per = None, {}


def diff_rows():
    return [("diff", h, 0, i) for h in range(4) for i in range(NB)]


def nsa_rows():
    return [("nsa", n, b, i) for n in range(8) for b in (1, 2) for i in range(NB)]


def fox_rows():
    return [("fox", n, 0, i) for n in range(8) for i in range(NB)]


def scores_of(row):
    return 2 if row[0] == "diff" else 1


LAG_TURN, LAG_MIX = 3, 4
TURNED_BY_ACT = (1, 2)


def two_blocks(nc, xt, cols_in, tabs_in, angles_in, w8, w11, out, stop):
    ctx = ExitStack()
    with ctx:
        def sb(name, shape, dt=F32, where=None):
            return (where or ctx).enter_context(nc.sbuf_tensor(name, shape, dt))

        def sem(name):
            return ctx.enter_context(nc.semaphore(name))

        x = sb("x", [P, KC, S])
        cols = sb("cols", [P, NCOL])
        tabs = sb("tabs", [P, NTAB])
        ones = sb("ones", [P, P])
        raw = sb("raw", [P, RAW, DOWN_UNIT * P])
        w_hi = sb("w_hi", [P, SLOTS, DOWN_UNIT * P], F32R)
        w_lo = sb("w_lo", [P, SLOTS, DOWN_UNIT * P], F32R)
        squares = sb("squares", [P, 2, S])
        total = sb("total", [P, S])
        scale_row = sb("scale_row", [P, S])
        variance = sb("variance", [P, NB])
        root = sb("root", [P, NB])
        scale_col = sb("scale_col", [P, NB])
        tmp = sb("tmp", [P, 2, S])
        ident16 = sb("ident16", [P, P], BF16)
        causal16 = sb("causal16", [P, P], BF16)
        spare = sb("spare", [P, 1])
        lam = sb("lam", [P, 8])
        subln_s = sb("subln_s", [P, 1])
        k_cmp = sb("k_cmp", [P, 2 * NCMP])
        v_cmp = sb("v_cmp", [P, 2, 4 * HD])
        cmp_small = sb("cmp_small", [P, 4, NB, 8])
        diff_ms = sb("diff_ms", [P, 4, 16])
        region = ExitStack()
        h_hi = sb("h_hi", [P, KC, S], F32R, region)
        region.close()
        m_ffn = sb("m_ffn", [P, KC, S])
        h_lo = sb("h_lo", [P, KC, S], F32R)

        region = ExitStack()
        g_hi = sb("g_hi", [P, FC, S], F32R, region)
        g_lo = sb("g_lo", [P, FC, S], F32R, region)
        region.close()
        region = ExitStack()
        m_mix = sb("m_mix", [P, KC, S], F32, region)
        region.close()
        region = ExitStack()
        dqk = sb("dqk", [P, 8, S], F32, region)
        nqk = sb("nqk", [P, 8, S], F32, region)
        v_diff = sb("v_diff", [P, NB, 4 * P], F32, region)
        v_nsa = sb("v_nsa", [P, 2, NB, P], F32, region)
        o_all = sb("o_all", [P, NB, D], F32, region)
        gates = sb("gates", [P, NB, 24], F32, region)
        angles = o_all[:, 0:2, 0:S]
        stage = ExitStack()
        blocks_hi = sb("blocks_hi", [P, 2, 16, 2 * NCMP], F32R, stage)
        blocks_lo = sb("blocks_lo", [P, 2, 16, 2 * NCMP], F32R, stage)
        blocks = sb("blocks", [P, 2, 16, 2 * NCMP], F32, stage)
        hid = sb("hid", [P, 4, 2 * NCMP], F32, stage)
        hid_s = sb("hid_s", [P, 4, 2 * NCMP], F32, stage)
        hid_hi = sb("hid_hi", [P, 4, 2 * NCMP], F32R, stage)
        hid_lo = sb("hid_lo", [P, 4, 2 * NCMP], F32R, stage)
        stage.close()
        e_ring = sb("e_ring", [P, 2, 4, S], F32, region)
        t_ring = sb("t_ring", [P, 3, NB, P], F32, region)
        neg_max = sb("neg_max", [P, 96], F32, region)
        row_sum = sb("row_sum", [P, 96], F32, region)
        inv_sum = sb("inv_sum", [P, 96], F32, region)
        coef = sb("coef", [P, 96], F32, region)
        region.close()
        region = ExitStack()
        sb("below_m_mix_b", [P, 1], F32, region)
        q_fox = sb("q_fox", [HD + 1, 8, S], F32, region)
        k_fox = sb("k_fox", [HD + 1, 8, S], F32, region)
        v_fox = sb("v_fox", [P, NB, 8 * HD], F32, region)
        o_fox = sb("o_fox", [P, NB, 8 * HD], F32, region)
        y_conv = sb("y_conv", [P, 4, S], F32, region)
        padded = sb("padded", [P, S + 2], F32, region)
        e_ring_b = sb("e_ring_b", [P, 2, 4, S], F32, region)
        t_ring_b = sb("t_ring_b", [P, 3, NB, P], F32, region)
        neg_max_b = sb("neg_max_b", [P, 32], F32, region)
        row_sum_b = sb("row_sum_b", [P, 32], F32, region)
        inv_sum_b = sb("inv_sum_b", [P, 32], F32, region)
        region.close()
        region = ExitStack()
        forget = sb("forget", [8, 5, S], F32, region)
        region.close()
        region = ExitStack()
        glu = sb("glu", [P, KC, S + TAPS - 1], F32, region)
        y_dw = sb("y_dw", [P, KC, S], F32, region)
        diag_hi = sb("diag_hi", [P, TAPS, P], F32R, region)
        diag_lo = sb("diag_lo", [P, TAPS, P], F32R, region)
        glu_hi = sb("glu_hi", [P, 2, S + TAPS - 1], F32R, region)
        glu_lo = sb("glu_lo", [P, 2, S + TAPS - 1], F32R, region)
        taps_hi = sb("taps_hi", [P, 2 * TAPS], F32R, region)
        taps_lo = sb("taps_lo", [P, 2 * TAPS], F32, region)
        region.close()

        psum = ctx.enter_context(nc.psum_tensor("psum", [P, 8, 512], F32))
        STAT_ROW, STAT_COL = 6, 7
        rot, ident = tabs[:, TAB["rot"]:TAB["rot"] + P], tabs[:, TAB["ident"]:TAB["ident"] + P]

        weights_landed = [sem(f"weights_landed_{j}") for j in range(RAW)]
        x_landed = [sem(f"x_landed_{j}") for j in range(4)]
        cols_landed, tabs_landed, decay_landed, stored = (
            sem(s) for s in ("cols_landed", "tabs_landed", "decay_landed", "stored"))
        unit_taken, high_split, units_split = sem("unit_taken"), sem("high_split"), sem("units_split")
        x_ready = sem("x_ready")
        unit_done, col_summed, column_added, row_spread, partnered, conv_done, tap_used = (
            sem(s) for s in ("unit_done", "col_summed", "column_added", "row_spread", "partnered", "conv_done", "tap_used"))
        lam_summed, cmp_scored, cmp_transposed, cmp_mixed = (
            sem(s) for s in ("lam_summed", "cmp_scored", "cmp_transposed", "cmp_mixed"))
        scored, transposed, mixed, o_turned = (sem(s) for s in ("scored", "transposed", "mixed", "o_turned"))
        evacuated, summed, col_scaled, col_ready, row_ready = (
            sem(s) for s in ("evacuated", "summed", "col_scaled", "col_ready", "row_ready"))
        post_scaled, h_low = sem("post_scaled"), sem("h_low")
        set_up, rope_cos, rope_added, angles_scaled, partner_read = (
            sem(s) for s in ("set_up", "rope_cos", "rope_added", "angles_scaled", "partner_read"))
        conv_chunk, glu_low, taps_split = sem("conv_chunk"), sem("glu_low"), sem("taps_split")
        blocks_added, blocks_low, hid_low, cmp_step, cmp_weighed, cmp_done = (
            sem(s) for s in ("blocks_added", "blocks_low", "hid_low", "cmp_step", "cmp_weighed", "cmp_done"))
        maxed, combined, coef_step, turned_dve, row_done, diff_step = (
            sem(s) for s in ("maxed", "combined", "coef_step", "turned_dve", "row_done", "diff_step"))
        hidden, hidden_low, mix_step, forget_step, conv_step, centred, normed = (
            sem(s) for s in ("hidden", "hidden_low", "mix_step", "forget_step", "conv_step", "centred", "normed"))
        glu_high, diag_ready = sem("glu_high"), sem("diag_ready")
        h_high, squared, rooted, lam_exped, gates_ready = (
            sem(s) for s in ("h_high", "squared", "rooted", "lam_exped", "gates_ready"))
        blocks_high, hid_silu, hid_high, cmp_exped, cmp_turned = (
            sem(s) for s in ("blocks_high", "hid_silu", "hid_high", "cmp_exped", "cmp_turned"))
        exped, turned_act, diff_squared, diff_rooted = (
            sem(s) for s in ("exped", "turned_act", "diff_squared", "diff_rooted"))
        silu_ready, hidden_high, forget_act, sigmoid_ready, ln_silu = (
            sem(s) for s in ("silu_ready", "hidden_high", "forget_act", "sigmoid_ready", "ln_silu"))

        def col(name, j=0, n=1):
            return cols[:, bass.ds(j + COL[name], n)]

        def rope_place(name):
            c = int(name[2]) if name[2:] else 0
            return {"dq": dqk[:, c, :], "dk": dqk[:, 4 + c, :], "nq": nqk[:, c, :], "kc": nqk[:, 4, :],
                    "ks": nqk[:, 6, :], "kw": nqk[:, 7, :]}[name[:2]]

        def query(row, m):
            kind, n, b, i = row
            t = slice(i * P, (i + 1) * P)
            if kind == "diff":
                return dqk[HD * m:HD * m + HD, n, t]
            if kind == "nsa":
                return nqk[HD * (n // 4):HD * (n // 4) + HD, n % 4, t]
            return q_fox[:, n, t]

        def keys(row, m):
            kind, n, b, i = row
            t = slice(0, (i + 1) * P)
            if kind == "diff":
                return dqk[HD * m:HD * m + HD, 4 + n, t]
            if kind == "nsa":
                return nqk[HD * (n // 4):HD * (n // 4) + HD, 5 + b, t]
            return k_fox[:, n, t]

        def values(row, j):
            kind, n, b, i = row
            if kind == "diff":
                return v_diff[:, j, n * P:(n + 1) * P]
            if kind == "nsa":
                return v_nsa[:, b - 1, j, HD * (n // 4):HD * (n // 4) + HD]
            return v_fox[:, j, HD * n:HD * n + HD]

        def mixed_place(row):
            kind, n, b, i = row
            if kind == "diff":
                return o_all[:, i, n * P:(n + 1) * P]
            if kind == "nsa":
                return o_all[:, i, 4 * P + HD * n:4 * P + HD * n + HD]
            return o_fox[:, i, HD * n:HD * n + HD]

        block = ctx.enter_context(nc.Block())

        @block.sync
        def _(sp):
            sp.dma_start(cols[:], cols_in).then_inc(cols_landed, 16)
            n = Count()
            at = {UNIT: 0, DOWN_UNIT: 0}

            def load(tiles, source, i, j):
                slot = j % RAW
                if n.base.get("units_split", 0) + 1 > RAW:
                    sp.wait_ge(units_split, n.now("units_split", 1 - RAW))
                n.take("units_split")
                sp.dma_start(raw[:, slot, 0:tiles * P], source[i]).then_inc(weights_landed[slot], 16)

            for tiles, count in SEGMENTS:
                source = w8 if tiles == UNIT else w11
                peel = SLOTS if n.base.get("units_split", 0) == 0 else 0
                for j in range(peel):
                    load(tiles, source, j, j)
                if peel:
                    sp.dma_start(tabs[:], tabs_in).then_inc(tabs_landed, 16)
                    sp.dma_start(angles, angles_in).then_inc(tabs_landed, 16)
                times, rest = divmod(count - peel, SLOTS)
                phase = n.base.get("units_split", 0)
                first = at[tiles] + peel
                with n.loop(sp, times, units_split=SLOTS) as i:
                    for j in range(SLOTS):
                        load(tiles, source, i * SLOTS + (first + j), phase + j)
                for j in range(rest):
                    load(tiles, source, first + times * SLOTS + j, phase + j)
                at[tiles] += count
            if stop == 99:
                for c in range(KC):
                    sp.wait_ge(x_ready, 5 * KC + c + 1)
                    sp.dma_start(out[:, c, :], x[:, c, :]).then_inc(stored, 16)
                sp.wait_ge(stored, 16 * KC)

        @block.gpsimd
        def _(pool):
            n = Count()

            def split(tiles, j):
                slot, w = j % SLOTS, tiles * P
                pool.wait_ge(weights_landed[j % RAW], n.take(f"landed_{j % RAW}", 16))
                if n.base.get("units", 0) >= SLOTS:
                    pool.wait_ge(unit_done, n.now("units", 1 - SLOTS))
                pool.sem_inc(unit_taken, 1)
                nc.gpsimd.tensor_scalar(w_hi[:, slot, 0:w], raw[:, j % RAW, 0:w], 1.0, 1.0, ALU.mult, ALU.mult)\
                    .then_inc(high_split, 1)
                pool.wait_ge(high_split, n.take("units"))
                nc.gpsimd.tensor_tensor(w_lo[:, slot, 0:w], raw[:, j % RAW, 0:w], w_hi[:, slot, 0:w].bitcast(F32),
                                        ALU.subtract).then_inc(units_split, 1)

            def add_norm():
                for c in range(KC):
                    pool.wait_ge(post_scaled, n.take("post_scaled"))
                    nc.gpsimd.tensor_tensor(x[:, c, :], x[:, c, :], tmp[:, c % 2, :], ALU.add).then_inc(x_ready, 1)

            ends, u = [], 0
            for tiles, count in SEGMENTS:
                cuts = [at + SLOTS for at in NORMS_AT[:-1] if u < at + SLOTS <= u + count]
                for at in cuts:
                    ends.append((tiles, at, True))
                if (cuts or [None])[-1] != u + count:
                    ends.append((tiles, u + count, False))
                u += count
            for tiles, end, norm_after in ends:
                count = end - n.base.get("units", 0)
                peel = SLOTS if n.base.get("units", 0) == 0 else 0
                for j in range(peel):
                    split(tiles, j)
                times, rest = divmod(count - peel, SLOTS)
                phase = n.base.get("units", 0)
                per = {f"landed_{j}": 16 * SLOTS // RAW for j in range(RAW)}
                if times:
                    with n.loop(pool, times, units=SLOTS, **per):
                        for j in range(SLOTS):
                            split(tiles, phase + j)
                for j in range(rest):
                    split(tiles, phase + j)
                if norm_after:
                    add_norm()
            add_norm()

        @block.tensor
        def _(pe):
            n = Count()

            def three(out_ap, lhs, rhs, first, last):
                pe.matmul(out_ap, lhs[0], rhs[0], start=first, stop=False)
                pe.matmul(out_ap, lhs[0], rhs[1], start=False, stop=False)
                return pe.matmul(out_ap, lhs[1], rhs[0], start=False, stop=last)

            def next_unit():
                slot = n.base.get("units_split", 0) % SLOTS
                pe.wait_ge(units_split, n.take("units_split"))
                return [lambda t, w=w: w[:, slot, t * P:(t + 1) * P] for w in (w_hi, w_lo)]

            def next_bank():
                g = n.base.get("group", 0)
                if g >= 4:
                    pe.wait_ge(evacuated, n.now("group", -3))
                n.take("group")
                return g % 4

            def feature_unit(h, tiles=UNIT, first=True, last=True, bank=None, width=S, k_wait=None):
                w = next_unit()
                for t in range(tiles):
                    if k_wait is not None:
                        pe.wait_ge(h_low, k_wait + t + 1)
                    mm = three(psum[:, bank, 0:width], [w[0](t), w[1](t)], h(t), first and t == 0,
                               last and t == tiles - 1)
                mm.then_inc(unit_done, 1)

            def h_of(t):
                return [h_hi[:, t, :], h_lo[:, t, :]]

            def col_stat():
                pe.wait_ge(summed, n.take("summed", KC + 1))
                n.take("squared", KC)
                for b in range(NB):
                    mm = pe.matmul(psum[:, STAT_COL, b:b + 1], total[:, b * P:(b + 1) * P], ones[:, 0:1],
                                   start=True, stop=True)
                mm.then_inc(col_summed, 1)

            def add_columns(source, b_first, last):
                for b in range(NB):
                    mm = pe.matmul(psum[:, STAT_COL, b:b + 1], source[:, b * P:(b + 1) * P], ones[:, 0:1],
                                   start=b_first and b == 0, stop=last and b == NB - 1, skip_group_check=True)
                mm.then_inc(column_added, 1)

            def row_stat():
                pe.wait_ge(col_ready, n.take("col_ready"))
                for b in range(NB):
                    mm = pe.matmul(psum[:, STAT_ROW, b * P:(b + 1) * P], scale_col[:, b:b + 1].to_broadcast([P, P]),
                                   ident, start=True, stop=True)
                mm.then_inc(row_spread, 1)

            def first_unit():
                bank = next_bank()
                w = next_unit()
                for t in range(UNIT):
                    pe.wait_ge(h_low, n.take("h_low"))
                    mm = three(psum[:, bank, :], [w[0](t), w[1](t)], h_of(t), t == 0, t == UNIT - 1)
                    if t == UNIT - 1:
                        mm.then_inc(unit_done, 1)
                    pe.wait_ge(squared, n.take("squared"))
                    add_columns(squares[:, t % 2, :], t == 0, t == UNIT - 1)

            def partner(name, behind=1):
                r = n.base.get("partners", 0)
                pe.wait_ge(evacuated, n.now("group", -behind))
                if r >= 2:
                    pe.wait_ge(partner_read, r - 1)
                if partnered_chunk(name) == "rope":
                    mm = pe.matmul(psum[:, 4 + r % 2, :], rot, tmp[:, r % 2, :], start=True, stop=True)
                else:
                    for b in range(NB):
                        mm = pe.transpose(psum[:, 4 + r % 2, b * P:(b + 1) * P], tmp[:, r % 2, b * P:(b + 1) * P], ident)
                mm.then_inc(partnered, 1)
                n.take("partners")

            def project(order, other=lambda name: False, after=lambda j: None):
                for j, name in enumerate(order):
                    if j == 0:
                        first_unit()
                    elif not other(name):
                        feature_unit(h_of, bank=next_bank())
                    if j == 1:
                        row_stat()
                    if j and partnered_chunk(order[j - 1]):
                        partner(order[j - 1])
                    after(j)

            def w_out():
                start = n.base["h_low"]
                n.take("h_low", KC)
                for u in range(KC):
                    feature_unit(h_of, bank=next_bank(), k_wait=start if u == 0 else None)
                col_stat()
                row_stat()

            def swiglu():
                project("-" * 4)
                times = (2 * FC - 4) // 4
                with n.loop(pe, times, units_split=4, group=4):
                    for u in range(4):
                        feature_unit(h_of, bank=next_bank())
                pe.wait_ge(hidden_low, n.take("hidden_low", FC))
                with n.loop(pe, 2, units_split=8, group=4):
                    for c in range(4):
                        bank = next_bank()
                        for half in range(2):
                            feature_unit(lambda t: [g_hi[:, half * DOWN_UNIT + t, :], g_lo[:, half * DOWN_UNIT + t, :]],
                                         DOWN_UNIT, half == 0, half == 1, bank)
                col_stat()
                row_stat()

            def attention(rows, e, t_out):
                base = {k: n.base.get(k, 0) for k in ("scored", "rows", "combined", "turned_act", "turned_dve")}
                pe.wait_ge(evacuated, n.now("group"))
                first_score = np.cumsum([0] + [scores_of(r) for r in rows]).tolist()

                def turned_before(r, what):
                    return sum((row[3] in TURNED_BY_ACT) == (what == "act") for row in rows[:r + 1])

                def wait_turned(r):
                    act = rows[r][3] in TURNED_BY_ACT
                    pe.wait_ge(turned_act if act else turned_dve,
                               base["turned_act" if act else "turned_dve"] + turned_before(r, "act" if act else "dve"))

                for t in range(len(rows) + LAG_MIX):
                    if t < len(rows):
                        i = rows[t][3]
                        for m in range(scores_of(rows[t])):
                            s = first_score[t] + m
                            if s >= 4:
                                pe.wait_ge(exped, base["scored"] + s - 3)
                            pe.matmul(psum[:, s % 4, 0:(i + 1) * P], query(rows[t], m), keys(rows[t], m),
                                      start=True, stop=False)
                            pe.matmul(psum[:, s % 4, i * P:(i + 1) * P], ident16[:], causal16[:],
                                      start=False, stop=True).then_inc(scored, 1)
                    r = t - LAG_TURN
                    if 0 <= r < len(rows):
                        if rows[r][0] == "diff":
                            pe.wait_ge(combined, base["combined"] + r + 1)
                        else:
                            pe.wait_ge(exped, base["scored"] + first_score[r + 1])
                        if r >= 2:
                            wait_turned(r - 2)
                        for j in range(rows[r][3] + 1):
                            mm = pe.transpose(psum[:, 4 + r % 2, j * P:(j + 1) * P], e[:, 0, r % 4, j * P:(j + 1) * P],
                                              ident)
                        mm.then_inc(transposed, 1)
                    r = t - LAG_MIX
                    if 0 <= r < len(rows):
                        wait_turned(r)
                        if r >= 2:
                            pe.wait_ge(row_done, base["rows"] + r - 1)
                        width = P if rows[r][0] == "diff" else HD
                        for j in range(rows[r][3] + 1):
                            mm = pe.matmul(psum[:, 6 + r % 2, 0:width], t_out[:, r % 3, j, :], values(rows[r], j),
                                           start=j == 0, stop=j == rows[r][3])
                        mm.then_inc(mixed, 1)
                n.take("scored", first_score[-1])
                n.take("rows", len(rows))
                n.take("combined", sum(r[0] == "diff" for r in rows))
                n.take("turned_act", turned_before(len(rows), "act"))
                n.take("turned_dve", turned_before(len(rows), "dve"))

            def turn_outputs(o, chunks, done):
                for c in range(chunks):
                    if c >= 4:
                        pe.wait_ge(h_low, done + c - 3)
                    for b in range(NB):
                        mm = pe.transpose(psum[:, 4 + c % 4, b * P:(b + 1) * P], o[:, b, c * P:(c + 1) * P], ident)
                    mm.then_inc(o_turned, 1)

            def compression(name):
                if name.startswith("cmp"):
                    kind, m = divmod(int(name[3]), 2)
                    pe.wait_ge(blocks_low, kind + 1)
                    bank = next_bank()
                    for half in range(2):
                        feature_unit(lambda t: [blocks_hi[:, kind, half * UNIT + t, :], blocks_lo[:, kind, half * UNIT + t, :]],
                                     UNIT, half == 0, half == 1, bank, 2 * NCMP)
                    return True
                if name != "w2":
                    return False
                pe.wait_ge(hid_low, 1)
                bank = next_bank()
                w = next_unit()
                for m in range(2):
                    three(psum[:, bank, 0:2 * NCMP], [w[0](m), w[1](m)], [hid_hi[:, m, :], hid_lo[:, m, :]], m == 0, m == 1)
                for g in range(2):
                    part = slice(g * NCMP, (g + 1) * NCMP)
                    for m in range(2):
                        mm = three(psum[0:NCMP, bank, HD + g * HD:2 * HD + g * HD],
                                   [hid_hi[:, 2 + m, part], hid_lo[:, 2 + m, part]],
                                   [w[0](2 + m)[:, 0:HD], w[1](2 + m)[:, 0:HD]], m == 0, m == 1)
                mm.then_inc(unit_done, 1)
                return True

            def cmp_attention(j):
                if j == 0:
                    pe.wait_ge(set_up, 2)
                    pe.matmul(psum[:, 3, 0:2], ones[0:HD, :], lam[0:HD, 0:2], start=True, stop=True).then_inc(lam_summed, 1)
                if j == 2:
                    pe.wait_ge(lam_exped, 1)
                i, step = divmod(j - CMP_FROM, 3)
                if j < CMP_FROM or i >= NB:
                    return
                if step == 0:
                    if i == 0:
                        pe.wait_ge(evacuated, A_ORDER.index("w2") + 1)
                        pe.wait_ge(rope_added, A_NQ_ROPES)
                    else:
                        pe.wait_ge(cmp_done, i)
                    for head in range(8):
                        g = head // 4
                        mm = pe.matmul(psum[:, 6 + g, 32 * (head % 4):32 * (head % 4) + NCMP],
                                       nqk[HD * g:HD * g + HD, head % 4, i * P:(i + 1) * P],
                                       k_cmp[HD * g:HD * g + HD, g * NCMP:(g + 1) * NCMP], start=True, stop=True)
                    mm.then_inc(cmp_scored, 1)
                elif step == 1:
                    pe.wait_ge(cmp_weighed, i + 1)
                    for g in range(2):
                        mm = pe.transpose(psum[:, 6, g * P:(g + 1) * P], e_ring[:, 0, i, g * P:(g + 1) * P], ident)
                    mm.then_inc(cmp_transposed, 1)
                else:
                    pe.wait_ge(cmp_turned, i + 1)
                    for g in range(2):
                        mm = pe.matmul(psum[:, 7, g * 4 * HD:(g + 1) * 4 * HD], t_ring[:, 0, 2 * (i % 2) + g, :],
                                       v_cmp[:, g, :], start=True, stop=True)
                    mm.then_inc(cmp_mixed, 1)

            project(A_ORDER, compression, cmp_attention)
            partner(A_ORDER[-1], 0)
            pe.wait_ge(cmp_done, NB)
            if stop == 2:
                return

            attention(diff_rows() + nsa_rows(), e_ring, t_ring)
            pe.wait_ge(row_done, n.now("rows"))
            pe.wait_ge(diff_step, 5)
            turn_outputs(o_all, KC, n.base["h_low"])
            w_out()
            if stop == 3:
                return
            swiglu()
            if stop == 4:
                return

            project(B_ORDER)
            pe.wait_ge(decay_landed, 16 * 8)
            attention(fox_rows(), e_ring_b, t_ring_b)
            pe.wait_ge(row_done, n.now("rows"))
            turn_outputs(o_fox, 4, n.base["h_low"])
            w_out()
            if stop == 5:
                return
            swiglu()
            if stop == 6:
                return

            def conv(j):
                pe.wait_ge(glu_low, j + 1)
                for k in range(TAPS):
                    pe.wait_ge(diag_ready, 2 * (j * TAPS + k + 1))
                    three(psum[:, 4 + j, :], [diag_hi[:, k, :], diag_lo[:, k, :]],
                          [glu_hi[:, j, k:k + S], glu_lo[:, j, k:k + S]], k == 0, k == TAPS - 1)\
                        .then_inc(tap_used, 1)

            project("-" * 8)
            for j in range(2):
                for u in range(4):
                    feature_unit(h_of, bank=next_bank())
                conv(j)
            for c in range(KC):
                pe.wait_ge(conv_chunk, c + 1)
                add_columns(y_dw[:, CONV_ORDER[c], :], c == 0, c == KC - 1)
            row_stat()
            for c in range(KC):
                pe.wait_ge(squared, n.take("squared"))
                add_columns(squares[:, c % 2, :], c == 0, c == KC - 1)
            row_stat()
            w_out()
            if stop == 7:
                return
            swiglu()

        @block.scalar
        def _(act):
            n = Count()

            def copy(out_ap, in_ap, **kw):
                return nc.scalar.activation(out_ap, in_ap, ACT.Copy, **kw)

            def square(j, source, of_x):
                if j >= 2 and of_x:
                    act.wait_ge(column_added, n.base.get("column_added", 0) + j - 1)
                elif j >= 2:
                    act.wait_ge(summed, n.base.get("summed", 0) + j)
                nc.scalar.activation(squares[:, j % 2, :], source, ACT.Square).then_inc(squared, 1)

            def stat_done(of_x):
                n.take("column_added" if of_x else "summed", KC if of_x else KC + 1)

            def load_sqrt():
                nc.scalar.activation(spare[:], ones[:, 0:1], ACT.Sqrt)

            def roots():
                act.wait_ge(col_scaled, n.take("col_scaled"))
                nc.scalar.activation(root[:], variance[:], ACT.Sqrt).then_inc(rooted, 1)

            def norm(pre):
                for c in range(KC):
                    act.wait_ge(x_ready, n.take("x_ready"))
                    copy(h_hi[:, c, :], x[:, c, :], scale=col(pre, c)).then_inc(h_high, 1)
                    square(c, x[:, c, :], True)
                stat_done(True)
                roots()

            def outputs(m, loops):
                load_sqrt()
                if not loops:
                    for c in range(KC):
                        act.wait_ge(evacuated, n.take("evacuated"))
                        square(c, m[:, c, :], False)
                else:
                    start = n.base["summed"]
                    for c in range(2):
                        act.wait_ge(evacuated, n.take("evacuated"))
                        square(c, m[:, c, :], False)
                    n.base["sq"] = start
                    with n.loop(act, 3, evacuated=2, sq=2) as i:
                        for c in range(2):
                            act.wait_ge(evacuated, n.take("evacuated"))
                            act.wait_ge(summed, n.take("sq") + 1)
                            nc.scalar.activation(squares[:, c, :], m[:, i * 2 + (2 + c), :], ACT.Square).then_inc(squared, 1)
                stat_done(False)
                roots()

            def swiglu(m):
                def chunk(f):
                    act.wait_ge(evacuated, n.take("evacuated"))
                    nc.scalar.activation(squares[:, 0, :], tmp[:, 0, :], ACT.Silu).then_inc(silu_ready, 1)
                    n.take("evacuated")
                    act.wait_ge(hidden, n.take("hidden"))
                    copy(g_hi[:, f, :], squares[:, 1, :]).then_inc(hidden_high, 1)

                chunk(0)
                chunk(1)
                with n.loop(act, FC // 2 - 1, evacuated=4, hidden=2) as i:
                    chunk(i * 2 + 2)
                    chunk(i * 2 + 3)
                outputs(m, True)

            def attention(rows, e, t_out, maxima, sums, extra=lambda t: None):
                base = {k: n.base.get(k, 0) for k in ("scored", "rows")}
                first_score = np.cumsum([0] + [scores_of(r) for r in rows]).tolist()
                for t in range(len(rows) + LAG_TURN + 1):
                    if t < len(rows):
                        i = rows[t][3]
                        if t >= 4:
                            act.wait_ge(transposed, base["rows"] + t - 3)
                        for m in range(scores_of(rows[t])):
                            s = first_score[t] + m
                            act.wait_ge(maxed, base["scored"] + s + 1)
                            nc.scalar.activation(e[:, m, t % 4, 0:(i + 1) * P], psum[:, s % 4, 0:(i + 1) * P], ACT.Exp,
                                                 bias=maxima[:, s:s + 1], accum_out=sums[:, s:s + 1]).then_inc(exped, 1)
                    r = t - LAG_TURN
                    if 0 <= r < len(rows) and rows[r][3] in TURNED_BY_ACT:
                        act.wait_ge(transposed, base["rows"] + r + 1)
                        if r >= 3:
                            act.wait_ge(mixed, base["rows"] + r - 2)
                        w = (rows[r][3] + 1) * P
                        copy(t_out[:, r % 3, 0:rows[r][3] + 1, :].rearrange("p b q -> p (b q)"), psum[:, 4 + r % 2, 0:w])\
                            .then_inc(turned_act, 1)
                    extra(t)
                n.take("scored", first_score[-1])
                n.take("rows", len(rows))

            def turn_outputs(chunks, scale, first):
                for c in range(chunks):
                    act.wait_ge(o_turned, n.take("o_turned"))
                    kw = dict(scale=subln_s[:, 0:1]) if scale and c < 4 else {}
                    copy(h_hi[:, first + c, :], psum[:, 4 + c % 4, :], **kw).then_inc(h_high, 1)

            for j in range(4):
                act.dma_start(x[:, 2 * j:2 * j + 2, :], xt[:, 2 * j:2 * j + 2, :]).then_inc(x_landed[j], 16)
            act.wait_ge(set_up, 1)
            load_sqrt()
            act.wait_ge(cols_landed, 16)
            for c in range(KC):
                act.wait_ge(x_landed[c // 2], 16)
                copy(h_hi[:, c, :], x[:, c, :], scale=col("attn_pre", c)).then_inc(h_high, 1)
                square(c, x[:, c, :], True)
            stat_done(True)
            roots()
            act.wait_ge(lam_summed, 1)
            nc.scalar.activation(lam[:, 2:4], psum[:, 3, 0:2], ACT.Exp).then_inc(lam_exped, 1)

            for kind in range(2):
                act.wait_ge(blocks_added, 8 * (kind + 1))
                copy(blocks_hi[:, kind, :, :], blocks[:, kind, :, :]).then_inc(blocks_high, 1)
            act.wait_ge(partner_read, 7)
            nc.scalar.activation(gates[:], gates[:], ACT.Sigmoid).then_inc(gates_ready, 1)
            act.wait_ge(evacuated, A_ORDER.index("cmp3") + 1)
            nc.scalar.activation(hid_s[:], hid[:], ACT.Silu).then_inc(hid_silu, 1)
            act.wait_ge(hid_silu, 1)
            copy(hid_hi[:], hid_s[:]).then_inc(hid_high, 1)
            for i in range(NB):
                act.wait_ge(cmp_step, 7 * i + (i > 0) + 5)
                nc.scalar.activation(e_ring[:, 0, i, 0:256], e_ring[:, 0, i, 0:256], ACT.Exp).then_inc(cmp_exped, 1)
                act.wait_ge(cmp_transposed, i + 1)
                copy(t_ring[:, 0, 2 * (i % 2):2 * (i % 2) + 2, :].rearrange("p b q -> p (b q)"), psum[:, 6, 0:256])\
                    .then_inc(cmp_turned, 1)
            n.take("evacuated", len(A_ORDER))
            if stop == 2:
                return

            def diff_norm(t):
                if t == 24:
                    act.wait_ge(row_done, 16)
                    nc.scalar.activation(m_ffn[:, 0:4, :], o_all[:, :, 0:4 * P], ACT.Square).then_inc(diff_squared, 1)
                if t == 30:
                    act.wait_ge(diff_step, 3)
                    nc.scalar.activation(diff_ms[:, 2, :], diff_ms[:, 1, :], ACT.Sqrt).then_inc(diff_rooted, 1)

            attention(diff_rows() + nsa_rows(), e_ring, t_ring, neg_max, row_sum, diff_norm)
            turn_outputs(KC, True, 0)
            outputs(m_mix, False)
            if stop == 3:
                return
            norm("ffn_pre")
            swiglu(m_ffn)
            if stop == 4:
                return

            norm("mix_pre_0")
            act.wait_ge(forget_step, 4)
            nc.scalar.activation(forget[:, 3, :], forget[:, 2, :], ACT.Exp, scale=-1.0).then_inc(forget_act, 1)
            act.wait_ge(forget_act, 1)
            nc.scalar.activation(forget[:, 4, :], forget[:, 3, :], ACT.Ln, bias=1.0).then_inc(forget_act, 1)
            act.wait_ge(forget_step, 6)
            for head in range(8):
                act.dma_start(k_fox[HD:HD + 1, head, :], forget[head:head + 1, 3, :]).then_inc(decay_landed, 16)
            n.take("evacuated", len(B_ORDER))
            for c in range(4):
                act.wait_ge(mix_step, 5 * (c + 1))
                if c == 0:
                    act.wait_ge(unit_done, NORMS_AT[1] + len(B_ORDER))
                copy(h_hi[:, c, :], y_conv[:, c, :]).then_inc(h_high, 1)
            attention(fox_rows(), e_ring_b, t_ring_b, neg_max_b, row_sum_b)
            turn_outputs(4, False, 4)
            outputs(m_mix, False)
            if stop == 5:
                return
            norm("ffn_pre_0")
            swiglu(m_ffn)
            if stop == 6:
                return

            norm("mix_pre_1")

            def gate(c):
                act.wait_ge(evacuated, n.take("evacuated"))
                nc.scalar.activation(squares[:, 0, :], tmp[:, 0, :], ACT.Sigmoid, bias=col("b_pw1", c + KC)).then_inc(sigmoid_ready, 1)
                n.take("evacuated")

            def diagonals(j, first, last):
                for k in range(first, last):
                    if j:
                        act.wait_ge(tap_used, k + 1)
                    copy(diag_hi[:, k, :], ident, scale=col("w_dw", CONV_PE[j] * TAPS + k)).then_inc(diag_ready, 1)
                    copy(diag_lo[:, k, :], ident, scale=taps_lo[:, j * TAPS + k:j * TAPS + k + 1]).then_inc(diag_ready, 1)

            act.wait_ge(taps_split, 2)
            for c, share in enumerate((10, 20, 26, TAPS)):
                gate(c)
                if c in CONV_PE:
                    act.wait_ge(conv_step, 1 + 2 * TAPS + c - 1)
                    copy(glu_hi[:, c - 2, :], glu[:, c, :]).then_inc(glu_high, 1)
                diagonals(0, (0, 10, 20, 26)[c], share)
            gate(4)
            gate(5)
            diagonals(1, 0, TAPS)
            gate(6)
            gate(7)
            load_sqrt()
            for c in range(KC):
                act.wait_ge(centred, c + 1)
                if c >= 2:
                    act.wait_ge(column_added, n.base["column_added"] + KC + c - 1)
                nc.scalar.activation(squares[:, c % 2, :], y_dw[:, c, :], ACT.Square).then_inc(squared, 1)
            n.take("column_added", 2 * KC)
            roots()
            for c in range(KC):
                act.wait_ge(normed, c + 1)
                if c >= 2:
                    act.wait_ge(h_low, 6 * KC + c - 1)
                nc.scalar.activation(squares[:, c % 2, :], tmp[:, c % 2, :], ACT.Silu, scale=col("ln_g", c),
                                     bias=col("ln_b", c)).then_inc(ln_silu, 1)
                act.wait_ge(ln_silu, c + 1)
                copy(h_hi[:, c, :], squares[:, c % 2, :]).then_inc(h_high, 1)
            act.wait_ge(h_low, 7 * KC)
            outputs(m_mix, False)
            if stop == 7:
                return
            norm("ffn_pre_1")
            swiglu(m_ffn)
            act.wait_ge(x_ready, 1)

        @block.vector
        def _(dve):
            n = Count()
            v = nc.vector

            def clear_total():
                v.memset(total[:], 0.0).then_inc(summed, 1)
                n.take("summed")

            def add_square(c):
                dve.wait_ge(squared, n.take("squared"))
                dve.wait_ge(summed, n.now("summed"))
                v.tensor_tensor(total[:], total[:], squares[:, c, :], ALU.add).then_inc(summed, 1)
                n.take("summed")

            def stat(eps, of_x=False):
                if of_x:
                    n.take("squared", KC)
                    dve.wait_ge(column_added, n.take("column_added", KC))
                else:
                    dve.wait_ge(col_summed, n.take("col_summed"))
                v.tensor_scalar(variance[:], psum[:, STAT_COL, 0:NB], 1.0 / D, eps, ALU.mult, ALU.add).then_inc(col_scaled, 1)
                dve.wait_ge(rooted, n.take("rooted"))
                v.reciprocal(scale_col[:], root[:]).then_inc(col_ready, 1)
                row()

            def row():
                dve.wait_ge(row_spread, n.take("row_spread"))
                v.tensor_copy(scale_row[:], psum[:, STAT_ROW, :]).then_inc(row_ready, 1)
                dve.wait_ge(row_ready, n.take("row_ready"))

            def low_part(c, pre):
                dve.wait_ge(h_high, n.take("h_high"))
                v.scalar_tensor_tensor(h_lo[:, c, :], x[:, c, :], col(pre, c), h_hi[:, c, :].bitcast(F32),
                                       ALU.mult, ALU.subtract).then_inc(h_low, 1)
                n.take("h_low")

            def norm(m, post, pre):
                for c in range(KC + 1):
                    if c < KC:
                        if c >= 2:
                            dve.wait_ge(x_ready, n.base.get("x_ready", 0) + c - 1)
                        v.scalar_tensor_tensor(tmp[:, c % 2, :], m[:, c, :], col(post, c), scale_row[:], ALU.mult, ALU.mult)\
                            .then_inc(post_scaled, 1)
                    if c and pre:
                        low_part(c - 1, pre)
                n.take("x_ready", KC)
                if pre:
                    stat(EPS_RMS, True)

            def group(u=1):
                bank = n.base.get("evacuated", 0) % 4
                dve.wait_ge(unit_done, n.take("unit_done", u))
                n.take("evacuated")
                return psum[:, bank, :]

            def outputs(m, times, units, bias=None):
                clear_total()

                def one(c, place):
                    source = group(units)
                    if bias:
                        v.tensor_scalar(m[:, c, :], source, col(bias, c), None, ALU.add).then_inc(evacuated, 1)
                    else:
                        v.tensor_copy(m[:, c, :], source).then_inc(evacuated, 1)
                    add_square(place)

                if times == 1:
                    for c in range(KC):
                        one(c, c % 2)
                else:
                    with n.loop(dve, times, unit_done=4 * units, evacuated=4, squared=4, summed=4) as i:
                        for c in range(4):
                            one(i * 4 + c, c % 2)
                stat(EPS_RMS)

            def swiglu(m):
                def chunk(f):
                    v.tensor_tensor(tmp[:, 0, :], group(), scale_row[:], ALU.mult).then_inc(evacuated, 1)
                    v.tensor_tensor(tmp[:, 1, :], group(), scale_row[:], ALU.mult).then_inc(evacuated, 1)
                    dve.wait_ge(silu_ready, n.take("silu_ready"))
                    dve.wait_ge(evacuated, n.now("evacuated"))
                    v.tensor_tensor(squares[:, 1, :], squares[:, 0, :], tmp[:, 1, :], ALU.mult).then_inc(hidden, 1)
                    dve.wait_ge(hidden_high, n.take("hidden_high"))
                    v.tensor_tensor(g_lo[:, f, :], squares[:, 1, :], g_hi[:, f, :].bitcast(F32), ALU.subtract)\
                        .then_inc(hidden_low, 1)

                chunk(0)
                chunk(1)
                with n.loop(dve, FC // 2 - 1, unit_done=4, evacuated=4, silu_ready=2, hidden_high=2) as i:
                    chunk(i * 2 + 2)
                    chunk(i * 2 + 3)
                outputs(m, 2, 2)

            def attention(rows, e, t_out, maxima, sums, inverse, extra=lambda t: None):
                base = {k: n.base.get(k, 0) for k in ("scored", "rows")}
                first_score = np.cumsum([0] + [scores_of(r) for r in rows]).tolist()
                for t in range(len(rows) + LAG_MIX + 1):
                    if t < len(rows):
                        for m in range(scores_of(rows[t])):
                            s = first_score[t] + m
                            dve.wait_ge(scored, base["scored"] + s + 1)
                            v.tensor_reduce(maxima[:, s:s + 1], psum[:, s % 4, 0:(rows[t][3] + 1) * P], AX, ALU.max, negate=True)\
                                .then_inc(maxed, 1)
                    r = t - 2
                    if 0 <= r < len(rows) and rows[r][0] == "diff":
                        s = first_score[r]
                        w = (rows[r][3] + 1) * P
                        dve.wait_ge(exped, base["scored"] + s + 2)
                        v.reciprocal(inverse[:, s + 1:s + 2], sums[:, s + 1:s + 2]).then_inc(coef_step, 1)
                        dve.wait_ge(coef_step, n.take("coef_step"))
                        v.scalar_tensor_tensor(coef[:, s:s + 1], sums[:, s:s + 1], inverse[:, s + 1:s + 2], lam[:, 5:6],
                                               ALU.mult, ALU.mult).then_inc(coef_step, 1)
                        dve.wait_ge(coef_step, n.take("coef_step"))
                        v.scalar_tensor_tensor(e[:, 0, r % 4, 0:w], e[:, 1, r % 4, 0:w], coef[:, s:s + 1], e[:, 0, r % 4, 0:w],
                                               ALU.mult, ALU.add).then_inc(combined, 1)
                    r = t - LAG_TURN
                    if 0 <= r < len(rows) and rows[r][3] not in TURNED_BY_ACT:
                        dve.wait_ge(transposed, base["rows"] + r + 1)
                        if r >= 3:
                            dve.wait_ge(mixed, base["rows"] + r - 2)
                        w = (rows[r][3] + 1) * P
                        v.tensor_copy(t_out[:, r % 3, 0:rows[r][3] + 1, :].rearrange("p b q -> p (b q)"), psum[:, 4 + r % 2, 0:w])\
                            .then_inc(turned_dve, 1)
                    r = t - LAG_MIX
                    if 0 <= r < len(rows):
                        kind, head, b, i = rows[r]
                        s = first_score[r]
                        v.reciprocal(inverse[:, s:s + 1], sums[:, s:s + 1]).then_inc(coef_step, 1)
                        dve.wait_ge(coef_step, n.take("coef_step"))
                        dve.wait_ge(mixed, base["rows"] + r + 1)
                        place = mixed_place(rows[r])
                        if kind == "nsa":
                            v.tensor_scalar(coef[:, s:s + 1], inverse[:, s:s + 1], gates[:, i, 3 * head + b:3 * head + b + 1],
                                            None, ALU.mult).then_inc(coef_step, 1)
                            dve.wait_ge(coef_step, n.take("coef_step"))
                            if b == 2:
                                dve.wait_ge(row_done, base["rows"] + r - NB + 1)
                            v.scalar_tensor_tensor(place, psum[:, 6 + r % 2, 0:HD], coef[:, s:s + 1], place,
                                                   ALU.mult, ALU.add).then_inc(row_done, 1)
                        else:
                            width = P if kind == "diff" else HD
                            v.tensor_scalar(place, psum[:, 6 + r % 2, 0:width], inverse[:, s:s + 1], None, ALU.mult)\
                                .then_inc(row_done, 1)
                    extra(t)
                n.take("scored", first_score[-1])
                n.take("rows", len(rows))

            def turn_outputs(chunks, scale, first):
                for c in range(chunks):
                    dve.wait_ge(h_high, n.take("h_high"))
                    hi = h_hi[:, first + c, :].bitcast(F32)
                    if scale and c < 4:
                        ins = v.scalar_tensor_tensor(h_lo[:, first + c, :], psum[:, 4 + c % 4, :], subln_s[:, 0:1], hi,
                                                     ALU.mult, ALU.subtract)
                    else:
                        ins = v.tensor_tensor(h_lo[:, first + c, :], psum[:, 4 + c % 4, :], hi, ALU.subtract)
                    ins.then_inc(h_low, 1)
                    n.take("h_low")

            v.memset(ones[:], 1.0).then_inc(set_up, 1)
            v.memset(v_cmp[:], 0.0)
            dve.wait_ge(cols_landed, 16)
            c0 = COL["lam"]
            v.tensor_tensor(lam[0:HD, 0:2], cols[0:HD, c0:c0 + 4:2], cols[0:HD, c0 + 1:c0 + 4:2], ALU.mult).then_inc(set_up, 1)
            v.tensor_scalar(subln_s[:], col("subln"), 1.0 - LAM_INIT, None, ALU.mult).then_inc(set_up, 1)
            for c in range(KC):
                low_part(c, "attn_pre")
            dve.wait_ge(tabs_landed, 32)
            v.tensor_copy(ident16[:], ident).then_inc(set_up, 1)
            v.tensor_copy(causal16[:], tabs[:, TAB["causal"]:TAB["causal"] + P]).then_inc(set_up, 1)
            stat(EPS_RMS, True)
            dve.wait_ge(lam_exped, 1)
            v.tensor_tensor(lam[:, 4:5], lam[:, 3:4], lam[:, 2:3], ALU.subtract).then_inc(set_up, 1)
            dve.wait_ge(set_up, 6)
            v.tensor_scalar(lam[:, 5:6], lam[:, 4:5], -LAM_INIT, None, ALU.add).then_inc(set_up, 1)
            for j in range(2):
                v.tensor_tensor(angles[:, j, :], angles[:, j, :], scale_row[:], ALU.mult).then_inc(angles_scaled, 1)

            def partner(name, at):
                r = n.base.get("partners", 0)
                ropes = n.base.get("ropes", 0)
                if partnered_chunk(name) == "rope":
                    scale = HD ** -0.5 if name[1] == "q" else 1.0
                    if ropes == 0:
                        dve.wait_ge(angles_scaled, 2)
                    else:
                        dve.wait_ge(rope_added, ropes)
                    dve.wait_ge(evacuated, at + 1)
                    v.scalar_tensor_tensor(squares[:, 0, :], tmp[:, r % 2, :], scale, angles[:, 0, :], ALU.mult, ALU.mult)\
                        .then_inc(rope_cos, 1)
                    dve.wait_ge(partnered, r + 1)
                    v.scalar_tensor_tensor(squares[:, 1, :], psum[:, 4 + r % 2, :], scale, angles[:, 1, :], ALU.mult, ALU.mult)\
                        .then_inc(partner_read, 1)
                    dve.wait_ge(rope_cos, ropes + 1)
                    dve.wait_ge(partner_read, r + 1)
                    v.tensor_tensor(rope_place(name), squares[:, 0, :], squares[:, 1, :], ALU.add).then_inc(rope_added, 1)
                    n.take("ropes")
                else:
                    dve.wait_ge(partnered, r + 1)
                    c = int(name[-1]) if name[-1].isdigit() else 0
                    place = {"dv": v_diff[:, :, c * P:(c + 1) * P], "vs": v_nsa[:, 0, :, :], "vw": v_nsa[:, 1, :, :],
                             "ga": gates[:]}.get(name[:2], v_fox[:, :, c * P:(c + 1) * P])
                    source = psum[:, 4 + r % 2, :].rearrange("p (b f) -> p b f", b=NB)
                    v.tensor_copy(place, source[:, :, 0:24] if name == "gates" else source).then_inc(partner_read, 1)
                n.take("partners")

            def split_blocks(kind):
                if kind == 0:
                    dve.wait_ge(rope_added, 1)
                dve.wait_ge(evacuated, 2)
                for g in range(2):
                    half = slice(g * HD, (g + 1) * HD)
                    tokens = nqk[half, 4 + kind, :].rearrange("p (n s) -> p n s", s=CMP_STRIDE)
                    for parity in range(2):
                        for a in range(2):
                            place = blocks[parity * HD:(parity + 1) * HD, kind, 8 * a:8 * a + 8, g * NCMP:(g + 1) * NCMP]
                            p0 = COL["k_pos" if kind == 0 else "v_pos"] + 16 * a + parity
                            pos = cols[half, p0:p0 + 15:2].unsqueeze(1).to_broadcast([HD, NCMP, 8])
                            v.tensor_tensor(place.rearrange("p b n -> p n b"), tokens[:, a:a + NCMP, parity:CMP_STRIDE:2], pos,
                                            ALU.add).then_inc(blocks_added, 1)
                dve.wait_ge(blocks_added, 8 * (kind + 1))
                dve.wait_ge(blocks_high, kind + 1)
                v.tensor_tensor(blocks_lo[:, kind, :, :], blocks[:, kind, :, :], blocks_hi[:, kind, :, :].bitcast(F32), ALU.subtract)\
                    .then_inc(blocks_low, 1)

            def cmp_softmax(i):
                e = e_ring[:, 0, i, 0:256].rearrange("p (h n) -> p h n", h=8)
                mask = tabs[:, TAB["cmp_mask"] + 32 * i:TAB["cmp_mask"] + 32 * i + NCMP].unsqueeze(1).to_broadcast([P, 4, NCMP])
                step = 7 * i + (i > 0)
                if i == 0:
                    v.memset(e_ring[:, 0, :, 0:256], NEG).then_inc(cmp_step, 1)
                    dve.wait_ge(gates_ready, 1)
                step += 1
                dve.wait_ge(cmp_step, 1)
                dve.wait_ge(cmp_scored, i + 1)
                for g in range(2):
                    v.tensor_tensor(e[:, 4 * g:4 * g + 4, 0:NCMP],
                                    psum[:, 6 + g, 0:P].rearrange("p (h n) -> p h n", h=4)[:, :, 0:NCMP], mask, ALU.add)\
                        .then_inc(cmp_step, 1)
                dve.wait_ge(cmp_step, step + 2)
                v.tensor_reduce(cmp_small[:, 0, i, :], e, AX, ALU.max).then_inc(cmp_step, 1)
                dve.wait_ge(cmp_step, step + 3)
                v.tensor_tensor(e, e, cmp_small[:, 0, i, :].unsqueeze(2).to_broadcast([P, 8, 32]), ALU.subtract).then_inc(cmp_step, 1)
                dve.wait_ge(cmp_exped, i + 1)
                v.tensor_reduce(cmp_small[:, 1, i, :], e, AX, ALU.add).then_inc(cmp_step, 1)
                dve.wait_ge(cmp_step, step + 5)
                v.reciprocal(cmp_small[:, 2, i, :], cmp_small[:, 1, i, :]).then_inc(cmp_step, 1)
                dve.wait_ge(cmp_step, step + 6)
                v.tensor_tensor(cmp_small[:, 3, i, :], cmp_small[:, 2, i, :], gates[:, i, 0:24:3], ALU.mult).then_inc(cmp_step, 1)
                step += 7
                if i == 0:
                    keep = tabs[:, TAB["cmp_keep"]:TAB["cmp_keep"] + 32].unsqueeze(1).to_broadcast([P, 8, 32])
                    v.tensor_tensor(e, e, keep, ALU.mult).then_inc(cmp_step, 1)
                    step += 1
                dve.wait_ge(cmp_step, step)
                v.tensor_tensor(e, e, cmp_small[:, 3, i, :].unsqueeze(2).to_broadcast([P, 8, 32]), ALU.mult).then_inc(cmp_weighed, 1)

            for j, name in enumerate(A_ORDER):
                bank = group(2 if name.startswith("cmp") else 1)
                if partnered_chunk(name) == "rope":
                    v.tensor_copy(tmp[:, n.now("raws") % 2, :], bank).then_inc(evacuated, 1)
                    n.take("raws")
                elif partnered_chunk(name) == "turn":
                    v.tensor_tensor(tmp[:, n.now("raws") % 2, :], bank, scale_row[:], ALU.mult).then_inc(evacuated, 1)
                    n.take("raws")
                elif name == "vc":
                    v.tensor_tensor(nqk[:, 5, :], bank, scale_row[:], ALU.mult).then_inc(evacuated, 1)
                elif name.startswith("cmp"):
                    v.tensor_copy(hid[:, int(name[3]), :], bank[:, 0:2 * NCMP]).then_inc(evacuated, 1)
                else:
                    v.tensor_copy(k_cmp[:], bank[:, 0:2 * NCMP])
                    for g in range(2):
                        for c in range(4):
                            ins = v.tensor_copy(v_cmp[32 * c:32 * c + NCMP, g, c * HD:(c + 1) * HD],
                                                bank[0:NCMP, HD + g * HD:2 * HD + g * HD])
                    ins.then_inc(evacuated, 1)
                if j and partnered_chunk(A_ORDER[j - 1]):
                    partner(A_ORDER[j - 1], j - 1)
                if name in ("vc", "nq0"):
                    split_blocks(int(name == "nq0"))
                if name == "cmp3":
                    dve.wait_ge(hid_high, 1)
                    v.tensor_tensor(hid_lo[:], hid_s[:], hid_hi[:].bitcast(F32), ALU.subtract).then_inc(hid_low, 1)
                i, step = divmod(j - CMP_FROM, 3)
                if j >= CMP_FROM and i < NB and step == 0:
                    cmp_softmax(i)
                if j >= CMP_FROM and i < NB and step == 2:
                    dve.wait_ge(cmp_mixed, i + 1)
                    v.tensor_copy(o_all[:, i, 4 * P:D], psum[:, 7, :]).then_inc(cmp_done, 1)
            partner(A_ORDER[-1], len(A_ORDER) - 1)
            dve.wait_ge(cmp_done, NB)
            if stop == 2:
                return

            def diff_norm(t):
                o = o_all[:, :, 0:4 * P].rearrange("p b (h e) -> p b h e", h=4)
                sixteen = [diff_ms[:, j, :].rearrange("p (b h) -> p b h", b=NB) for j in range(4)]
                if t == 26:
                    dve.wait_ge(diff_squared, 1)
                    v.tensor_reduce(diff_ms[:, 0, :], m_ffn[:, 0:4, :].rearrange("p b (h e) -> p (b h) e", h=4), AX, ALU.add)\
                        .then_inc(diff_step, 1)
                if t == 27:
                    dve.wait_ge(diff_step, 1)
                    v.tensor_scalar(diff_ms[:, 3, :], diff_ms[:, 0, :], 1.0 / P, EPS_RMS, ALU.mult, ALU.add).then_inc(diff_step, 1)
                    dve.wait_ge(diff_step, 2)
                    v.tensor_copy(diff_ms[:, 1, :], diff_ms[:, 3, :]).then_inc(diff_step, 1)
                if t == 31:
                    dve.wait_ge(diff_rooted, 1)
                    v.reciprocal(diff_ms[:, 3, :], diff_ms[:, 2, :]).then_inc(diff_step, 1)
                    dve.wait_ge(diff_step, 4)
                    dve.wait_ge(row_done, 16)
                    for b in range(NB):
                        part = o_all[:, b, 0:4 * P].rearrange("p (h e) -> p h e", h=4)
                        ins = v.tensor_tensor(part, part, diff_ms[:, 3, 4 * b:4 * b + 4].unsqueeze(2).to_broadcast([P, 4, P]), ALU.mult)
                    ins.then_inc(diff_step, 1)

            attention(diff_rows() + nsa_rows(), e_ring, t_ring, neg_max, row_sum, inv_sum, diff_norm)
            turn_outputs(KC, True, 0)
            outputs(m_mix, 1, 1)
            norm(m_mix, "attn_post", "ffn_pre")
            if stop == 3:
                return
            swiglu(m_ffn)
            norm(m_ffn, "ffn_post", "mix_pre_0")
            if stop == 4:
                return

            for j, name in enumerate(B_ORDER):
                which, c = name.rstrip("0123"), int(name[-1]) if name != "f" else 0
                bank = group()
                if which == "f":
                    v.tensor_tensor(forget[:, 0, :], bank[0:8, :], scale_row[0:8, :], ALU.mult).then_inc(evacuated, 1)
                    dve.wait_ge(evacuated, n.now("evacuated"))
                    v.tensor_scalar(forget[:, 1, :], forget[:, 0, :], cols[0:8, COL["b_forget"]:COL["b_forget"] + 1], None, ALU.add)\
                        .then_inc(forget_step, 1)
                    dve.wait_ge(forget_step, 1)
                    v.tensor_scalar(forget[:, 0, :], forget[:, 1, :], 0.0, None, ALU.min).then_inc(forget_step, 1)
                    v.memset(forget[:, 3, :], 1.0).then_inc(forget_step, 1)
                    v.scalar_tensor_tensor(forget[:, 2, :], forget[:, 1, :], -1.0, forget[:, 1, :], ALU.mult, ALU.max)\
                        .then_inc(forget_step, 1)
                    dve.wait_ge(forget_act, 2)
                    v.tensor_tensor(forget[:, 1, :], forget[:, 4, :], forget[:, 0, :], ALU.subtract).then_inc(forget_step, 1)
                    dve.wait_ge(forget_step, 5)
                    v.tensor_tensor_scan(forget[:, 3, :], ones[0:8, 0:1].to_broadcast([8, S]), forget[:, 1, :], 0.0,
                                         ALU.mult, ALU.add).then_inc(forget_step, 1)
                    v.memset(padded[:, 0:2], 0.0)
                    n.take("set")
                elif which == "v":
                    dve.wait_ge(mix_step, n.now("mix_step"))
                    v.tensor_tensor(tmp[:, n.now("raws") % 2, :], bank, scale_row[:], ALU.mult).then_inc(evacuated, 1)
                    n.take("raws")
                elif which in ("gc", "xa"):
                    if c:
                        dve.wait_ge(mix_step, n.now("mix_step"))
                    v.tensor_tensor(tmp[:, int(which == "xa"), :], bank, scale_row[:], ALU.mult).then_inc(evacuated, 1)
                elif which == "gb":
                    dve.wait_ge(evacuated, n.now("evacuated", -1))
                    v.tensor_tensor(padded[:, 2:S + 2], tmp[:, 0, :], tmp[:, 1, :], ALU.mult).then_inc(mix_step, 1)
                    dve.wait_ge(mix_step, n.take("mix_step"))
                    v.tensor_tensor(tmp[:, 0, :], bank, scale_row[:], ALU.mult).then_inc(evacuated, 1)
                    w = [col("w_short", 3 * c + k) for k in range(3)]
                    v.tensor_scalar(squares[:, 0, :], padded[:, 0:S], w[0], None, ALU.mult).then_inc(mix_step, 1)
                    dve.wait_ge(mix_step, n.take("mix_step"))
                    v.scalar_tensor_tensor(squares[:, 1, :], padded[:, 1:S + 1], w[1], squares[:, 0, :], ALU.mult, ALU.add)\
                        .then_inc(mix_step, 1)
                    dve.wait_ge(mix_step, n.take("mix_step"))
                    v.scalar_tensor_tensor(squares[:, 0, :], padded[:, 2:S + 2], w[2], squares[:, 1, :], ALU.mult, ALU.add)\
                        .then_inc(mix_step, 1)
                    dve.wait_ge(mix_step, n.take("mix_step"))
                    dve.wait_ge(evacuated, n.now("evacuated"))
                    v.tensor_tensor(y_conv[:, c, :], squares[:, 0, :], tmp[:, 0, :], ALU.mult).then_inc(mix_step, 1)
                    n.take("mix_step")
                elif which in ("q", "k"):
                    if (which, c) == ("q", 0):
                        dve.wait_ge(decay_landed, 16 * 8)
                        v.memset(q_fox[HD:HD + 1, :, :], 1.0)
                    place = q_fox if which == "q" else k_fox
                    scale = HD ** -0.5 if which == "q" else 1.0
                    for half in range(2):
                        part = slice(half * HD, (half + 1) * HD)
                        ins = v.scalar_tensor_tensor(place[0:HD, 2 * c + half, :], bank[part, :], scale, scale_row[part, :],
                                                     ALU.mult, ALU.mult)
                    ins.then_inc(evacuated, 1)
                if j and partnered_chunk(B_ORDER[j - 1]):
                    partner(B_ORDER[j - 1], j - 1)
            for c in range(4):
                dve.wait_ge(h_high, n.take("h_high"))
                v.tensor_tensor(h_lo[:, c, :], y_conv[:, c, :], h_hi[:, c, :].bitcast(F32), ALU.subtract).then_inc(h_low, 1)
                n.take("h_low")
            attention(fox_rows(), e_ring_b, t_ring_b, neg_max_b, row_sum_b, inv_sum_b)
            turn_outputs(4, False, 4)
            outputs(m_mix, 1, 1)
            norm(m_mix, "mix_post_0", "ffn_pre_0")
            if stop == 5:
                return
            swiglu(m_ffn)
            norm(m_ffn, "ffn_post_0", "mix_pre_1")
            if stop == 6:
                return

            v.memset(glu[:, :, 0:TAPS - 1], 0.0).then_inc(conv_step, 1)
            n.take("conv_step")
            first = COL["w_dw"] + CONV_PE[0] * TAPS
            v.tensor_copy(taps_hi[:], cols[:, first:first + 2 * TAPS]).then_inc(taps_split, 1)
            dve.wait_ge(taps_split, 1)
            v.tensor_tensor(taps_lo[:], cols[:, first:first + 2 * TAPS], taps_hi[:].bitcast(F32), ALU.subtract).then_inc(taps_split, 1)

            def conformer_chunk(c, on_pe=False):
                v.tensor_tensor(tmp[:, 0, :], group(), scale_row[:], ALU.mult).then_inc(evacuated, 1)
                v.tensor_tensor(tmp[:, 1, :], group(), scale_row[:], ALU.mult).then_inc(evacuated, 1)
                dve.wait_ge(sigmoid_ready, n.take("sigmoid_ready"))
                dve.wait_ge(evacuated, n.now("evacuated"))
                v.scalar_tensor_tensor(glu[:, c, TAPS - 1:TAPS - 1 + S], tmp[:, 1, :], col("b_pw1", c), squares[:, 0, :], ALU.add, ALU.mult)\
                    .then_inc(conv_step, 1)
                dve.wait_ge(conv_step, n.take("conv_step"))
                if on_pe:
                    dve.wait_ge(glu_high, c - 1)
                    v.tensor_tensor(glu_lo[:, c - 2, :], glu[:, c, :], glu_hi[:, c - 2, :].bitcast(F32), ALU.subtract).then_inc(glu_low, 1)
                    return
                v.tensor_scalar(y_dw[:, c, :], glu[:, c, 0:S], col("w_dw", c * TAPS), col("b_dw", c), ALU.mult, ALU.add)\
                    .then_inc(conv_step, 1)
                for k in range(1, TAPS):
                    dve.wait_ge(conv_step, n.take("conv_step"))
                    v.scalar_tensor_tensor(y_dw[:, c, :], glu[:, c, k:k + S], col("w_dw", c * TAPS + k), y_dw[:, c, :],
                                           ALU.mult, ALU.add).then_inc(conv_chunk if k == TAPS - 1 else conv_step, 1)

            conformer_chunk(0)
            conformer_chunk(1)
            for c in CONV_PE:
                conformer_chunk(c, True)
            with n.loop(dve, 2, unit_done=4, evacuated=4, sigmoid_ready=2, conv_step=2 * TAPS) as i:
                conformer_chunk(i * 2 + 4)
                conformer_chunk(i * 2 + 5)
            for j, c in enumerate(CONV_PE):
                dve.wait_ge(tap_used, (j + 1) * TAPS)
                v.tensor_scalar(y_dw[:, c, :], psum[:, 4 + j, :], col("b_dw", c), None, ALU.add).then_inc(conv_chunk, 1)
            dve.wait_ge(column_added, n.take("column_added", KC))
            v.tensor_scalar(scale_col[:], psum[:, STAT_COL, 0:NB], 1.0 / D, None, ALU.mult).then_inc(col_ready, 1)
            row()
            dve.wait_ge(conv_chunk, KC)
            for c in range(KC):
                v.tensor_tensor(y_dw[:, c, :], y_dw[:, c, :], scale_row[:], ALU.subtract).then_inc(centred, 1)
            stat(EPS_LN, True)
            for c in range(KC + 1):
                if c < KC:
                    if c >= 2:
                        dve.wait_ge(ln_silu, c - 1)
                    v.tensor_tensor(tmp[:, c % 2, :], y_dw[:, c, :], scale_row[:], ALU.mult).then_inc(normed, 1)
                if c:
                    dve.wait_ge(h_high, n.take("h_high"))
                    v.tensor_tensor(h_lo[:, c - 1, :], squares[:, (c - 1) % 2, :], h_hi[:, c - 1, :].bitcast(F32), ALU.subtract)\
                        .then_inc(h_low, 1)
                    n.take("h_low")
            outputs(m_mix, 1, 1, "b_pw2")
            norm(m_mix, "mix_post_1", "ffn_pre_1")
            if stop == 7:
                return
            swiglu(m_ffn)
            norm(m_ffn, "ffn_post_1", None)


def shape_tables():
    inv = (1.0 / (np.float32(10000.0) ** (np.arange(0, HD, 2, dtype=np.float32) / np.float32(HD)))).astype(np.float32)
    angle = np.arange(S, dtype=np.float32)[:, None] * inv[None, :]
    which = np.arange(P) % 32
    angles = np.stack([np.cos(angle).T[which], np.sin(angle).T[which]], axis=1).astype(np.float32)
    t = np.zeros((P, NTAB), np.float32)
    out = np.arange(P)
    lower = out % HD < 32
    t[np.where(lower, out + 32, out - 32), TAB["rot"] + out] = np.where(lower, -1.0, 1.0)
    t[:, TAB["ident"]:TAB["ident"] + P] = np.eye(P)
    t[:, TAB["causal"]:TAB["causal"] + P] = np.where(np.arange(P)[None, :] <= np.arange(P)[:, None], 0.0, NEG)
    token = np.arange(S).reshape(NB, P).T
    end = np.arange(32) * CMP_STRIDE + CMP_LEN - 1
    seen = (end[None, None, :] <= token[:, :, None]) & (np.arange(32) < NCMP)
    t[:, TAB["cmp_mask"]:TAB["cmp_mask"] + NB * 32] = np.where(seen, 0.0, NEG).reshape(P, NB * 32)
    t[:, TAB["cmp_keep"]:TAB["cmp_keep"] + 32] = seen[:, 0, :]
    return angles, t


def tiles_of(w, rows, cols):
    return w.reshape(-1, P, w.shape[1])[rows, :, cols * P:(cols + 1) * P].transpose(1, 0, 2)


def pad_columns(w, n):
    out = np.zeros((w.shape[0], n), w.dtype)
    out[:, :w.shape[1]] = w
    return out


def lay_out(a):
    a = {k: np.asarray(v) for k, v in a.items()}
    w_in = a["w_in"][0]
    nq = 12 * P
    order = np.concatenate([np.arange(nq)] + [np.arange(nq + HD * (c + 4 * g), nq + HD * (c + 4 * g) + HD)
                                              for c in range(4) for g in range(2)] + [np.arange(nq + 8 * HD, w_in.shape[1])])
    w_in = pad_columns(w_in[:, order], 23 * P)
    all8 = slice(0, 8)
    w2 = np.zeros((P, 8, P), np.float32)
    k2, v2 = a["k_cmp_w2"][0].reshape(2, P, HD), a["v_cmp_w2"][0].reshape(2, P, HD)
    for m in range(2):
        w2[:, m, 0:HD] = w2[:, m, HD:P] = k2[m]
        w2[:, 2 + m, 0:HD] = v2[m]
    w1 = [a["k_cmp_w1"][0], a["v_cmp_w1"][0]]
    wide = []
    for name in A_ORDER:
        if name.startswith("cmp"):
            kind, m = divmod(int(name[3]), 2)
            wide += [tiles_of(w1[kind], slice(8 * half, 8 * half + 8), m) for half in range(2)]
        else:
            wide.append(w2 if name == "w2" else tiles_of(w_in, all8, A_CHUNK[name]))
    down = []

    def swiglu(gate, up, w_down):
        for f in range(FC):
            wide.extend([tiles_of(gate, all8, f), tiles_of(up, all8, f)])
        for c in range(KC):
            down.extend([tiles_of(w_down, slice(DOWN_UNIT * h, DOWN_UNIT * (h + 1)), c) for h in range(2)])

    wide += [tiles_of(a["w_out"][0], all8, c) for c in range(KC)]
    swiglu(a["w_gate"][0], a["w_up"][0], a["w_down"][0])
    w = pad_columns(a["w_in_2"][0], 25 * P)
    wide += [tiles_of(w, all8, B_CHUNK[name]) for name in B_ORDER]
    wide += [tiles_of(a["w_out_2"][0], all8, c) for c in range(KC)]
    swiglu(a["w_ffn_in_2"][0][:, :F], a["w_ffn_in_2"][0][:, F:], a["w_ffn_out_2"][0])
    for c in range(KC):
        wide += [tiles_of(a["w_pw1_2"][0], all8, KC + c), tiles_of(a["w_pw1_2"][0], all8, c)]
    wide += [tiles_of(a["w_pw2_2"][0], all8, c) for c in range(KC)]
    swiglu(a["w_ffn_in_2"][1][:, :F], a["w_ffn_in_2"][1][:, F:], a["w_ffn_out_2"][1])

    cols = np.zeros((P, NCOL), np.float32)

    def put(name, vector):
        vector = vector.reshape(-1, P).T
        cols[:, COL[name]:COL[name] + vector.shape[1]] = vector

    for name, source in (("attn_pre", a["attn_pre_norm"][0]), ("attn_post", a["attn_post_norm"][0]),
                         ("ffn_pre", a["ffn_pre_norm"][0]), ("ffn_post", a["ffn_post_norm"][0]),
                         ("b_pw1", a["b_pw1_2"][0]), ("b_dw", a["b_dw_2"][0]), ("ln_g", a["ln_g_2"][0]),
                         ("ln_b", a["ln_b_2"][0]), ("b_pw2", a["b_pw2_2"][0]), ("subln", a["diff_subln"][0])):
        put(name, source)
    for j in range(2):
        put(f"mix_pre_{j}", a["norm_mix_pre_2"][j])
        put(f"mix_post_{j}", a["norm_mix_post_2"][j])
        put(f"ffn_pre_{j}", a["norm_ffn_pre_2"][j])
        put(f"ffn_post_{j}", a["norm_ffn_post_2"][j])
    cols[:, COL["w_dw"]:COL["w_dw"] + 8 * TAPS] = a["w_dw_2"][0].reshape(TAPS, KC, P).transpose(2, 1, 0).reshape(P, -1)
    cols[:, COL["w_short"]:COL["w_short"] + 12] = a["w_short_conv_2"][0].reshape(3, 4, P).transpose(2, 1, 0).reshape(P, -1)
    cols[0:8, COL["b_forget"]] = a["b_forget_2"][0]
    for name, source in (("k_pos", a["k_cmp_pos"][0]), ("v_pos", a["v_cmp_pos"][0])):
        cols[0:HD, COL[name]:COL[name] + 32] = cols[HD:P, COL[name]:COL[name] + 32] = source.T
    for j, name in enumerate(("lambda_q1", "lambda_k1", "lambda_q2", "lambda_k2")):
        cols[0:HD, COL["lam"] + j] = a[name][0]
    angles, tables = shape_tables()
    return {
        "in_xt": np.ascontiguousarray(a["x"][0].reshape(S, KC, P).transpose(2, 1, 0)),
        "in_cols": cols, "in_tables": tables, "in_angles": angles,
        "in_wide": np.ascontiguousarray(np.stack(wide)).reshape(len(wide), P, UNIT * P),
        "in_down": np.ascontiguousarray(np.stack(down)).reshape(len(down), P, DOWN_UNIT * P),
    }


def declare(nc, arrays, stop=99):
    ins = [nc.dram_tensor(k, v.shape, F32, kind="ExternalInput").ap() for k, v in arrays.items()]
    out = nc.dram_tensor("out", (P, KC, S), F32, kind="ExternalOutput").ap()
    two_blocks(nc, *ins, out, stop)


def kernel(**inputs):
    import concourse.bacc as _bacc
    from concourse.bass_utils import run_bass_kernel_spmd as _run
    arrays = lay_out(inputs)
    nc = _bacc.Bacc("TRN2", target_bir_lowering=False, num_devices=1, dynamic_dma_scratch_size=1024)
    declare(nc, arrays)
    got = _run(nc, [arrays], core_ids=[0]).results[0]["out"]
    return np.ascontiguousarray(got.transpose(2, 1, 0).reshape(1, S, D))
```

```python
import math
from contextlib import ExitStack, contextmanager

import numpy as np

import concourse.bass as bass
from concourse import mybir

P = 128
S = 512
D = 1024
KC = D // P
NB = S // P
HD = 64
F = 2816
FC = F // P
CMP_STRIDE, CMP_LEN = 16, 32
NCMP = (S - CMP_LEN) // CMP_STRIDE + 1
TAPS = 31
NEG = -1e30
EPS_RMS, EPS_LN = 1e-6, 1e-5
LAM_INIT = 0.8 - 0.6 * math.exp(-0.3 * 0)

UNIT, DOWN_UNIT = 8, FC // 2
SLOTS, RAW = 4, 4
A_ORDER = ["kc", "vc", "nq0", "nq1", "nq2", "cmp0", "nq3", "cmp1", "gates", "cmp2", "ks", "cmp3", "vs", "w2", "kw", "vw"] + \
          [f"{w}{c}" for w in ("dq", "dk", "dv") for c in range(4)]
A_CHUNK = {**{f"{w}{c}": 4 * j + c for j, w in enumerate(("dq", "dk", "dv", "nq")) for c in range(4)},
           "kc": 16, "vc": 17, "ks": 18, "vs": 19, "kw": 20, "vw": 21, "gates": 22}
A_UNITS = sum(2 if a.startswith("cmp") else 1 for a in A_ORDER)
CMP_FROM = A_ORDER.index("kw") + 1
B_ORDER = ["f"] + [f"{w}{c}" for c in range(4) for w in ("gc", "xa", "gb")] + [f"{w}{c}" for w in "vqk" for c in range(4)]
B_CHUNK = {**{f"{w}{c}": 4 * j + c for j, w in enumerate(("gb", "gc", "xa", "q", "k", "v")) for c in range(4)}, "f": 24}
SEGMENTS = [(UNIT, A_UNITS + KC + 2 * FC), (DOWN_UNIT, 2 * KC),
            (UNIT, len(B_ORDER) + KC + 2 * FC), (DOWN_UNIT, 2 * KC),
            (UNIT, 2 * KC + KC + 2 * FC), (DOWN_UNIT, 2 * KC)]
_A, _B = A_UNITS + KC, len(B_ORDER) + KC
_FFN = 2 * FC + 2 * KC
NORMS_AT = [_A, _A + _FFN, _A + _FFN + _B, _A + 2 * _FFN + _B, _A + 2 * _FFN + _B + 3 * KC, _A + 3 * _FFN + _B + 3 * KC]
A_NQ_ROPES = 5
CONV_PE = (5, 6, 7)
CONV_ORDER = [0, 1, 2, 5, 3, 6, 4, 7]
CONV_PACE = 10
DIAGONALS = 40


def partnered_chunk(name):
    if name[:2] in ("dq", "dk", "nq", "kc", "ks", "kw"):
        return "rope"
    return "turn" if name[:2] in ("dv", "vs", "vw", "ga", "v0", "v1", "v2", "v3") else None


F32, F32R, BF16 = mybir.dt.float32, mybir.dt.float32r, mybir.dt.bfloat16
ALU = mybir.AluOpType
ACT = mybir.ActivationFunctionType
AX = mybir.AxisListType.X

_COLS = [("attn_pre", 8), ("attn_post", 8), ("ffn_pre", 8), ("ffn_post", 8),
         ("mix_pre_0", 8), ("mix_post_0", 8), ("ffn_pre_0", 8), ("ffn_post_0", 8),
         ("mix_pre_1", 8), ("mix_post_1", 8), ("ffn_pre_1", 8), ("ffn_post_1", 8),
         ("b_pw1", 16), ("b_dw", 8), ("ln_g", 8), ("ln_b", 8), ("b_pw2", 8), ("w_dw", 8 * TAPS), ("w_short", 12),
         ("subln", 1), ("b_forget", 1), ("k_pos", 32), ("v_pos", 32), ("lam", 4)]
COL, NCOL = {}, 0
for _name, _n in _COLS:
    COL[_name] = NCOL
    NCOL += _n
_TABS = [("rot", P), ("ident", P), ("causal", P), ("cmp_mask", NB * 32), ("cmp_keep", 32)]
TAB, NTAB = {}, 0
for _name, _n in _TABS:
    TAB[_name] = NTAB
    NTAB += _n


class Count:

    def __init__(self):
        self.base, self.reg, self.per = {}, None, {}

    def now(self, name, more=0):
        value = self.base.get(name, 0) + more
        return self.reg * self.per[name] + value if self.reg is not None and name in self.per else value

    def take(self, name, n=1):
        self.base[name] = self.base.get(name, 0) + n
        return self.now(name)

    @contextmanager
    def loop(self, engine, times, **per):
        start = dict(self.base)
        with engine.Fori(0, times) as i:
            self.reg, self.per = i, per
            yield i
        for name, value in self.base.items():
            assert value - start.get(name, 0) == per.get(name, 0), name
            self.base[name] = start.get(name, 0) + times * (value - start.get(name, 0))
        self.reg, self.per = None, {}


def diff_rows():
    return [("diff", h, 0, i) for h in range(4) for i in range(NB)]


def nsa_rows():
    return [("nsa", n, b, i) for n in range(8) for b in (1, 2) for i in range(NB)]


def fox_rows():
    return [("fox", n, 0, i) for n in range(8) for i in range(NB)]


def scores_of(row):
    return 2 if row[0] == "diff" else 1


LAG_TURN, LAG_MIX = 3, 4
TURNED_BY_ACT = (1, 2, 3)


def two_blocks(nc, xt, cols_in, tabs_in, angles_in, w8, w11, out):
    ctx = ExitStack()
    with ctx:
        def sb(name, shape, dt=F32, where=None):
            return (where or ctx).enter_context(nc.sbuf_tensor(name, shape, dt))

        def sem(name):
            return ctx.enter_context(nc.semaphore(name))

        x = sb("x", [P, KC, S])
        cols = sb("cols", [P, NCOL])
        tabs = sb("tabs", [P, NTAB])
        ones = sb("ones", [P, P])
        raw = sb("raw", [P, RAW, DOWN_UNIT * P])
        w_hi = sb("w_hi", [P, SLOTS, DOWN_UNIT * P], F32R)
        w_lo = sb("w_lo", [P, SLOTS, DOWN_UNIT * P], F32R)
        squares = sb("squares", [P, 2, S])
        total = sb("total", [P, S])
        scale_row = sb("scale_row", [P, S])
        variance = sb("variance", [P, NB])
        root = sb("root", [P, NB])
        scale_col = sb("scale_col", [P, NB])
        tmp = sb("tmp", [P, 2, S])
        ident16 = sb("ident16", [P, P], BF16)
        causal16 = sb("causal16", [P, P], BF16)
        spare = sb("spare", [P, 1])
        lam = sb("lam", [P, 8])
        subln_s = sb("subln_s", [P, 1])
        k_cmp = sb("k_cmp", [P, 2 * NCMP])
        v_cmp = sb("v_cmp", [P, 2, 4 * HD])
        cmp_small = sb("cmp_small", [P, 4, NB, 8])
        diff_ms = sb("diff_ms", [P, 4, 16])
        region = ExitStack()
        h_hi = sb("h_hi", [P, KC, S], F32R, region)
        region.close()
        m_ffn = sb("m_ffn", [P, KC, S])
        h_lo = sb("h_lo", [P, KC, S], F32R)

        region = ExitStack()
        g_hi = sb("g_hi", [P, FC, S], F32R, region)
        g_lo = sb("g_lo", [P, FC, S], F32R, region)
        region.close()
        region = ExitStack()
        m_mix = sb("m_mix", [P, KC, S], F32, region)
        region.close()
        region = ExitStack()
        dqk = sb("dqk", [P, 8, S], F32, region)
        nqk = sb("nqk", [P, 8, S], F32, region)
        v_diff = sb("v_diff", [P, NB, 4 * P], F32, region)
        v_nsa = sb("v_nsa", [P, 2, NB, P], F32, region)
        o_all = sb("o_all", [P, NB, D], F32, region)
        gates = sb("gates", [P, NB, 24], F32, region)
        angles = o_all[:, 0:2, 0:S]
        stage = ExitStack()
        blocks_hi = sb("blocks_hi", [P, 2, 16, 2 * NCMP], F32R, stage)
        blocks_lo = sb("blocks_lo", [P, 2, 16, 2 * NCMP], F32R, stage)
        blocks = sb("blocks", [P, 2, 16, 2 * NCMP], F32, stage)
        hid = sb("hid", [P, 4, 2 * NCMP], F32, stage)
        hid_s = sb("hid_s", [P, 4, 2 * NCMP], F32, stage)
        hid_hi = sb("hid_hi", [P, 4, 2 * NCMP], F32R, stage)
        hid_lo = sb("hid_lo", [P, 4, 2 * NCMP], F32R, stage)
        stage.close()
        e_ring = sb("e_ring", [P, 2, 4, S], F32, region)
        t_ring = sb("t_ring", [P, 3, NB, P], F32, region)
        neg_max = sb("neg_max", [P, 96], F32, region)
        row_sum = sb("row_sum", [P, 96], F32, region)
        inv_sum = sb("inv_sum", [P, 96], F32, region)
        coef = sb("coef", [P, 96], F32, region)
        region.close()
        region = ExitStack()
        sb("below_m_mix_b", [P, 1], F32, region)
        q_fox = sb("q_fox", [HD + 1, 8, S], F32, region)
        k_fox = sb("k_fox", [HD + 1, 8, S], F32, region)
        v_fox = sb("v_fox", [P, NB, 8 * HD], F32, region)
        o_fox = sb("o_fox", [P, NB, 8 * HD], F32, region)
        y_conv = sb("y_conv", [P, 4, S], F32, region)
        padded = sb("padded", [P, S + 2], F32, region)
        e_ring_b = sb("e_ring_b", [P, 2, 4, S], F32, region)
        t_ring_b = sb("t_ring_b", [P, 3, NB, P], F32, region)
        neg_max_b = sb("neg_max_b", [P, 32], F32, region)
        row_sum_b = sb("row_sum_b", [P, 32], F32, region)
        inv_sum_b = sb("inv_sum_b", [P, 32], F32, region)
        region.close()
        region = ExitStack()
        forget = sb("forget", [8, 5, S], F32, region)
        region.close()
        region = ExitStack()
        glu = sb("glu", [P, KC, S + TAPS - 1], F32, region)
        y_dw = sb("y_dw", [P, KC, S], F32, region)
        diag_hi = sb("diag_hi", [P, DIAGONALS, P], F32R, region)
        diag_lo = sb("diag_lo", [P, DIAGONALS, P], F32R, region)
        glu_hi = sb("glu_hi", [P, len(CONV_PE), S + TAPS - 1], F32R, region)
        glu_lo = sb("glu_lo", [P, len(CONV_PE), S + TAPS - 1], F32R, region)
        taps_hi = sb("taps_hi", [P, len(CONV_PE) * TAPS], F32R, region)
        taps_lo = sb("taps_lo", [P, len(CONV_PE) * TAPS], F32, region)
        region.close()

        psum = ctx.enter_context(nc.psum_tensor("psum", [P, 8, 512], F32))
        STAT_ROW, STAT_COL = 6, 7
        rot, ident = tabs[:, TAB["rot"]:TAB["rot"] + P], tabs[:, TAB["ident"]:TAB["ident"] + P]

        weights_landed = [sem(f"weights_landed_{j}") for j in range(RAW)]
        x_landed = [sem(f"x_landed_{j}") for j in range(4)]
        cols_landed, tabs_landed, decay_landed, stored = (
            sem(s) for s in ("cols_landed", "tabs_landed", "decay_landed", "stored"))
        unit_taken, high_split, units_split = sem("unit_taken"), sem("high_split"), sem("units_split")
        x_ready = sem("x_ready")
        unit_done, column_added, row_added, row_turned, row_spread, partnered, conv_done, tap_used = (
            sem(s) for s in ("unit_done", "column_added", "row_added", "row_turned", "row_spread", "partnered", "conv_done", "tap_used"))
        lam_summed, cmp_scored, cmp_transposed, cmp_mixed = (
            sem(s) for s in ("lam_summed", "cmp_scored", "cmp_transposed", "cmp_mixed"))
        scored, transposed, mixed, o_turned = (sem(s) for s in ("scored", "transposed", "mixed", "o_turned"))
        row_out = sem("row_out")
        evacuated, summed, col_scaled, col_ready, row_ready = (
            sem(s) for s in ("evacuated", "summed", "col_scaled", "col_ready", "row_ready"))
        post_scaled, h_low = sem("post_scaled"), sem("h_low")
        set_up, rope_cos, rope_added, angles_scaled, partner_read = (
            sem(s) for s in ("set_up", "rope_cos", "rope_added", "angles_scaled", "partner_read"))
        conv_chunk, glu_low, taps_split = sem("conv_chunk"), sem("glu_low"), sem("taps_split")
        blocks_added, blocks_low, hid_low, cmp_step, cmp_weighed, cmp_done = (
            sem(s) for s in ("blocks_added", "blocks_low", "hid_low", "cmp_step", "cmp_weighed", "cmp_done"))
        maxed, combined, coef_step, turned_dve, row_done, diff_step = (
            sem(s) for s in ("maxed", "combined", "coef_step", "turned_dve", "row_done", "diff_step"))
        hidden, hidden_low, mix_step, forget_step, glu_ready, tapped, centred, normed = (
            sem(s) for s in ("hidden", "hidden_low", "mix_step", "forget_step", "glu_ready", "tapped", "centred", "normed"))
        glu_high, diag_ready = sem("glu_high"), sem("diag_ready")
        h_high, squared, rooted, lam_exped, gates_ready = (
            sem(s) for s in ("h_high", "squared", "rooted", "lam_exped", "gates_ready"))
        blocks_high, hid_silu, hid_high, cmp_exped, cmp_turned = (
            sem(s) for s in ("blocks_high", "hid_silu", "hid_high", "cmp_exped", "cmp_turned"))
        exped, turned_act, diff_squared, diff_rooted = (
            sem(s) for s in ("exped", "turned_act", "diff_squared", "diff_rooted"))
        silu_ready, hidden_high, forget_act, sigmoid_ready, ln_silu = (
            sem(s) for s in ("silu_ready", "hidden_high", "forget_act", "sigmoid_ready", "ln_silu"))

        def col(name, j=0, n=1):
            return cols[:, bass.ds(j + COL[name], n)]

        def rope_place(name):
            c = int(name[2]) if name[2:] else 0
            return {"dq": dqk[:, c, :], "dk": dqk[:, 4 + c, :], "nq": nqk[:, c, :], "kc": nqk[:, 4, :],
                    "ks": nqk[:, 6, :], "kw": nqk[:, 7, :]}[name[:2]]

        def query(row, m):
            kind, n, b, i = row
            t = slice(i * P, (i + 1) * P)
            if kind == "diff":
                return dqk[HD * m:HD * m + HD, n, t]
            if kind == "nsa":
                return nqk[HD * (n // 4):HD * (n // 4) + HD, n % 4, t]
            return q_fox[:, n, t]

        def keys(row, m):
            kind, n, b, i = row
            t = slice(0, (i + 1) * P)
            if kind == "diff":
                return dqk[HD * m:HD * m + HD, 4 + n, t]
            if kind == "nsa":
                return nqk[HD * (n // 4):HD * (n // 4) + HD, 5 + b, t]
            return k_fox[:, n, t]

        def values(row, j):
            kind, n, b, i = row
            if kind == "diff":
                return v_diff[:, j, n * P:(n + 1) * P]
            if kind == "nsa":
                return v_nsa[:, b - 1, j, HD * (n // 4):HD * (n // 4) + HD]
            return v_fox[:, j, HD * n:HD * n + HD]

        def mixed_place(row):
            kind, n, b, i = row
            if kind == "diff":
                return o_all[:, i, n * P:(n + 1) * P]
            if kind == "nsa":
                return o_all[:, i, 4 * P + HD * n:4 * P + HD * n + HD]
            return o_fox[:, i, HD * n:HD * n + HD]

        block = ctx.enter_context(nc.Block())

        @block.sync
        def _(sp):
            sp.dma_start(cols[:], cols_in).then_inc(cols_landed, 16)
            n = Count()
            at = {UNIT: 0, DOWN_UNIT: 0}

            def load(tiles, source, i, j):
                slot = j % RAW
                if n.base.get("units_split", 0) + 1 > RAW:
                    sp.wait_ge(units_split, n.now("units_split", 1 - RAW))
                n.take("units_split")
                sp.dma_start(raw[:, slot, 0:tiles * P], source[i]).then_inc(weights_landed[slot], 16)

            for tiles, count in SEGMENTS:
                source = w8 if tiles == UNIT else w11
                peel = SLOTS if n.base.get("units_split", 0) == 0 else 0
                for j in range(peel):
                    load(tiles, source, j, j)
                if peel:
                    sp.dma_start(tabs[:], tabs_in).then_inc(tabs_landed, 16)
                    sp.dma_start(angles, angles_in).then_inc(tabs_landed, 16)
                times, rest = divmod(count - peel, SLOTS)
                phase = n.base.get("units_split", 0)
                first = at[tiles] + peel
                with n.loop(sp, times, units_split=SLOTS) as i:
                    for j in range(SLOTS):
                        load(tiles, source, i * SLOTS + (first + j), phase + j)
                for j in range(rest):
                    load(tiles, source, first + times * SLOTS + j, phase + j)
                at[tiles] += count
            for c in range(KC):
                sp.wait_ge(x_ready, 5 * KC + c + 1)
                sp.dma_start(out[:, c, :], x[:, c, :]).then_inc(stored, 16)
            sp.wait_ge(stored, 16 * KC)

        @block.gpsimd
        def _(pool):
            n = Count()

            def split(tiles, j):
                slot, w = j % SLOTS, tiles * P
                pool.wait_ge(weights_landed[j % RAW], n.take(f"landed_{j % RAW}", 16))
                if n.base.get("units", 0) >= SLOTS:
                    pool.wait_ge(unit_done, n.now("units", 1 - SLOTS))
                pool.sem_inc(unit_taken, 1)
                nc.gpsimd.tensor_scalar(w_hi[:, slot, 0:w], raw[:, j % RAW, 0:w], 1.0, 1.0, ALU.mult, ALU.mult)\
                    .then_inc(high_split, 1)
                pool.wait_ge(high_split, n.take("units"))
                nc.gpsimd.tensor_tensor(w_lo[:, slot, 0:w], raw[:, j % RAW, 0:w], w_hi[:, slot, 0:w].bitcast(F32),
                                        ALU.subtract).then_inc(units_split, 1)

            def add_norm():
                n.take("post_scaled")
                for c in range(1, KC):
                    pool.wait_ge(post_scaled, n.take("post_scaled"))
                    nc.gpsimd.tensor_tensor(x[:, c, :], x[:, c, :], tmp[:, c % 2, :], ALU.add).then_inc(x_ready, 1)

            ends, u = [], 0
            for tiles, count in SEGMENTS:
                cuts = [at + SLOTS for at in NORMS_AT[:-1] if u < at + SLOTS <= u + count]
                for at in cuts:
                    ends.append((tiles, at, True))
                if (cuts or [None])[-1] != u + count:
                    ends.append((tiles, u + count, False))
                u += count
            for tiles, end, norm_after in ends:
                count = end - n.base.get("units", 0)
                peel = SLOTS if n.base.get("units", 0) == 0 else 0
                for j in range(peel):
                    split(tiles, j)
                times, rest = divmod(count - peel, SLOTS)
                phase = n.base.get("units", 0)
                per = {f"landed_{j}": 16 * SLOTS // RAW for j in range(RAW)}
                if times:
                    with n.loop(pool, times, units=SLOTS, **per):
                        for j in range(SLOTS):
                            split(tiles, phase + j)
                for j in range(rest):
                    split(tiles, phase + j)
                if norm_after:
                    add_norm()
            add_norm()

        @block.tensor
        def _(pe):
            n = Count()

            def three(out_ap, lhs, rhs, first, last):
                pe.matmul(out_ap, lhs[0], rhs[0], start=first, stop=False)
                pe.matmul(out_ap, lhs[0], rhs[1], start=False, stop=False)
                return pe.matmul(out_ap, lhs[1], rhs[0], start=False, stop=last)

            def next_unit():
                slot = n.base.get("units_split", 0) % SLOTS
                pe.wait_ge(units_split, n.take("units_split"))
                return [lambda t, w=w: w[:, slot, t * P:(t + 1) * P] for w in (w_hi, w_lo)]

            def next_bank():
                g = n.base.get("group", 0)
                if g >= 4:
                    pe.wait_ge(evacuated, n.now("group", -3))
                n.take("group")
                return g % 4

            def feature_unit(h, tiles=UNIT, first=True, last=True, bank=None, width=S, k_wait=None):
                w = next_unit()
                for t in range(tiles):
                    if k_wait is not None:
                        pe.wait_ge(h_low, k_wait + t + 1)
                    mm = three(psum[:, bank, 0:width], [w[0](t), w[1](t)], h(t), first and t == 0,
                               last and t == tiles - 1)
                mm.then_inc(unit_done, 1)

            def h_of(t):
                return [h_hi[:, t, :], h_lo[:, t, :]]

            def stay_warm(times, bank=5):
                for _ in range(times):
                    pe.matmul(psum[:, bank, :].rearrange("p (b t) -> p b t", b=NB), ones[:],
                              ones[:].unsqueeze(1).to_broadcast([P, NB, P]), start=True, stop=True)

            def col_stat():
                stay_warm(1)
                pe.wait_ge(summed, n.take("summed", KC))
                add_columns(total, True, False)
                pe.wait_ge(squared, n.take("squared", KC))
                add_columns(squares[:, (KC - 1) % 2, :], False, True)
                stay_warm(2)

            def add_columns(source, first, last):
                for b in range(NB):
                    mm = pe.matmul(psum[:, STAT_COL, b:b + 1], source[:, b * P:(b + 1) * P], ones[:, 0:1],
                                   start=first and b == 0, stop=last and b == NB - 1, skip_group_check=True)
                mm.then_inc(column_added, 1)

            def add_row(source, first, last, bank=STAT_COL):
                pe.matmul(psum[:, bank, :], ones[:], source, start=first, stop=last).then_inc(row_added, 1)

            def row_to_column():
                pe.wait_ge(row_out, n.take("row_out"))
                for b in range(NB):
                    mm = pe.matmul(psum[:, STAT_COL, b:b + 1], total[0:1, b * P:(b + 1) * P], ones[0:1, 0:1], start=True, stop=True)
                mm.then_inc(row_turned, 1)

            def row_stat():
                pe.wait_ge(col_ready, n.take("col_ready"))
                for b in range(NB):
                    mm = pe.matmul(psum[:, STAT_ROW, b * P:(b + 1) * P], scale_col[:, b:b + 1].to_broadcast([P, P]),
                                   ident, start=True, stop=True)
                mm.then_inc(row_spread, 1)

            def first_unit():
                bank = next_bank()
                w = next_unit()
                for t in range(UNIT):
                    pe.wait_ge(h_low, n.take("h_low"))
                    mm = three(psum[:, bank, :], [w[0](t), w[1](t)], h_of(t), t == 0, t == UNIT - 1)
                    if t == UNIT - 1:
                        mm.then_inc(unit_done, 1)
                    if t:
                        pe.wait_ge(squared, n.take("squared"))
                        add_row(squares[:, (t - 1) % 2, :], t == 1, False)
                pe.wait_ge(squared, n.take("squared"))
                add_row(squares[:, (UNIT - 1) % 2, :], False, True)

            def partner(name, behind=1):
                r = n.base.get("partners", 0)
                pe.wait_ge(evacuated, n.now("group", -behind))
                if r >= 2:
                    pe.wait_ge(partner_read, r - 1)
                if partnered_chunk(name) == "rope":
                    mm = pe.matmul(psum[:, 4 + r % 2, :], rot, tmp[:, r % 2, :], start=True, stop=True)
                else:
                    for b in range(NB):
                        mm = pe.transpose(psum[:, 4 + r % 2, b * P:(b + 1) * P], tmp[:, r % 2, b * P:(b + 1) * P], ident)
                mm.then_inc(partnered, 1)
                n.take("partners")

            def project(order, other=lambda name: False, after=lambda j: None):
                for j, name in enumerate(order):
                    if j == 0:
                        first_unit()
                    elif not other(name):
                        feature_unit(h_of, bank=next_bank())
                    if j == 0:
                        row_to_column()
                    if j == 1:
                        row_stat()
                    if j and partnered_chunk(order[j - 1]):
                        partner(order[j - 1])
                    after(j)

            def w_out():
                start = n.base["h_low"]
                n.take("h_low", KC)
                for u in range(KC):
                    feature_unit(h_of, bank=next_bank(), k_wait=start if u == 0 else None)
                col_stat()
                row_stat()
                stay_warm(4)

            def swiglu():
                project("-" * 4)
                times = (2 * FC - 4) // 4
                with n.loop(pe, times, units_split=4, group=4):
                    for u in range(4):
                        feature_unit(h_of, bank=next_bank())
                pe.wait_ge(hidden_low, n.take("hidden_low", FC))
                with n.loop(pe, 2, units_split=8, group=4):
                    for c in range(4):
                        bank = next_bank()
                        for half in range(2):
                            feature_unit(lambda t: [g_hi[:, half * DOWN_UNIT + t, :], g_lo[:, half * DOWN_UNIT + t, :]],
                                         DOWN_UNIT, half == 0, half == 1, bank)
                col_stat()
                row_stat()
                stay_warm(4)

            def attention(rows, e, t_out, warm):
                base = {k: n.base.get(k, 0) for k in ("scored", "rows", "combined", "turned_act", "turned_dve")}
                pe.wait_ge(evacuated, n.now("group"))
                first_score = np.cumsum([0] + [scores_of(r) for r in rows]).tolist()

                def turned_before(r, what):
                    return sum((row[3] in TURNED_BY_ACT) == (what == "act") for row in rows[:r + 1])

                def wait_turned(r):
                    act = rows[r][3] in TURNED_BY_ACT
                    pe.wait_ge(turned_act if act else turned_dve,
                               base["turned_act" if act else "turned_dve"] + turned_before(r, "act" if act else "dve"))

                for t in range(len(rows) + LAG_MIX):
                    if t < len(rows):
                        i = rows[t][3]
                        for m in range(scores_of(rows[t])):
                            s = first_score[t] + m
                            if s >= 4:
                                pe.wait_ge(exped, base["scored"] + s - 3)
                            if m == 0:
                                stay_warm(warm.get(t, 0), s % 4)
                            pe.matmul(psum[:, s % 4, 0:(i + 1) * P], query(rows[t], m), keys(rows[t], m),
                                      start=True, stop=False)
                            pe.matmul(psum[:, s % 4, i * P:(i + 1) * P], ident16[:], causal16[:],
                                      start=False, stop=True).then_inc(scored, 1)
                    r = t - LAG_TURN
                    if 0 <= r < len(rows):
                        if rows[r][0] == "diff":
                            pe.wait_ge(combined, base["combined"] + r + 1)
                        else:
                            pe.wait_ge(exped, base["scored"] + first_score[r + 1])
                        if r >= 2:
                            wait_turned(r - 2)
                        for j in range(rows[r][3] + 1):
                            mm = pe.transpose(psum[:, 4 + r % 2, j * P:(j + 1) * P], e[:, 0, r % 4, j * P:(j + 1) * P],
                                              ident)
                        mm.then_inc(transposed, 1)
                    r = t - LAG_MIX
                    if 0 <= r < len(rows):
                        wait_turned(r)
                        if r >= 2:
                            pe.wait_ge(row_done, base["rows"] + r - 1)
                        width = P if rows[r][0] == "diff" else HD
                        for j in range(rows[r][3] + 1):
                            mm = pe.matmul(psum[:, 6 + r % 2, 0:width], t_out[:, r % 3, j, :], values(rows[r], j),
                                           start=j == 0, stop=j == rows[r][3])
                        mm.then_inc(mixed, 1)
                n.take("scored", first_score[-1])
                n.take("rows", len(rows))
                n.take("combined", sum(r[0] == "diff" for r in rows))
                n.take("turned_act", turned_before(len(rows), "act"))
                n.take("turned_dve", turned_before(len(rows), "dve"))

            def turn_outputs(o, chunks, done):
                for c in range(chunks):
                    if c >= 4:
                        pe.wait_ge(h_low, done + c - 3)
                    for b in range(NB):
                        mm = pe.transpose(psum[:, 4 + c % 4, b * P:(b + 1) * P], o[:, b, c * P:(c + 1) * P], ident)
                    mm.then_inc(o_turned, 1)

            def compression(name):
                if name.startswith("cmp"):
                    kind, m = divmod(int(name[3]), 2)
                    pe.wait_ge(blocks_low, kind + 1)
                    bank = next_bank()
                    for half in range(2):
                        feature_unit(lambda t: [blocks_hi[:, kind, half * UNIT + t, :], blocks_lo[:, kind, half * UNIT + t, :]],
                                     UNIT, half == 0, half == 1, bank, 2 * NCMP)
                    return True
                if name != "w2":
                    return False
                pe.wait_ge(hid_low, 1)
                bank = next_bank()
                w = next_unit()
                for m in range(2):
                    three(psum[:, bank, 0:2 * NCMP], [w[0](m), w[1](m)], [hid_hi[:, m, :], hid_lo[:, m, :]], m == 0, m == 1)
                for g in range(2):
                    part = slice(g * NCMP, (g + 1) * NCMP)
                    for m in range(2):
                        mm = three(psum[0:NCMP, bank, HD + g * HD:2 * HD + g * HD],
                                   [hid_hi[:, 2 + m, part], hid_lo[:, 2 + m, part]],
                                   [w[0](2 + m)[:, 0:HD], w[1](2 + m)[:, 0:HD]], m == 0, m == 1)
                mm.then_inc(unit_done, 1)
                return True

            def cmp_attention(j):
                if j == 0:
                    pe.wait_ge(set_up, 2)
                    pe.matmul(psum[:, 3, 0:2], ones[0:HD, :], lam[0:HD, 0:2], start=True, stop=True).then_inc(lam_summed, 1)
                if j == 2:
                    pe.wait_ge(lam_exped, 1)
                i, step = divmod(j - CMP_FROM, 3)
                if j < CMP_FROM or i >= NB:
                    return
                if step == 0:
                    if i == 0:
                        pe.wait_ge(evacuated, A_ORDER.index("w2") + 1)
                        pe.wait_ge(rope_added, A_NQ_ROPES)
                    else:
                        pe.wait_ge(cmp_done, i)
                    for head in range(8):
                        g = head // 4
                        mm = pe.matmul(psum[:, 6 + g, 32 * (head % 4):32 * (head % 4) + NCMP],
                                       nqk[HD * g:HD * g + HD, head % 4, i * P:(i + 1) * P],
                                       k_cmp[HD * g:HD * g + HD, g * NCMP:(g + 1) * NCMP], start=True, stop=True)
                    mm.then_inc(cmp_scored, 1)
                elif step == 1:
                    pe.wait_ge(cmp_weighed, i + 1)
                    for g in range(2):
                        mm = pe.transpose(psum[:, 6, g * P:(g + 1) * P], e_ring[:, 0, i, g * P:(g + 1) * P], ident)
                    mm.then_inc(cmp_transposed, 1)
                else:
                    pe.wait_ge(cmp_turned, i + 1)
                    for g in range(2):
                        mm = pe.matmul(psum[:, 7, g * 4 * HD:(g + 1) * 4 * HD], t_ring[:, 0, 2 * (i % 2) + g, :],
                                       v_cmp[:, g, :], start=True, stop=True)
                    mm.then_inc(cmp_mixed, 1)

            pe.wait_ge(set_up, 1)
            stay_warm(7)
            project(A_ORDER, compression, cmp_attention)
            partner(A_ORDER[-1], 0)
            pe.wait_ge(cmp_done, NB)

            attention(diff_rows() + nsa_rows(), e_ring, t_ring, {28: 2, 29: 2, 30: 2, 31: 2, 32: 2, 33: 2})
            pe.wait_ge(row_done, n.now("rows"))
            pe.wait_ge(diff_step, 2 * NB + 2)
            turn_outputs(o_all, KC, n.base["h_low"])
            w_out()
            swiglu()

            project(B_ORDER)
            pe.wait_ge(decay_landed, 16 * 8)
            attention(fox_rows(), e_ring_b, t_ring_b, {1: 2, 2: 2, 3: 2, 4: 2, 5: 1})
            pe.wait_ge(row_done, n.now("rows"))
            turn_outputs(o_fox, 4, n.base["h_low"])
            w_out()
            swiglu()

            def conv(j):
                pe.wait_ge(glu_low, j + 1)
                for k in range(TAPS):
                    d = j * TAPS + k
                    pe.wait_ge(diag_ready, 2 * (d + 1))
                    d %= DIAGONALS
                    three(psum[:, 4 + j % 2, :], [diag_hi[:, d, :], diag_lo[:, d, :]],
                          [glu_hi[:, j, k:k + S], glu_lo[:, j, k:k + S]], k == 0, k == TAPS - 1)\
                        .then_inc(tap_used, 1)

            def add_means(first, last):
                for c in range(first, last):
                    pe.wait_ge(conv_chunk, c + 1)
                    add_row(y_dw[:, CONV_ORDER[c], :], c == 0, c == KC - 1)

            project("-" * 4)
            with n.loop(pe, 3, units_split=4, group=4):
                for u in range(4):
                    feature_unit(h_of, bank=next_bank())
            conv(0)
            add_means(0, 3)
            conv(1)
            add_means(3, 5)
            conv(2)
            add_means(5, KC)
            for c in range(KC):
                pe.wait_ge(squared, n.take("squared"))
                add_row(squares[:, c % 2, :], c == 0, c == KC - 1, STAT_ROW)
            row_to_column()
            row_stat()
            w_out()
            swiglu()

        @block.scalar
        def _(act):
            n = Count()

            def copy(out_ap, in_ap, **kw):
                return nc.scalar.activation(out_ap, in_ap, ACT.Copy, **kw)

            def square(j, source, of_x):
                if j >= 2 and of_x:
                    act.wait_ge(row_added, n.base.get("row_added", 0) + j - 1)
                elif j >= 2:
                    act.wait_ge(summed, n.base.get("summed", 0) + j)
                nc.scalar.activation(squares[:, j % 2, :], source, ACT.Square).then_inc(squared, 1)

            def load_sqrt():
                nc.scalar.activation(spare[:], ones[:, 0:1], ACT.Sqrt)

            def roots(of_x):
                if of_x:
                    n.take("row_added", KC)
                    act.wait_ge(row_turned, n.take("row_turned"))
                else:
                    n.take("summed", KC)
                    act.wait_ge(col_scaled, n.take("col_scaled"))
                nc.scalar.activation(root[:], psum[:, STAT_COL, 0:NB] if of_x else variance[:], ACT.Sqrt).then_inc(rooted, 1)

            def norm(pre):
                for c in range(KC + 1):
                    if c < KC:
                        act.wait_ge(x_ready, n.take("x_ready"))
                        copy(h_hi[:, c, :], x[:, c, :], scale=col(pre, c)).then_inc(h_high, 1)
                    if c:
                        square(c - 1, x[:, c - 1, :], True)
                roots(True)

            def outputs(m, k, bias=None):
                load_sqrt()
                for c in range(KC - 1):
                    act.wait_ge(evacuated, n.take("evacuated"))
                    square(c, m[:, c, :], False)
                act.wait_ge(unit_done, NORMS_AT[k])
                act.wait_ge(summed, n.base.get("summed", 0) + KC - 1)
                kw = dict(bias=col(bias, KC - 1)) if bias else {}
                bank = n.base["evacuated"] % 4
                nc.scalar.activation(squares[:, (KC - 1) % 2, :], psum[:, bank, :], ACT.Square, **kw).then_inc(squared, 1)
                n.take("evacuated")
                roots(False)

            def swiglu(m, k):
                def chunk(f):
                    act.wait_ge(evacuated, n.take("evacuated"))
                    nc.scalar.activation(squares[:, 0, :], tmp[:, 0, :], ACT.Silu).then_inc(silu_ready, 1)
                    n.take("evacuated")
                    act.wait_ge(hidden, n.take("hidden"))
                    copy(g_hi[:, f, :], squares[:, 1, :]).then_inc(hidden_high, 1)

                chunk(0)
                chunk(1)
                with n.loop(act, FC // 2 - 1, evacuated=4, hidden=2) as i:
                    chunk(i * 2 + 2)
                    chunk(i * 2 + 3)
                outputs(m, k)

            def attention(rows, e, t_out, maxima, sums, extra=lambda t: None):
                base = {k: n.base.get(k, 0) for k in ("scored", "rows")}
                first_score = np.cumsum([0] + [scores_of(r) for r in rows]).tolist()
                for t in range(len(rows) + LAG_TURN + 1):
                    if t < len(rows):
                        i = rows[t][3]
                        if t >= 4:
                            act.wait_ge(transposed, base["rows"] + t - 3)
                        for m in range(scores_of(rows[t])):
                            s = first_score[t] + m
                            act.wait_ge(maxed, base["scored"] + s + 1)
                            nc.scalar.activation(e[:, m, t % 4, 0:(i + 1) * P], psum[:, s % 4, 0:(i + 1) * P], ACT.Exp,
                                                 bias=maxima[:, s:s + 1], accum_out=sums[:, s:s + 1]).then_inc(exped, 1)
                    r = t - LAG_TURN
                    if 0 <= r < len(rows) and rows[r][3] in TURNED_BY_ACT:
                        act.wait_ge(transposed, base["rows"] + r + 1)
                        if r >= 3:
                            act.wait_ge(mixed, base["rows"] + r - 2)
                        w = (rows[r][3] + 1) * P
                        copy(t_out[:, r % 3, 0:rows[r][3] + 1, :].rearrange("p b q -> p (b q)"), psum[:, 4 + r % 2, 0:w])\
                            .then_inc(turned_act, 1)
                    extra(t)
                n.take("scored", first_score[-1])
                n.take("rows", len(rows))

            def turn_outputs(chunks, scale, first):
                for c in range(chunks):
                    act.wait_ge(o_turned, n.take("o_turned"))
                    kw = dict(scale=subln_s[:, 0:1]) if scale and c < 4 else {}
                    copy(h_hi[:, first + c, :], psum[:, 4 + c % 4, :], **kw).then_inc(h_high, 1)

            for j in range(4):
                act.dma_start(x[:, 2 * j:2 * j + 2, :], xt[:, 2 * j:2 * j + 2, :]).then_inc(x_landed[j], 16)
            act.wait_ge(set_up, 1)
            load_sqrt()
            act.wait_ge(cols_landed, 16)
            for c in range(KC + 1):
                if c < KC:
                    act.wait_ge(x_landed[c // 2], 16)
                    copy(h_hi[:, c, :], x[:, c, :], scale=col("attn_pre", c)).then_inc(h_high, 1)
                if c:
                    square(c - 1, x[:, c - 1, :], True)
            roots(True)
            act.wait_ge(lam_summed, 1)
            nc.scalar.activation(lam[:, 2:4], psum[:, 3, 0:2], ACT.Exp).then_inc(lam_exped, 1)

            for kind in range(2):
                act.wait_ge(blocks_added, 8 * (kind + 1))
                copy(blocks_hi[:, kind, :, :], blocks[:, kind, :, :]).then_inc(blocks_high, 1)
            act.wait_ge(partner_read, 7)
            nc.scalar.activation(gates[:], gates[:], ACT.Sigmoid).then_inc(gates_ready, 1)
            act.wait_ge(evacuated, A_ORDER.index("cmp3") + 1)
            nc.scalar.activation(hid_s[:], hid[:], ACT.Silu).then_inc(hid_silu, 1)
            act.wait_ge(hid_silu, 1)
            copy(hid_hi[:], hid_s[:]).then_inc(hid_high, 1)
            for i in range(NB):
                act.wait_ge(cmp_step, 7 * i + (i > 0) + 5)
                nc.scalar.activation(e_ring[:, 0, i, 0:256], e_ring[:, 0, i, 0:256], ACT.Exp).then_inc(cmp_exped, 1)
                act.wait_ge(cmp_transposed, i + 1)
                copy(t_ring[:, 0, 2 * (i % 2):2 * (i % 2) + 2, :].rearrange("p b q -> p (b q)"), psum[:, 6, 0:256])\
                    .then_inc(cmp_turned, 1)
            n.take("evacuated", len(A_ORDER))

            def diff_norm(t):
                if 24 <= t < 24 + NB:
                    b = t - 24
                    act.wait_ge(row_done, 16)
                    nc.scalar.activation(m_ffn[:, b, :], o_all[:, b, 0:4 * P], ACT.Square).then_inc(diff_squared, 1)
                if t == 32:
                    act.wait_ge(diff_step, NB + 1)
                    nc.scalar.activation(diff_ms[:, 2, :], diff_ms[:, 3, :], ACT.Sqrt).then_inc(diff_rooted, 1)

            attention(diff_rows() + nsa_rows(), e_ring, t_ring, neg_max, row_sum, diff_norm)
            turn_outputs(KC, True, 0)
            outputs(m_mix, 0)
            norm("ffn_pre")
            swiglu(m_ffn, 1)

            norm("mix_pre_0")
            act.wait_ge(forget_step, 4)
            nc.scalar.activation(forget[:, 3, :], forget[:, 2, :], ACT.Exp, scale=-1.0).then_inc(forget_act, 1)
            act.wait_ge(forget_act, 1)
            nc.scalar.activation(forget[:, 4, :], forget[:, 3, :], ACT.Ln, bias=1.0).then_inc(forget_act, 1)
            act.wait_ge(forget_step, 6)
            for head in range(8):
                act.dma_start(k_fox[HD:HD + 1, head, :], forget[head:head + 1, 3, :]).then_inc(decay_landed, 16)
            n.take("evacuated", len(B_ORDER))
            for c in range(4):
                act.wait_ge(mix_step, 5 * (c + 1))
                if c == 0:
                    act.wait_ge(unit_done, NORMS_AT[1] + len(B_ORDER))
                copy(h_hi[:, c, :], y_conv[:, c, :]).then_inc(h_high, 1)
            attention(fox_rows(), e_ring_b, t_ring_b, neg_max_b, row_sum_b)
            turn_outputs(4, False, 4)
            outputs(m_mix, 2)
            norm("ffn_pre_0")
            swiglu(m_ffn, 3)

            norm("mix_pre_1")

            def gate(c):
                act.wait_ge(evacuated, n.take("evacuated"))
                nc.scalar.activation(squares[:, 0, :], tmp[:, 0, :], ACT.Sigmoid, bias=col("b_pw1", c + KC)).then_inc(sigmoid_ready, 1)
                n.take("evacuated")

            def diagonals(first, last):
                for d in range(first, last):
                    if d >= DIAGONALS:
                        act.wait_ge(tap_used, d - DIAGONALS + 1)
                    copy(diag_hi[:, d % DIAGONALS, :], ident, scale=col("w_dw", CONV_PE[0] * TAPS + d)).then_inc(diag_ready, 1)
                    copy(diag_lo[:, d % DIAGONALS, :], ident, scale=taps_lo[:, d:d + 1]).then_inc(diag_ready, 1)

            act.wait_ge(taps_split, 2)
            for c in range(KC):
                gate(c)
                if c in CONV_PE:
                    act.wait_ge(glu_ready, c + 2)
                    copy(glu_hi[:, c - CONV_PE[0], :], glu[:, c, :]).then_inc(glu_high, 1)
                diagonals(DIAGONALS * c // KC, DIAGONALS * (c + 1) // KC)
            diagonals(DIAGONALS, len(CONV_PE) * TAPS)
            load_sqrt()
            for c in range(KC):
                act.wait_ge(centred, c + 1)
                if c >= 2:
                    act.wait_ge(row_added, n.base["row_added"] + KC + c - 1)
                nc.scalar.activation(squares[:, c % 2, :], y_dw[:, c, :], ACT.Square).then_inc(squared, 1)
            n.take("row_added", KC)
            roots(True)
            for c in range(KC):
                act.wait_ge(normed, c + 1)
                if c >= 2:
                    act.wait_ge(h_low, 6 * KC + c - 1)
                nc.scalar.activation(squares[:, c % 2, :], tmp[:, c % 2, :], ACT.Silu, scale=col("ln_g", c),
                                     bias=col("ln_b", c)).then_inc(ln_silu, 1)
                act.wait_ge(ln_silu, c + 1)
                copy(h_hi[:, c, :], squares[:, c % 2, :]).then_inc(h_high, 1)
            act.wait_ge(h_low, 7 * KC)
            outputs(m_mix, 4, "b_pw2")
            norm("ffn_pre_1")
            swiglu(m_ffn, 5)
            act.wait_ge(x_ready, 1)

        @block.vector
        def _(dve):
            n = Count()
            v = nc.vector

            def clear_total():
                v.memset(total[:], 0.0).then_inc(summed, 1)
                n.take("summed")

            def add_square(c):
                dve.wait_ge(squared, n.take("squared"))
                dve.wait_ge(summed, n.now("summed"))
                v.tensor_tensor(total[:], total[:], squares[:, c, :], ALU.add).then_inc(summed, 1)
                n.take("summed")

            def stat(eps, of_x=False, bank=STAT_COL):
                if of_x:
                    n.take("squared", KC)
                    dve.wait_ge(row_added, n.take("row_added", KC))
                    v.tensor_scalar(total[0:1, :], psum[0:1, bank, :], 1.0 / D, eps, ALU.mult, ALU.add).then_inc(row_out, 1)
                else:
                    dve.wait_ge(column_added, n.take("column_added", 2))
                    v.tensor_scalar(variance[:], psum[:, STAT_COL, 0:NB], 1.0 / D, eps, ALU.mult, ALU.add).then_inc(col_scaled, 1)
                dve.wait_ge(rooted, n.take("rooted"))
                v.reciprocal(scale_col[:], root[:]).then_inc(col_ready, 1)
                dve.wait_ge(row_spread, n.take("row_spread"))
                if of_x:
                    v.tensor_copy(scale_row[:], psum[:, STAT_ROW, :]).then_inc(row_ready, 1)
                    dve.wait_ge(row_ready, n.take("row_ready"))

            def low_part(c, pre):
                dve.wait_ge(h_high, n.take("h_high"))
                v.scalar_tensor_tensor(h_lo[:, c, :], x[:, c, :], col(pre, c), h_hi[:, c, :].bitcast(F32),
                                       ALU.mult, ALU.subtract).then_inc(h_low, 1)
                n.take("h_low")

            def norm(m, post, pre):
                for c in range(KC + 1):
                    if c < KC:
                        if c >= 2:
                            dve.wait_ge(x_ready, n.base.get("x_ready", 0) + c - 1)
                        v.scalar_tensor_tensor(tmp[:, c % 2, :], m[:, c, :], col(post, c), psum[:, STAT_ROW, :],
                                               ALU.mult, ALU.mult).then_inc(post_scaled, 1)
                        n.take("post_scaled")
                        if c == 0:
                            dve.wait_ge(post_scaled, n.now("post_scaled"))
                            v.tensor_tensor(x[:, 0, :], x[:, 0, :], tmp[:, 0, :], ALU.add).then_inc(x_ready, 1)
                    if c and pre:
                        low_part(c - 1, pre)
                n.take("x_ready", KC)
                if pre:
                    stat(EPS_RMS, True)

            def group(u=1):
                bank = n.base.get("evacuated", 0) % 4
                dve.wait_ge(unit_done, n.take("unit_done", u))
                n.take("evacuated")
                return psum[:, bank, :]

            def outputs(m, units, bias=None):
                clear_total()
                for c in range(KC):
                    source = group(units)
                    if c == KC - 1:
                        dve.wait_ge(squared, n.take("squared"))
                    if bias:
                        v.tensor_scalar(m[:, c, :], source, col(bias, c), None, ALU.add).then_inc(evacuated, 1)
                    else:
                        v.tensor_copy(m[:, c, :], source).then_inc(evacuated, 1)
                    if c < KC - 1:
                        add_square(c % 2)
                stat(EPS_RMS)

            def swiglu(m):
                def chunk(f):
                    v.tensor_tensor(tmp[:, 0, :], group(), scale_row[:], ALU.mult).then_inc(evacuated, 1)
                    v.tensor_tensor(tmp[:, 1, :], group(), scale_row[:], ALU.mult).then_inc(evacuated, 1)
                    dve.wait_ge(silu_ready, n.take("silu_ready"))
                    dve.wait_ge(evacuated, n.now("evacuated"))
                    v.tensor_tensor(squares[:, 1, :], squares[:, 0, :], tmp[:, 1, :], ALU.mult).then_inc(hidden, 1)
                    dve.wait_ge(hidden_high, n.take("hidden_high"))
                    v.tensor_tensor(g_lo[:, f, :], squares[:, 1, :], g_hi[:, f, :].bitcast(F32), ALU.subtract)\
                        .then_inc(hidden_low, 1)

                chunk(0)
                chunk(1)
                with n.loop(dve, FC // 2 - 1, unit_done=4, evacuated=4, silu_ready=2, hidden_high=2) as i:
                    chunk(i * 2 + 2)
                    chunk(i * 2 + 3)
                outputs(m, 2)

            def attention(rows, e, t_out, maxima, sums, inverse, extra=lambda t: None):
                base = {k: n.base.get(k, 0) for k in ("scored", "rows")}
                first_score = np.cumsum([0] + [scores_of(r) for r in rows]).tolist()
                for t in range(len(rows) + LAG_MIX + 1):
                    if t < len(rows):
                        for m in range(scores_of(rows[t])):
                            s = first_score[t] + m
                            dve.wait_ge(scored, base["scored"] + s + 1)
                            v.tensor_reduce(maxima[:, s:s + 1], psum[:, s % 4, 0:(rows[t][3] + 1) * P], AX, ALU.max, negate=True)\
                                .then_inc(maxed, 1)
                    r = t - 2
                    if 0 <= r < len(rows) and rows[r][0] == "diff":
                        s = first_score[r]
                        w = (rows[r][3] + 1) * P
                        dve.wait_ge(exped, base["scored"] + s + 2)
                        v.reciprocal(inverse[:, s + 1:s + 2], sums[:, s + 1:s + 2]).then_inc(coef_step, 1)
                        dve.wait_ge(coef_step, n.take("coef_step"))
                        v.scalar_tensor_tensor(coef[:, s:s + 1], sums[:, s:s + 1], inverse[:, s + 1:s + 2], lam[:, 5:6],
                                               ALU.mult, ALU.mult).then_inc(coef_step, 1)
                        dve.wait_ge(coef_step, n.take("coef_step"))
                        v.scalar_tensor_tensor(e[:, 0, r % 4, 0:w], e[:, 1, r % 4, 0:w], coef[:, s:s + 1], e[:, 0, r % 4, 0:w],
                                               ALU.mult, ALU.add).then_inc(combined, 1)
                    r = t - LAG_TURN
                    if 0 <= r < len(rows) and rows[r][3] not in TURNED_BY_ACT:
                        dve.wait_ge(transposed, base["rows"] + r + 1)
                        if r >= 3:
                            dve.wait_ge(mixed, base["rows"] + r - 2)
                        w = (rows[r][3] + 1) * P
                        v.tensor_copy(t_out[:, r % 3, 0:rows[r][3] + 1, :].rearrange("p b q -> p (b q)"), psum[:, 4 + r % 2, 0:w])\
                            .then_inc(turned_dve, 1)
                    r = t - LAG_MIX
                    if 0 <= r < len(rows):
                        kind, head, b, i = rows[r]
                        s = first_score[r]
                        v.reciprocal(inverse[:, s:s + 1], sums[:, s:s + 1]).then_inc(coef_step, 1)
                        dve.wait_ge(coef_step, n.take("coef_step"))
                        dve.wait_ge(mixed, base["rows"] + r + 1)
                        place = mixed_place(rows[r])
                        if kind == "nsa":
                            v.tensor_scalar(coef[:, s:s + 1], inverse[:, s:s + 1], gates[:, i, 3 * head + b:3 * head + b + 1],
                                            None, ALU.mult).then_inc(coef_step, 1)
                            dve.wait_ge(coef_step, n.take("coef_step"))
                            if b == 2:
                                dve.wait_ge(row_done, base["rows"] + r - NB + 1)
                            v.scalar_tensor_tensor(place, psum[:, 6 + r % 2, 0:HD], coef[:, s:s + 1], place,
                                                   ALU.mult, ALU.add).then_inc(row_done, 1)
                        else:
                            width = P if kind == "diff" else HD
                            v.tensor_scalar(place, psum[:, 6 + r % 2, 0:width], inverse[:, s:s + 1], None, ALU.mult)\
                                .then_inc(row_done, 1)
                    extra(t)
                n.take("scored", first_score[-1])
                n.take("rows", len(rows))

            def turn_outputs(chunks, scale, first):
                for c in range(chunks):
                    dve.wait_ge(h_high, n.take("h_high"))
                    hi = h_hi[:, first + c, :].bitcast(F32)
                    if scale and c < 4:
                        ins = v.scalar_tensor_tensor(h_lo[:, first + c, :], psum[:, 4 + c % 4, :], subln_s[:, 0:1], hi,
                                                     ALU.mult, ALU.subtract)
                    else:
                        ins = v.tensor_tensor(h_lo[:, first + c, :], psum[:, 4 + c % 4, :], hi, ALU.subtract)
                    ins.then_inc(h_low, 1)
                    n.take("h_low")

            v.memset(ones[:], 1.0).then_inc(set_up, 1)
            v.memset(v_cmp[:], 0.0)
            dve.wait_ge(cols_landed, 16)
            c0 = COL["lam"]
            v.tensor_tensor(lam[0:HD, 0:2], cols[0:HD, c0:c0 + 4:2], cols[0:HD, c0 + 1:c0 + 4:2], ALU.mult).then_inc(set_up, 1)
            v.tensor_scalar(subln_s[:], col("subln"), 1.0 - LAM_INIT, None, ALU.mult).then_inc(set_up, 1)
            for c in range(KC):
                low_part(c, "attn_pre")
            dve.wait_ge(tabs_landed, 32)
            v.tensor_copy(ident16[:], ident).then_inc(set_up, 1)
            v.tensor_copy(causal16[:], tabs[:, TAB["causal"]:TAB["causal"] + P]).then_inc(set_up, 1)
            stat(EPS_RMS, True)
            dve.wait_ge(lam_exped, 1)
            v.tensor_tensor(lam[:, 4:5], lam[:, 3:4], lam[:, 2:3], ALU.subtract).then_inc(set_up, 1)
            dve.wait_ge(set_up, 6)
            v.tensor_scalar(lam[:, 5:6], lam[:, 4:5], -LAM_INIT, None, ALU.add).then_inc(set_up, 1)
            for j in range(2):
                v.tensor_tensor(angles[:, j, :], angles[:, j, :], scale_row[:], ALU.mult).then_inc(angles_scaled, 1)

            def partner(name, at):
                r = n.base.get("partners", 0)
                ropes = n.base.get("ropes", 0)
                if partnered_chunk(name) == "rope":
                    scale = HD ** -0.5 if name[1] == "q" else 1.0
                    if ropes == 0:
                        dve.wait_ge(angles_scaled, 2)
                    else:
                        dve.wait_ge(rope_added, ropes)
                    dve.wait_ge(evacuated, at + 1)
                    v.scalar_tensor_tensor(squares[:, 0, :], tmp[:, r % 2, :], scale, angles[:, 0, :], ALU.mult, ALU.mult)\
                        .then_inc(rope_cos, 1)
                    dve.wait_ge(partnered, r + 1)
                    v.scalar_tensor_tensor(squares[:, 1, :], psum[:, 4 + r % 2, :], scale, angles[:, 1, :], ALU.mult, ALU.mult)\
                        .then_inc(partner_read, 1)
                    dve.wait_ge(rope_cos, ropes + 1)
                    dve.wait_ge(partner_read, r + 1)
                    v.tensor_tensor(rope_place(name), squares[:, 0, :], squares[:, 1, :], ALU.add).then_inc(rope_added, 1)
                    n.take("ropes")
                else:
                    dve.wait_ge(partnered, r + 1)
                    c = int(name[-1]) if name[-1].isdigit() else 0
                    place = {"dv": v_diff[:, :, c * P:(c + 1) * P], "vs": v_nsa[:, 0, :, :], "vw": v_nsa[:, 1, :, :],
                             "ga": gates[:]}.get(name[:2], v_fox[:, :, c * P:(c + 1) * P])
                    source = psum[:, 4 + r % 2, :].rearrange("p (b f) -> p b f", b=NB)
                    v.tensor_copy(place, source[:, :, 0:24] if name == "gates" else source).then_inc(partner_read, 1)
                n.take("partners")

            def split_blocks(kind):
                if kind == 0:
                    dve.wait_ge(rope_added, 1)
                dve.wait_ge(evacuated, 2)
                for g in range(2):
                    half = slice(g * HD, (g + 1) * HD)
                    tokens = nqk[half, 4 + kind, :].rearrange("p (n s) -> p n s", s=CMP_STRIDE)
                    for parity in range(2):
                        for a in range(2):
                            place = blocks[parity * HD:(parity + 1) * HD, kind, 8 * a:8 * a + 8, g * NCMP:(g + 1) * NCMP]
                            p0 = COL["k_pos" if kind == 0 else "v_pos"] + 16 * a + parity
                            pos = cols[half, p0:p0 + 15:2].unsqueeze(1).to_broadcast([HD, NCMP, 8])
                            v.tensor_tensor(place.rearrange("p b n -> p n b"), tokens[:, a:a + NCMP, parity:CMP_STRIDE:2], pos,
                                            ALU.add).then_inc(blocks_added, 1)
                dve.wait_ge(blocks_added, 8 * (kind + 1))
                dve.wait_ge(blocks_high, kind + 1)
                v.tensor_tensor(blocks_lo[:, kind, :, :], blocks[:, kind, :, :], blocks_hi[:, kind, :, :].bitcast(F32), ALU.subtract)\
                    .then_inc(blocks_low, 1)

            def cmp_softmax(i):
                e = e_ring[:, 0, i, 0:256].rearrange("p (h n) -> p h n", h=8)
                mask = tabs[:, TAB["cmp_mask"] + 32 * i:TAB["cmp_mask"] + 32 * i + NCMP].unsqueeze(1).to_broadcast([P, 4, NCMP])
                step = 7 * i + (i > 0)
                if i == 0:
                    v.memset(e_ring[:, 0, :, 0:256], NEG).then_inc(cmp_step, 1)
                    dve.wait_ge(gates_ready, 1)
                step += 1
                dve.wait_ge(cmp_step, 1)
                dve.wait_ge(cmp_scored, i + 1)
                for g in range(2):
                    v.tensor_tensor(e[:, 4 * g:4 * g + 4, 0:NCMP],
                                    psum[:, 6 + g, 0:P].rearrange("p (h n) -> p h n", h=4)[:, :, 0:NCMP], mask, ALU.add)\
                        .then_inc(cmp_step, 1)
                dve.wait_ge(cmp_step, step + 2)
                v.tensor_reduce(cmp_small[:, 0, i, :], e, AX, ALU.max).then_inc(cmp_step, 1)
                dve.wait_ge(cmp_step, step + 3)
                v.tensor_tensor(e, e, cmp_small[:, 0, i, :].unsqueeze(2).to_broadcast([P, 8, 32]), ALU.subtract).then_inc(cmp_step, 1)
                dve.wait_ge(cmp_exped, i + 1)
                v.tensor_reduce(cmp_small[:, 1, i, :], e, AX, ALU.add).then_inc(cmp_step, 1)
                dve.wait_ge(cmp_step, step + 5)
                v.reciprocal(cmp_small[:, 2, i, :], cmp_small[:, 1, i, :]).then_inc(cmp_step, 1)
                dve.wait_ge(cmp_step, step + 6)
                v.tensor_tensor(cmp_small[:, 3, i, :], cmp_small[:, 2, i, :], gates[:, i, 0:24:3], ALU.mult).then_inc(cmp_step, 1)
                step += 7
                if i == 0:
                    keep = tabs[:, TAB["cmp_keep"]:TAB["cmp_keep"] + 32].unsqueeze(1).to_broadcast([P, 8, 32])
                    v.tensor_tensor(e, e, keep, ALU.mult).then_inc(cmp_step, 1)
                    step += 1
                dve.wait_ge(cmp_step, step)
                v.tensor_tensor(e, e, cmp_small[:, 3, i, :].unsqueeze(2).to_broadcast([P, 8, 32]), ALU.mult).then_inc(cmp_weighed, 1)

            for j, name in enumerate(A_ORDER):
                bank = group(2 if name.startswith("cmp") else 1)
                if partnered_chunk(name) == "rope":
                    v.tensor_copy(tmp[:, n.now("raws") % 2, :], bank).then_inc(evacuated, 1)
                    n.take("raws")
                elif partnered_chunk(name) == "turn":
                    v.tensor_tensor(tmp[:, n.now("raws") % 2, :], bank, scale_row[:], ALU.mult).then_inc(evacuated, 1)
                    n.take("raws")
                elif name == "vc":
                    v.tensor_tensor(nqk[:, 5, :], bank, scale_row[:], ALU.mult).then_inc(evacuated, 1)
                elif name.startswith("cmp"):
                    v.tensor_copy(hid[:, int(name[3]), :], bank[:, 0:2 * NCMP]).then_inc(evacuated, 1)
                else:
                    v.tensor_copy(k_cmp[:], bank[:, 0:2 * NCMP])
                    for g in range(2):
                        for c in range(4):
                            ins = v.tensor_copy(v_cmp[32 * c:32 * c + NCMP, g, c * HD:(c + 1) * HD],
                                                bank[0:NCMP, HD + g * HD:2 * HD + g * HD])
                    ins.then_inc(evacuated, 1)
                if j and partnered_chunk(A_ORDER[j - 1]):
                    partner(A_ORDER[j - 1], j - 1)
                if name in ("vc", "nq0"):
                    split_blocks(int(name == "nq0"))
                if name == "cmp3":
                    dve.wait_ge(hid_high, 1)
                    v.tensor_tensor(hid_lo[:], hid_s[:], hid_hi[:].bitcast(F32), ALU.subtract).then_inc(hid_low, 1)
                i, step = divmod(j - CMP_FROM, 3)
                if j >= CMP_FROM and i < NB and step == 0:
                    cmp_softmax(i)
                if j >= CMP_FROM and i < NB and step == 2:
                    dve.wait_ge(cmp_mixed, i + 1)
                    v.tensor_copy(o_all[:, i, 4 * P:D], psum[:, 7, :]).then_inc(cmp_done, 1)
            partner(A_ORDER[-1], len(A_ORDER) - 1)
            dve.wait_ge(cmp_done, NB)

            def diff_norm(t):
                if 26 <= t < 26 + NB:
                    b = t - 26
                    dve.wait_ge(diff_squared, b + 1)
                    v.tensor_reduce(diff_ms[:, 0, 4 * b:4 * b + 4], m_ffn[:, b, :].rearrange("p (h e) -> p h e", h=4), AX, ALU.add)\
                        .then_inc(diff_step, 1)
                if t == 30:
                    dve.wait_ge(diff_step, NB)
                    v.tensor_scalar(diff_ms[:, 3, :], diff_ms[:, 0, :], 1.0 / P, EPS_RMS, ALU.mult, ALU.add).then_inc(diff_step, 1)
                if t == 34:
                    dve.wait_ge(diff_rooted, 1)
                    v.reciprocal(diff_ms[:, 1, :], diff_ms[:, 2, :]).then_inc(diff_step, 1)
                if 36 <= t < 36 + 4 * NB and t % 4 == 0:
                    b = (t - 36) // 4
                    dve.wait_ge(diff_step, NB + 2)
                    dve.wait_ge(row_done, 16)
                    part = o_all[:, b, 0:4 * P].rearrange("p (h e) -> p h e", h=4)
                    v.tensor_tensor(part, part, diff_ms[:, 1, 4 * b:4 * b + 4].unsqueeze(2).to_broadcast([P, 4, P]), ALU.mult)\
                        .then_inc(diff_step, 1)

            attention(diff_rows() + nsa_rows(), e_ring, t_ring, neg_max, row_sum, inv_sum, diff_norm)
            turn_outputs(KC, True, 0)
            outputs(m_mix, 1)
            norm(m_mix, "attn_post", "ffn_pre")
            swiglu(m_ffn)
            norm(m_ffn, "ffn_post", "mix_pre_0")

            for j, name in enumerate(B_ORDER):
                which, c = name.rstrip("0123"), int(name[-1]) if name != "f" else 0
                bank = group()
                if which == "f":
                    v.tensor_tensor(forget[:, 0, :], bank[0:8, :], scale_row[0:8, :], ALU.mult).then_inc(evacuated, 1)
                    dve.wait_ge(evacuated, n.now("evacuated"))
                    v.tensor_scalar(forget[:, 1, :], forget[:, 0, :], cols[0:8, COL["b_forget"]:COL["b_forget"] + 1], None, ALU.add)\
                        .then_inc(forget_step, 1)
                    dve.wait_ge(forget_step, 1)
                    v.tensor_scalar(forget[:, 0, :], forget[:, 1, :], 0.0, None, ALU.min).then_inc(forget_step, 1)
                    v.memset(forget[:, 3, :], 1.0).then_inc(forget_step, 1)
                    v.scalar_tensor_tensor(forget[:, 2, :], forget[:, 1, :], -1.0, forget[:, 1, :], ALU.mult, ALU.max)\
                        .then_inc(forget_step, 1)
                    dve.wait_ge(forget_act, 2)
                    v.tensor_tensor(forget[:, 1, :], forget[:, 4, :], forget[:, 0, :], ALU.subtract).then_inc(forget_step, 1)
                    dve.wait_ge(forget_step, 5)
                    v.tensor_tensor_scan(forget[:, 3, :], ones[0:8, 0:1].to_broadcast([8, S]), forget[:, 1, :], 0.0,
                                         ALU.mult, ALU.add).then_inc(forget_step, 1)
                    v.memset(padded[:, 0:2], 0.0)
                    n.take("set")
                elif which == "v":
                    dve.wait_ge(mix_step, n.now("mix_step"))
                    v.tensor_tensor(tmp[:, n.now("raws") % 2, :], bank, scale_row[:], ALU.mult).then_inc(evacuated, 1)
                    n.take("raws")
                elif which in ("gc", "xa"):
                    if c:
                        dve.wait_ge(mix_step, n.now("mix_step"))
                    v.tensor_tensor(tmp[:, int(which == "xa"), :], bank, scale_row[:], ALU.mult).then_inc(evacuated, 1)
                elif which == "gb":
                    dve.wait_ge(evacuated, n.now("evacuated", -1))
                    v.tensor_tensor(padded[:, 2:S + 2], tmp[:, 0, :], tmp[:, 1, :], ALU.mult).then_inc(mix_step, 1)
                    dve.wait_ge(mix_step, n.take("mix_step"))
                    v.tensor_tensor(tmp[:, 0, :], bank, scale_row[:], ALU.mult).then_inc(evacuated, 1)
                    w = [col("w_short", 3 * c + k) for k in range(3)]
                    v.tensor_scalar(squares[:, 0, :], padded[:, 0:S], w[0], None, ALU.mult).then_inc(mix_step, 1)
                    dve.wait_ge(mix_step, n.take("mix_step"))
                    v.scalar_tensor_tensor(squares[:, 1, :], padded[:, 1:S + 1], w[1], squares[:, 0, :], ALU.mult, ALU.add)\
                        .then_inc(mix_step, 1)
                    dve.wait_ge(mix_step, n.take("mix_step"))
                    v.scalar_tensor_tensor(squares[:, 0, :], padded[:, 2:S + 2], w[2], squares[:, 1, :], ALU.mult, ALU.add)\
                        .then_inc(mix_step, 1)
                    dve.wait_ge(mix_step, n.take("mix_step"))
                    dve.wait_ge(evacuated, n.now("evacuated"))
                    v.tensor_tensor(y_conv[:, c, :], squares[:, 0, :], tmp[:, 0, :], ALU.mult).then_inc(mix_step, 1)
                    n.take("mix_step")
                elif which in ("q", "k"):
                    if (which, c) == ("q", 0):
                        dve.wait_ge(decay_landed, 16 * 8)
                        v.memset(q_fox[HD:HD + 1, :, :], 1.0)
                    place = q_fox if which == "q" else k_fox
                    scale = HD ** -0.5 if which == "q" else 1.0
                    for half in range(2):
                        part = slice(half * HD, (half + 1) * HD)
                        ins = v.scalar_tensor_tensor(place[0:HD, 2 * c + half, :], bank[part, :], scale, scale_row[part, :],
                                                     ALU.mult, ALU.mult)
                    ins.then_inc(evacuated, 1)
                if j and partnered_chunk(B_ORDER[j - 1]):
                    partner(B_ORDER[j - 1], j - 1)
            for c in range(4):
                dve.wait_ge(h_high, n.take("h_high"))
                v.tensor_tensor(h_lo[:, c, :], y_conv[:, c, :], h_hi[:, c, :].bitcast(F32), ALU.subtract).then_inc(h_low, 1)
                n.take("h_low")
            attention(fox_rows(), e_ring_b, t_ring_b, neg_max_b, row_sum_b, inv_sum_b)
            turn_outputs(4, False, 4)
            outputs(m_mix, 1)
            norm(m_mix, "mix_post_0", "ffn_pre_0")
            swiglu(m_ffn)
            norm(m_ffn, "ffn_post_0", "mix_pre_1")

            v.memset(glu[:, :, 0:TAPS - 1], 0.0).then_inc(glu_ready, 1)
            first, last = COL["w_dw"] + CONV_PE[0] * TAPS, COL["w_dw"] + KC * TAPS
            v.tensor_copy(taps_hi[:], cols[:, first:last]).then_inc(taps_split, 1)
            dve.wait_ge(taps_split, 1)
            v.tensor_tensor(taps_lo[:], cols[:, first:last], taps_hi[:].bitcast(F32), ALU.subtract).then_inc(taps_split, 1)

            def glu_chunk(c):
                v.tensor_tensor(tmp[:, 0, :], group(), scale_row[:], ALU.mult).then_inc(evacuated, 1)
                v.tensor_tensor(tmp[:, 1, :], group(), scale_row[:], ALU.mult).then_inc(evacuated, 1)
                dve.wait_ge(sigmoid_ready, n.take("sigmoid_ready"))
                dve.wait_ge(evacuated, n.now("evacuated"))
                v.scalar_tensor_tensor(glu[:, c, TAPS - 1:TAPS - 1 + S], tmp[:, 1, :], col("b_pw1", c), squares[:, 0, :], ALU.add, ALU.mult)\
                    .then_inc(glu_ready, 1)
                if c in CONV_PE:
                    j = c - CONV_PE[0]
                    dve.wait_ge(glu_high, j + 1)
                    v.tensor_tensor(glu_lo[:, j, :], glu[:, c, :], glu_hi[:, j, :].bitcast(F32), ALU.subtract).then_inc(glu_low, 1)

            def conv_taps(first, last):
                for t in range(first, last):
                    c, k = divmod(t, TAPS)
                    if k == 0:
                        dve.wait_ge(glu_ready, c + 2)
                        v.tensor_scalar(y_dw[:, c, :], glu[:, c, 0:S], col("w_dw", c * TAPS), col("b_dw", c), ALU.mult, ALU.add)\
                            .then_inc(tapped, 1)
                    else:
                        dve.wait_ge(tapped, n.take("tapped"))
                        v.scalar_tensor_tensor(y_dw[:, c, :], glu[:, c, k:k + S], col("w_dw", c * TAPS + k), y_dw[:, c, :],
                                               ALU.mult, ALU.add).then_inc(conv_chunk if k == TAPS - 1 else tapped, 1)

            def conv_out(j):
                dve.wait_ge(tap_used, (j + 1) * TAPS)
                v.tensor_scalar(y_dw[:, CONV_PE[j], :], psum[:, 4 + j % 2, :], col("b_dw", CONV_PE[j]), None, ALU.add)\
                    .then_inc(conv_chunk, 1)

            for c in range(KC):
                glu_chunk(c)
                conv_taps(CONV_PACE * c, CONV_PACE * (c + 1))
            conv_taps(CONV_PACE * KC, 112)
            conv_out(0)
            conv_taps(112, 142)
            conv_out(1)
            conv_taps(142, CONV_PE[0] * TAPS)
            conv_out(2)
            dve.wait_ge(row_added, n.take("row_added", KC))
            for c in range(KC):
                v.scalar_tensor_tensor(y_dw[:, c, :], psum[:, STAT_COL, :], -1.0 / D, y_dw[:, c, :], ALU.mult, ALU.add)\
                    .then_inc(centred, 1)
            stat(EPS_LN, True, STAT_ROW)
            for c in range(KC + 1):
                if c < KC:
                    if c >= 2:
                        dve.wait_ge(ln_silu, c - 1)
                    v.tensor_tensor(tmp[:, c % 2, :], y_dw[:, c, :], scale_row[:], ALU.mult).then_inc(normed, 1)
                if c:
                    dve.wait_ge(h_high, n.take("h_high"))
                    v.tensor_tensor(h_lo[:, c - 1, :], squares[:, (c - 1) % 2, :], h_hi[:, c - 1, :].bitcast(F32), ALU.subtract)\
                        .then_inc(h_low, 1)
                    n.take("h_low")
            outputs(m_mix, 1, "b_pw2")
            norm(m_mix, "mix_post_1", "ffn_pre_1")
            swiglu(m_ffn)
            norm(m_ffn, "ffn_post_1", None)


def shape_tables():
    inv = (1.0 / (np.float32(10000.0) ** (np.arange(0, HD, 2, dtype=np.float32) / np.float32(HD)))).astype(np.float32)
    angle = np.arange(S, dtype=np.float32)[:, None] * inv[None, :]
    which = np.arange(P) % 32
    angles = np.stack([np.cos(angle).T[which], np.sin(angle).T[which]], axis=1).astype(np.float32)
    t = np.zeros((P, NTAB), np.float32)
    out = np.arange(P)
    lower = out % HD < 32
    t[np.where(lower, out + 32, out - 32), TAB["rot"] + out] = np.where(lower, -1.0, 1.0)
    t[:, TAB["ident"]:TAB["ident"] + P] = np.eye(P)
    t[:, TAB["causal"]:TAB["causal"] + P] = np.where(np.arange(P)[None, :] <= np.arange(P)[:, None], 0.0, NEG)
    token = np.arange(S).reshape(NB, P).T
    end = np.arange(32) * CMP_STRIDE + CMP_LEN - 1
    seen = (end[None, None, :] <= token[:, :, None]) & (np.arange(32) < NCMP)
    t[:, TAB["cmp_mask"]:TAB["cmp_mask"] + NB * 32] = np.where(seen, 0.0, NEG).reshape(P, NB * 32)
    t[:, TAB["cmp_keep"]:TAB["cmp_keep"] + 32] = seen[:, 0, :]
    return angles, t


def tiles_of(w, rows, cols):
    return w.reshape(-1, P, w.shape[1])[rows, :, cols * P:(cols + 1) * P].transpose(1, 0, 2)


def pad_columns(w, n):
    out = np.zeros((w.shape[0], n), w.dtype)
    out[:, :w.shape[1]] = w
    return out


def lay_out(a):
    a = {k: np.asarray(v) for k, v in a.items()}
    w_in = a["w_in"][0]
    nq = 12 * P
    order = np.concatenate([np.arange(nq)] + [np.arange(nq + HD * (c + 4 * g), nq + HD * (c + 4 * g) + HD)
                                              for c in range(4) for g in range(2)] + [np.arange(nq + 8 * HD, w_in.shape[1])])
    w_in = pad_columns(w_in[:, order], 23 * P)
    all8 = slice(0, 8)
    w2 = np.zeros((P, 8, P), np.float32)
    k2, v2 = a["k_cmp_w2"][0].reshape(2, P, HD), a["v_cmp_w2"][0].reshape(2, P, HD)
    for m in range(2):
        w2[:, m, 0:HD] = w2[:, m, HD:P] = k2[m]
        w2[:, 2 + m, 0:HD] = v2[m]
    w1 = [a["k_cmp_w1"][0], a["v_cmp_w1"][0]]
    wide = []
    for name in A_ORDER:
        if name.startswith("cmp"):
            kind, m = divmod(int(name[3]), 2)
            wide += [tiles_of(w1[kind], slice(8 * half, 8 * half + 8), m) for half in range(2)]
        else:
            wide.append(w2 if name == "w2" else tiles_of(w_in, all8, A_CHUNK[name]))
    down = []

    def swiglu(gate, up, w_down):
        for f in range(FC):
            wide.extend([tiles_of(gate, all8, f), tiles_of(up, all8, f)])
        for c in range(KC):
            down.extend([tiles_of(w_down, slice(DOWN_UNIT * h, DOWN_UNIT * (h + 1)), c) for h in range(2)])

    wide += [tiles_of(a["w_out"][0], all8, c) for c in range(KC)]
    swiglu(a["w_gate"][0], a["w_up"][0], a["w_down"][0])
    w = pad_columns(a["w_in_2"][0], 25 * P)
    wide += [tiles_of(w, all8, B_CHUNK[name]) for name in B_ORDER]
    wide += [tiles_of(a["w_out_2"][0], all8, c) for c in range(KC)]
    swiglu(a["w_ffn_in_2"][0][:, :F], a["w_ffn_in_2"][0][:, F:], a["w_ffn_out_2"][0])
    for c in range(KC):
        wide += [tiles_of(a["w_pw1_2"][0], all8, KC + c), tiles_of(a["w_pw1_2"][0], all8, c)]
    wide += [tiles_of(a["w_pw2_2"][0], all8, c) for c in range(KC)]
    swiglu(a["w_ffn_in_2"][1][:, :F], a["w_ffn_in_2"][1][:, F:], a["w_ffn_out_2"][1])

    cols = np.zeros((P, NCOL), np.float32)

    def put(name, vector):
        vector = vector.reshape(-1, P).T
        cols[:, COL[name]:COL[name] + vector.shape[1]] = vector

    for name, source in (("attn_pre", a["attn_pre_norm"][0]), ("attn_post", a["attn_post_norm"][0]),
                         ("ffn_pre", a["ffn_pre_norm"][0]), ("ffn_post", a["ffn_post_norm"][0]),
                         ("b_pw1", a["b_pw1_2"][0]), ("b_dw", a["b_dw_2"][0]), ("ln_g", a["ln_g_2"][0]),
                         ("ln_b", a["ln_b_2"][0]), ("b_pw2", a["b_pw2_2"][0]), ("subln", a["diff_subln"][0])):
        put(name, source)
    for j in range(2):
        put(f"mix_pre_{j}", a["norm_mix_pre_2"][j])
        put(f"mix_post_{j}", a["norm_mix_post_2"][j])
        put(f"ffn_pre_{j}", a["norm_ffn_pre_2"][j])
        put(f"ffn_post_{j}", a["norm_ffn_post_2"][j])
    cols[:, COL["w_dw"]:COL["w_dw"] + 8 * TAPS] = a["w_dw_2"][0].reshape(TAPS, KC, P).transpose(2, 1, 0).reshape(P, -1)
    cols[:, COL["w_short"]:COL["w_short"] + 12] = a["w_short_conv_2"][0].reshape(3, 4, P).transpose(2, 1, 0).reshape(P, -1)
    cols[0:8, COL["b_forget"]] = a["b_forget_2"][0]
    for name, source in (("k_pos", a["k_cmp_pos"][0]), ("v_pos", a["v_cmp_pos"][0])):
        cols[0:HD, COL[name]:COL[name] + 32] = cols[HD:P, COL[name]:COL[name] + 32] = source.T
    for j, name in enumerate(("lambda_q1", "lambda_k1", "lambda_q2", "lambda_k2")):
        cols[0:HD, COL["lam"] + j] = a[name][0]
    angles, tables = shape_tables()
    return {
        "in_xt": np.ascontiguousarray(a["x"][0].reshape(S, KC, P).transpose(2, 1, 0)),
        "in_cols": cols, "in_tables": tables, "in_angles": angles,
        "in_wide": np.ascontiguousarray(np.stack(wide)).reshape(len(wide), P, UNIT * P),
        "in_down": np.ascontiguousarray(np.stack(down)).reshape(len(down), P, DOWN_UNIT * P),
    }


def declare(nc, arrays):
    ins = [nc.dram_tensor(k, v.shape, F32, kind="ExternalInput").ap() for k, v in arrays.items()]
    out = nc.dram_tensor("out", (P, KC, S), F32, kind="ExternalOutput").ap()
    two_blocks(nc, *ins, out)


def kernel(**inputs):
    import concourse.bacc as _bacc
    from concourse.bass_utils import run_bass_kernel_spmd as _run
    arrays = lay_out(inputs)
    nc = _bacc.Bacc("TRN2", target_bir_lowering=False, num_devices=1, dynamic_dma_scratch_size=1024)
    declare(nc, arrays)
    got = _run(nc, [arrays], core_ids=[0]).results[0]["out"]
    return np.ascontiguousarray(got.transpose(2, 1, 0).reshape(1, S, D))
```
